# Optimizing a Trainium2 kernel written in Bass

```python
import math
import jax, jax.numpy as jnp
from jax import lax
import numpy as np

D_MODEL = 2048
BATCH = 1
SEQ = 256
DEPTH = 1

HEAD_DIM = 128
N_MIX_HEADS = D_MODEL // HEAD_DIM
A_HEADS = N_MIX_HEADS // 4
B_HEADS = (N_MIX_HEADS - A_HEADS) // 2
C_HEADS = N_MIX_HEADS - A_HEADS - B_HEADS
A_DK = HEAD_DIM
A_DV = HEAD_DIM
A_W = A_HEADS * A_DK
B_W = B_HEADS * HEAD_DIM
C_W = C_HEADS * HEAD_DIM
MIX_W = A_W + B_W + C_W
IN_SPLITS = [A_W, A_W, A_W, A_W, B_W, B_W, B_W, B_HEADS, C_W, C_W, C_W]
IN_COLS = sum(IN_SPLITS)
A_CHUNK = 64
B_Q_BLOCK = 128
C_BLOCK = 256
C_TOPK = 3
C_Q_BLOCK = 64
D_FF = 5632
CONV_W = 3
PLE_DIM = 256
EPS = 1e-6
TINY = 1e-30
NEG = -1e30


def rmsnorm(x, g):
    xf = x.astype(jnp.float32)
    y = xf * lax.rsqrt(jnp.mean(xf * xf, axis=-1, keepdims=True) + EPS)
    return (y * g.astype(jnp.float32)).astype(x.dtype)

def heads(t, n):
    b, s, _ = t.shape
    return t.reshape(b, s, n, -1).transpose(0, 2, 1, 3)

def merge_blocks(o):
    nqb, b, h, q, d = o.shape
    return o.transpose(1, 0, 3, 2, 4).reshape(b, nqb * q, h * d)

def alibi_slopes(n):
    return jnp.exp2(-8.0 * jnp.arange(1, n + 1, dtype=jnp.float32) / n)

def hgrn2_lower_bounds(lb_logits):
    sm = jax.nn.softmax(lb_logits.astype(jnp.float32), axis=0)
    return jnp.cumsum(sm, axis=0) - sm[0:1]

def hgrn2_mixer(q, f_logit, i, g, lb, o_norm_g):
    bsz, s, _ = q.shape
    dt = q.dtype
    z = f_logit.astype(jnp.float32)
    lbf = lb.astype(jnp.float32)
    f = lbf + (1.0 - lbf) * jax.nn.sigmoid(z)
    log_f = jnp.log(jnp.maximum(f, TINY))
    k = (1.0 - lbf) * jax.nn.sigmoid(-z)
    qh = heads(jax.nn.silu(q.astype(jnp.float32)), A_HEADS)
    kh = heads(k, A_HEADS)
    gh = heads(log_f, A_HEADS)
    vh = heads(i.astype(jnp.float32), A_HEADS)
    nc = s // A_CHUNK

    def chunks(t):
        return t.reshape(bsz, A_HEADS, nc, A_CHUNK, t.shape[-1]).transpose(2, 0, 1, 3, 4)

    causal = jnp.tril(jnp.ones((A_CHUNK, A_CHUNK), dtype=bool))[:, :, None]

    def step(state, xs):
        qc, kc, gc, vc = xs
        b = jnp.cumsum(gc, axis=2)
        o_inter = jnp.einsum('bhtd,bhde->bhte', qc * jnp.exp(b), state)
        diff = b[:, :, :, None, :] - b[:, :, None, :, :]
        decay = jnp.where(causal, jnp.exp(jnp.where(causal, diff, 0.0)), 0.0)
        attn = jnp.einsum('bhtd,bhsd,bhtsd->bhts', qc, kc, decay)
        o = o_inter + jnp.einsum('bhts,bhse->bhte', attn, vc)
        b_last = b[:, :, -1:, :]
        k_dec = kc * jnp.exp(b_last - b)
        state = jnp.exp(b_last[:, :, 0, :])[..., None] * state + jnp.einsum('bhsd,bhse->bhde', k_dec, vc)
        return state, o

    s0 = jnp.zeros((bsz, A_HEADS, A_DK, A_DV), jnp.float32)
    _, o = lax.scan(step, s0, (chunks(qh), chunks(kh), chunks(gh), chunks(vh)))
    o = o.transpose(1, 2, 0, 3, 4).reshape(bsz, A_HEADS, s, A_DV)
    o = rmsnorm(o, o_norm_g) * jax.nn.silu(heads(g.astype(jnp.float32), A_HEADS))
    return o.transpose(0, 2, 1, 3).reshape(bsz, s, A_W).astype(dt)

def fox_mixer(q, k, v, f_logit, b_f, qn_g, kn_g):
    bsz, s, _ = q.shape
    dt = q.dtype
    qh = rmsnorm(heads(q, B_HEADS), qn_g)
    kh = rmsnorm(heads(k, B_HEADS), kn_g)
    vh = heads(v, B_HEADS)
    log_f = jax.nn.log_sigmoid(f_logit.astype(jnp.float32) + b_f.astype(jnp.float32))
    fcum = jnp.cumsum(log_f, axis=1).transpose(0, 2, 1)
    nqb = s // B_Q_BLOCK
    qb = qh.reshape(bsz, B_HEADS, nqb, B_Q_BLOCK, HEAD_DIM).transpose(2, 0, 1, 3, 4)
    fq = fcum.reshape(bsz, B_HEADS, nqb, B_Q_BLOCK).transpose(2, 0, 1, 3)
    kpos = jnp.arange(s)
    scale = HEAD_DIM ** -0.5

    def block(xs):
        qi, fi, bi = xs
        qpos = bi * B_Q_BLOCK + jnp.arange(B_Q_BLOCK)
        logits = (jnp.einsum('bhqd,bhkd->bhqk', qi, kh).astype(jnp.float32) * scale
                  + fi[..., None] - fcum[:, :, None, :])
        logits = jnp.where(kpos[None, :] <= qpos[:, None], logits, NEG)
        w = jax.nn.softmax(logits, axis=-1).astype(dt)
        return jnp.einsum('bhqk,bhkd->bhqd', w, vh)

    o = lax.map(block, (qb, fq, jnp.arange(nqb)))
    return merge_blocks(o)

def moba_mixer(q, k, v, qn_g, kn_g, slopes):
    bsz, s, _ = q.shape
    dt = q.dtype
    h = C_HEADS
    qh = rmsnorm(heads(q, h), qn_g)
    kh = rmsnorm(heads(k, h), kn_g)
    vh = heads(v, h)
    nb = -(-s // C_BLOCK)
    s_pad = nb * C_BLOCK
    pad = ((0, 0), (0, 0), (0, s_pad - s), (0, 0))
    kp = jnp.pad(kh, pad)
    vp = jnp.pad(vh, pad)
    kblk = kp.reshape(bsz, h, nb, C_BLOCK, HEAD_DIM)
    vblk = vp.reshape(bsz, h, nb, C_BLOCK, HEAD_DIM)
    pos = jnp.arange(s)
    own = pos // C_BLOCK
    topk = min(C_TOPK, nb - 1)
    scale = HEAD_DIM ** -0.5
    kflat = kblk.reshape(bsz * h * nb, C_BLOCK, HEAD_DIM)
    vflat = vblk.reshape(bsz * h * nb, C_BLOCK, HEAD_DIM)
    bh_off = (jnp.arange(bsz * h, dtype=jnp.int32) * nb).reshape(bsz, h, 1, 1)
    blk_off = jnp.arange(C_BLOCK)
    sl = slopes[None, :, None, None]
    nqb = s // C_Q_BLOCK

    def to_blocks(t):
        t = t.reshape((bsz, h, nqb, C_Q_BLOCK) + t.shape[3:])
        return jnp.moveaxis(t, 2, 0)

    if topk > 0:
        kbar = jnp.mean(kblk.astype(jnp.float32), axis=3)
        gate = jnp.einsum('bhsd,bhnd->bhsn', qh.astype(jnp.float32), kbar)
        past = jnp.arange(nb)[None, :] < own[:, None]
        gate = jnp.where(past, gate, NEG)
        gval, gidx = lax.top_k(gate, topk)
        gvalid = gval > NEG / 2
        xs = (to_blocks(qh), jnp.arange(nqb), to_blocks(gidx), to_blocks(gvalid))
    else:
        xs = (to_blocks(qh), jnp.arange(nqb))

    def block(xs):
        qi, bi = xs[0], xs[1]
        qpos = bi * C_Q_BLOCK + jnp.arange(C_Q_BLOCK)
        start = (bi * C_Q_BLOCK // C_BLOCK) * C_BLOCK
        k_own = lax.dynamic_slice_in_dim(kp, start, C_BLOCK, axis=2)
        v_own = lax.dynamic_slice_in_dim(vp, start, C_BLOCK, axis=2)
        dist = (qpos[:, None] - (start + blk_off)[None, :]).astype(jnp.float32)
        s_own = jnp.einsum('bhqd,bhkd->bhqk', qi, k_own).astype(jnp.float32) * scale - sl * dist
        scores = [jnp.where(dist >= 0, s_own, NEG)]
        flats = []
        if topk > 0:
            idx, valid = xs[2], xs[3]
            flat = bh_off + idx
            for j in range(topk):
                fj = flat[..., j]
                flats.append(fj)
                kg = kflat[fj]
                kpos_g = idx[..., j][..., None] * C_BLOCK + blk_off
                dist_g = (qpos[None, None, :, None] - kpos_g).astype(jnp.float32)
                sj = jnp.einsum('bhqd,bhqkd->bhqk', qi, kg).astype(jnp.float32) * scale - sl * dist_g
                scores.append(jnp.where(valid[..., j][..., None], sj, NEG))
        w = jax.nn.softmax(jnp.concatenate(scores, axis=-1), axis=-1).astype(dt)
        out = jnp.einsum('bhqk,bhkd->bhqd', w[..., :C_BLOCK], v_own)
        for j, fj in enumerate(flats):
            vg = vflat[fj]
            wj = w[..., (j + 1) * C_BLOCK:(j + 2) * C_BLOCK]
            out = out + jnp.einsum('bhqk,bhqkd->bhqd', wj, vg)
        return out

    o = lax.map(block, xs)
    return merge_blocks(o)

def conv_ffn(x, w_gate, w_up, conv_w, conv_b, w_down):
    hg = x @ w_gate
    hg = lax.conv_general_dilated(hg, conv_w[:, None, :], window_strides=(1,),
                                  padding=[(CONV_W - 1, 0)],
                                  dimension_numbers=('NWC', 'WIO', 'NWC'),
                                  feature_group_count=hg.shape[-1]) + conv_b
    return (jax.nn.gelu(hg, approximate=True) * (x @ w_up)) @ w_down

def first_inputs(seed: int = 0) -> dict:
    key = jax.random.key(seed)
    ks = jax.random.split(key, 21)
    f32 = jnp.float32

    def nrm(k, shape, scale):
        return jax.random.normal(k, shape, f32) * scale

    return {
        "x": nrm(ks[0], (BATCH, SEQ, D_MODEL), 1.0),
        "p": nrm(ks[1], (DEPTH, BATCH, SEQ, PLE_DIM), 1.0),
        "attn_norm": 1.0 + nrm(ks[2], (DEPTH, D_MODEL), 0.02),
        "w_in": nrm(ks[3], (DEPTH, D_MODEL, IN_COLS), D_MODEL ** -0.5),
        "fox_bf": nrm(ks[4], (DEPTH, B_HEADS), 0.1),
        "lb_logits": nrm(ks[5], (DEPTH, A_W), 0.1),
        "hgrn_onorm": 1.0 + nrm(ks[6], (DEPTH, A_DV), 0.02),
        "fox_qnorm": 1.0 + nrm(ks[7], (DEPTH, HEAD_DIM), 0.02),
        "fox_knorm": 1.0 + nrm(ks[8], (DEPTH, HEAD_DIM), 0.02),
        "moba_qnorm": 1.0 + nrm(ks[9], (DEPTH, HEAD_DIM), 0.02),
        "moba_knorm": 1.0 + nrm(ks[10], (DEPTH, HEAD_DIM), 0.02),
        "w_out": nrm(ks[11], (DEPTH, MIX_W, D_MODEL), MIX_W ** -0.5),
        "ffn_norm": 1.0 + nrm(ks[12], (DEPTH, D_MODEL), 0.02),
        "w_gate": nrm(ks[13], (DEPTH, D_MODEL, D_FF), D_MODEL ** -0.5),
        "w_up": nrm(ks[14], (DEPTH, D_MODEL, D_FF), D_MODEL ** -0.5),
        "conv_w": nrm(ks[15], (DEPTH, CONV_W, D_FF), CONV_W ** -0.5),
        "conv_b": nrm(ks[16], (DEPTH, D_FF), 0.01),
        "w_down": nrm(ks[17], (DEPTH, D_FF, D_MODEL), D_FF ** -0.5),
        "ple_norm": 1.0 + nrm(ks[18], (DEPTH, D_MODEL), 0.02),
        "w_ple_gate": nrm(ks[19], (DEPTH, D_MODEL, D_MODEL), D_MODEL ** -0.5),
        "w_ple_proj": nrm(ks[20], (DEPTH, PLE_DIM, D_MODEL), PLE_DIM ** -0.5),
    }

def first_block(x, p, attn_norm, w_in, fox_bf, lb_logits, hgrn_onorm, fox_qnorm, fox_knorm,
              moba_qnorm, moba_knorm, w_out, ffn_norm, w_gate, w_up, conv_w, conv_b, w_down,
              ple_norm, w_ple_gate, w_ple_proj):
    lbs = hgrn2_lower_bounds(lb_logits)
    slopes = alibi_slopes(C_HEADS)
    split_idx = []
    acc = 0
    for n in IN_SPLITS[:-1]:
        acc += n
        split_idx.append(acc)
    h = x
    for i in range(DEPTH):
        a = rmsnorm(h, attn_norm[i])
        proj = a @ w_in[i]
        aq, af, ai, ag, bq, bk, bv, bf, cq, ck, cv = jnp.split(proj, split_idx, axis=-1)
        oa = hgrn2_mixer(aq, af, ai, ag, lbs[i], hgrn_onorm[i])
        ob = fox_mixer(bq, bk, bv, bf, fox_bf[i], fox_qnorm[i], fox_knorm[i])
        oc = moba_mixer(cq, ck, cv, moba_qnorm[i], moba_knorm[i], slopes)
        h = h + jnp.concatenate([oa, ob, oc], axis=-1) @ w_out[i]
        c = rmsnorm(h, ffn_norm[i])
        h = h + conv_ffn(c, w_gate[i], w_up[i], conv_w[i], conv_b[i], w_down[i])
        e = rmsnorm(h, ple_norm[i])
        h = h + jax.nn.sigmoid(e @ w_ple_gate[i]) * (p[i] @ w_ple_proj[i])
    return h


MIX_WIDTH = D_MODEL
BLOCK = 128

SWA_HEADS = 16
SWA_KV_HEADS = 2
SWA_HEAD_DIM = 64
SWA_GROUP = SWA_HEADS // SWA_KV_HEADS
WINDOW = 128

REL_BUCKETS = 32
REL_MAX_DIST = 128

MLA_HEADS = 8
MLA_Q_RANK = 384
MLA_KV_RANK = 128
MLA_NOPE_DIM = 128
MLA_ROPE_DIM = 64
MLA_V_DIM = 128
MLA_QK_DIM = MLA_NOPE_DIM + MLA_ROPE_DIM
ROPE_THETA = 10000.0

D_FF_2 = 4 * D_MODEL

SWA_Q_COLS = SWA_HEADS * SWA_HEAD_DIM
SWA_KV_COLS = SWA_KV_HEADS * SWA_HEAD_DIM
OFF_SWA_Q = 0
OFF_SWA_K = OFF_SWA_Q + SWA_Q_COLS
OFF_SWA_V = OFF_SWA_K + SWA_KV_COLS
OFF_MLA_CQ = OFF_SWA_V + SWA_KV_COLS
OFF_MLA_CKV = OFF_MLA_CQ + MLA_Q_RANK
OFF_MLA_KR = OFF_MLA_CKV + MLA_KV_RANK
IN_COLS_2 = OFF_MLA_KR + MLA_ROPE_DIM
SWA_OUT = SWA_HEADS * SWA_HEAD_DIM
MLA_OUT = MLA_HEADS * MLA_V_DIM


def rmsnorm_2(x, g):
    x32 = x.astype(jnp.float32)
    y = x32 * lax.rsqrt(jnp.mean(x32 * x32, axis=-1, keepdims=True) + EPS)
    return y.astype(x.dtype) * g

def t5_causal_bucket(dist):
    n = jnp.maximum(dist, 0)
    max_exact = REL_BUCKETS // 2
    is_small = n < max_exact
    nf = jnp.maximum(n, 1).astype(jnp.float32)
    large = max_exact + (jnp.log(nf / max_exact) / math.log(REL_MAX_DIST / max_exact)
                         * (REL_BUCKETS - max_exact)).astype(jnp.int32)
    large = jnp.minimum(large, REL_BUCKETS - 1)
    return jnp.where(is_small, n, large)

def rope(x, positions):
    half = x.shape[-1] // 2
    inv_freq = ROPE_THETA ** (-jnp.arange(half, dtype=jnp.float32) / half)
    ang = positions.astype(jnp.float32)[:, None] * inv_freq[None, :]
    extra = x.ndim - 3
    ang = ang.reshape((1, ang.shape[0]) + (1,) * extra + (half,))
    cos = jnp.cos(ang).astype(x.dtype)
    sin = jnp.sin(ang).astype(x.dtype)
    x1, x2 = x[..., :half], x[..., half:]
    return jnp.concatenate([x1 * cos - x2 * sin, x2 * cos + x1 * sin], axis=-1)

def swa_sink_attention(q, k, v, sinks, rel_bias):
    B, S = q.shape[0], q.shape[1]
    nb = S // BLOCK
    qb = q.reshape(B, nb, BLOCK, SWA_KV_HEADS, SWA_GROUP, SWA_HEAD_DIM)
    kb = k.reshape(B, nb, BLOCK, SWA_KV_HEADS, SWA_HEAD_DIM)
    vb = v.reshape(B, nb, BLOCK, SWA_KV_HEADS, SWA_HEAD_DIM)
    zero = jnp.zeros_like(kb[:, :1])
    k_band = jnp.concatenate([jnp.concatenate([zero, kb[:, :-1]], axis=1), kb], axis=2)
    v_band = jnp.concatenate([jnp.concatenate([zero, vb[:, :-1]], axis=1), vb], axis=2)
    s = jnp.einsum('bnqhgd,bnkhd->bnhgqk', qb, k_band).astype(jnp.float32) * (SWA_HEAD_DIM ** -0.5)

    q_loc = jnp.arange(BLOCK)[:, None]
    k_loc = jnp.arange(2 * BLOCK)[None, :]
    dist = q_loc + BLOCK - k_loc
    in_window = (dist >= 0) & (dist < WINDOW)
    blk = jnp.arange(nb)[:, None]
    key_valid = (blk * BLOCK - BLOCK + k_loc) >= 0
    mask = in_window[None] & key_valid[:, None, :]

    bias = rel_bias.astype(jnp.float32)[t5_causal_bucket(dist)]
    bias = bias.transpose(2, 0, 1).reshape(SWA_KV_HEADS, SWA_GROUP, BLOCK, 2 * BLOCK)
    s = s + bias[None, None]
    s = jnp.where(mask[None, :, None, None], s, -jnp.inf)

    sink = sinks.astype(jnp.float32).reshape(SWA_KV_HEADS, SWA_GROUP)[None, None, :, :, None, None]
    m = jnp.maximum(jnp.max(s, axis=-1, keepdims=True), sink)
    p = jnp.exp(s - m)
    p = p / (jnp.sum(p, axis=-1, keepdims=True) + jnp.exp(sink - m))
    o = jnp.einsum('bnhgqk,bnkhd->bnqhgd', p.astype(v.dtype), v_band)
    return o.reshape(B, S, SWA_OUT)

def mla_attention(q_nope, q_rope, k_nope, k_rope, v):
    B, S = q_nope.shape[0], q_nope.shape[1]
    nb = S // BLOCK
    qn = q_nope.reshape(B, nb, BLOCK, MLA_HEADS, MLA_NOPE_DIM).transpose(1, 0, 2, 3, 4)
    qr = q_rope.reshape(B, nb, BLOCK, MLA_HEADS, MLA_ROPE_DIM).transpose(1, 0, 2, 3, 4)
    key_pos = jnp.arange(S)
    scale = MLA_QK_DIM ** -0.5

    def one_block(args):
        i, qn_i, qr_i = args
        s = (jnp.einsum('bqhd,bkhd->bhqk', qn_i, k_nope)
             + jnp.einsum('bqhd,bkd->bhqk', qr_i, k_rope)).astype(jnp.float32) * scale
        q_pos = i * BLOCK + jnp.arange(BLOCK)
        causal = key_pos[None, :] <= q_pos[:, None]
        s = jnp.where(causal[None, None], s, -jnp.inf)
        p = jax.nn.softmax(s, axis=-1)
        return jnp.einsum('bhqk,bkhd->bqhd', p.astype(v.dtype), v)

    o = lax.map(one_block, (jnp.arange(nb), qn, qr))
    return o.transpose(1, 0, 2, 3, 4).reshape(B, S, MLA_OUT)

def second_inputs(seed: int = 0) -> dict:
    key = jax.random.key(seed)
    ks = jax.random.split(key, 20)
    f32 = jnp.float32
    nrm = lambda k, shape, s: jax.random.normal(k, shape, f32) * s
    return {
        "x": nrm(ks[0], (BATCH, SEQ, D_MODEL), 1.0),
        "c": nrm(ks[1], (BATCH, D_MODEL), 1.0),
        "w_mod": nrm(ks[2], (DEPTH, D_MODEL, 6 * D_MODEL), 0.5 * D_MODEL ** -0.5),
        "b_mod": nrm(ks[3], (DEPTH, 6 * D_MODEL), 0.01),
        "attn_norm_g": 1.0 + nrm(ks[4], (DEPTH, D_MODEL), 0.02),
        "w_in": nrm(ks[5], (DEPTH, D_MODEL, IN_COLS_2), D_MODEL ** -0.5),
        "swa_sinks": nrm(ks[6], (DEPTH, SWA_HEADS), 1.0),
        "rel_bias": nrm(ks[7], (REL_BUCKETS, SWA_HEADS), 0.5),
        "mla_q_norm_g": 1.0 + nrm(ks[8], (DEPTH, MLA_Q_RANK), 0.02),
        "w_uq": nrm(ks[9], (DEPTH, MLA_Q_RANK, MLA_HEADS * MLA_QK_DIM), MLA_Q_RANK ** -0.5),
        "mla_kv_norm_g": 1.0 + nrm(ks[10], (DEPTH, MLA_KV_RANK), 0.02),
        "w_ukv": nrm(ks[11], (DEPTH, MLA_KV_RANK, MLA_HEADS * (MLA_NOPE_DIM + MLA_V_DIM)), MLA_KV_RANK ** -0.5),
        "w_out": nrm(ks[12], (DEPTH, MIX_WIDTH, D_MODEL), MIX_WIDTH ** -0.5),
        "mlp_norm_g": 1.0 + nrm(ks[13], (DEPTH, D_MODEL), 0.02),
        "w_ff1": nrm(ks[14], (DEPTH, D_MODEL, D_FF_2), D_MODEL ** -0.5),
        "w_ff2": nrm(ks[15], (DEPTH, D_FF_2, D_MODEL), D_FF_2 ** -0.5),
        "final_norm_g": 1.0 + nrm(ks[16], (D_MODEL,), 0.02),
    }

def second_block(x, c, w_mod, b_mod, attn_norm_g, w_in, swa_sinks, rel_bias, mla_q_norm_g, w_uq,
              mla_kv_norm_g, w_ukv, w_out, mlp_norm_g, w_ff1, w_ff2, final_norm_g):
    B, S, _ = x.shape
    positions = jnp.arange(S)
    c_act = jax.nn.silu(c)
    for l in range(DEPTH):
        mod = c_act @ w_mod[l] + b_mod[l]
        sh1, sc1, g1, sh2, sc2, g2 = [m[:, None, :] for m in jnp.split(mod, 6, axis=-1)]

        h = rmsnorm_2(x, attn_norm_g[l]) * (1.0 + sc1) + sh1
        proj = jnp.einsum('bsd,df->bsf', h, w_in[l])

        q_a = proj[..., OFF_SWA_Q:OFF_SWA_K].reshape(B, S, SWA_HEADS, SWA_HEAD_DIM)
        k_a = proj[..., OFF_SWA_K:OFF_SWA_V].reshape(B, S, SWA_KV_HEADS, SWA_HEAD_DIM)
        v_a = proj[..., OFF_SWA_V:OFF_MLA_CQ].reshape(B, S, SWA_KV_HEADS, SWA_HEAD_DIM)
        o_a = swa_sink_attention(q_a, k_a, v_a, swa_sinks[l], rel_bias)

        c_q = rmsnorm_2(proj[..., OFF_MLA_CQ:OFF_MLA_CKV], mla_q_norm_g[l])
        c_kv = rmsnorm_2(proj[..., OFF_MLA_CKV:OFF_MLA_KR], mla_kv_norm_g[l])
        k_rope = rope(proj[..., OFF_MLA_KR:IN_COLS_2], positions)
        q_b = jnp.einsum('bsr,rf->bsf', c_q, w_uq[l]).reshape(B, S, MLA_HEADS, MLA_QK_DIM)
        q_nope = q_b[..., :MLA_NOPE_DIM]
        q_rope = rope(q_b[..., MLA_NOPE_DIM:], positions)
        kv_b = jnp.einsum('bsr,rf->bsf', c_kv, w_ukv[l]).reshape(B, S, MLA_HEADS, MLA_NOPE_DIM + MLA_V_DIM)
        k_nope = kv_b[..., :MLA_NOPE_DIM]
        v_b = kv_b[..., MLA_NOPE_DIM:]
        o_b = mla_attention(q_nope, q_rope, k_nope, k_rope, v_b)

        mix = jnp.concatenate([o_a, o_b], axis=-1)
        x = x + g1 * jnp.einsum('bsm,md->bsd', mix, w_out[l])

        h = rmsnorm_2(x, mlp_norm_g[l]) * (1.0 + sc2) + sh2
        u = jax.nn.relu(jnp.einsum('bsd,df->bsf', h, w_ff1[l]))
        x = x + g2 * jnp.einsum('bsf,fd->bsd', u * u, w_ff2[l])
    return rmsnorm_2(x, final_norm_g)


def setup_inputs(seed=0):
    out = dict(first_inputs(seed))
    for name, value in second_inputs(seed + 1).items():
        if name != "x":
            out[name + "_2"] = value
    return out


def reference(
    x, p, attn_norm, w_in, fox_bf, lb_logits, hgrn_onorm, fox_qnorm, fox_knorm, moba_qnorm,
    moba_knorm, w_out, ffn_norm, w_gate, w_up, conv_w, conv_b, w_down, ple_norm, w_ple_gate,
    w_ple_proj, c_2, w_mod_2, b_mod_2, attn_norm_g_2, w_in_2, swa_sinks_2, rel_bias_2,
    mla_q_norm_g_2, w_uq_2, mla_kv_norm_g_2, w_ukv_2, w_out_2, mlp_norm_g_2, w_ff1_2, w_ff2_2,
    final_norm_g_2,
):
    x = first_block(
        x, p, attn_norm, w_in, fox_bf, lb_logits, hgrn_onorm, fox_qnorm, fox_knorm, moba_qnorm,
        moba_knorm, w_out, ffn_norm, w_gate, w_up, conv_w, conv_b, w_down, ple_norm, w_ple_gate,
        w_ple_proj,
    )
    return second_block(
        x, c_2, w_mod_2, b_mod_2, attn_norm_g_2, w_in_2, swa_sinks_2, rel_bias_2,
        mla_q_norm_g_2, w_uq_2, mla_kv_norm_g_2, w_ukv_2, w_out_2, mlp_norm_g_2, w_ff1_2,
        w_ff2_2, final_norm_g_2,
    )


_drawn_inputs = setup_inputs


def setup_inputs(seed=0):
    import zlib

    import numpy as np

    out = dict(_drawn_inputs(seed))
    spreads = {}
    factors = {'attn_norm': 3.946,
     'fox_bf': 4.395,
     'hgrn_onorm': 8.0,
     'fox_qnorm': 8.0,
     'fox_knorm': 8.0,
     'moba_qnorm': 8.0,
     'moba_knorm': 8.0,
     'ffn_norm': 4.233,
     'conv_b': 8.0,
     'ple_norm': 64.0,
     'b_mod_2': 5.096,
     'attn_norm_g_2': 8.0,
     'swa_sinks_2': 200.0,
     'rel_bias_2': 12.301,
     'mla_q_norm_g_2': 31.587,
     'mla_kv_norm_g_2': 38.469,
     'mlp_norm_g_2': 22.836,
     'final_norm_g_2': 21.845}
    for name, (base, spread) in spreads.items():
        noise = np.random.default_rng([zlib.crc32(name.encode()), seed]).standard_normal(out[name].shape)
        drawn = base * np.exp(spread * noise) if base else spread * noise
        out[name] = __import__('jax').numpy.asarray(drawn.astype(out[name].dtype))
    for name, factor in factors.items():
        out[name] = (out[name] * factor).astype(out[name].dtype)
    return out
```

```python
from contextlib import ExitStack

import numpy as np
import concourse.bass as bass
from concourse import mybir

F32 = mybir.dt.float32
F32R = mybir.dt.float32r
ACT = mybir.ActivationFunctionType
ALU = mybir.AluOpType
AX = mybir.AxisListType

P = 128
T = 256
DM = 2048
KB = DM // P
EPS = 1e-6
TINY = 1e-30
NEG = -1e30
HD = 128
A_H, B_H, C_H = 4, 6, 6
D_FF = 5632
D_FF2 = 8192
SWA_H, SWA_D, SWA_KV = 16, 64, 2
MLA_H, MLA_N, MLA_R = 8, 128, 64
MLA_QR, MLA_KVR = 384, 128
REL = 32
LVL = [1, 2, 4, 8, 16, 32, 64]
LN_SPLIT = 2.0 ** -40
SLOPES = [float(np.float32(2.0) ** np.float32(-8.0 * (i + 1) / C_H)) for i in range(C_H)]

CH = 4
NC1 = D_FF // (CH * P)
NC2 = D_FF2 // (CH * P)
U_A, U_B, U_C = 16, 19, 18
U_OUT = 16
U_FFN1 = NC1 * 12
U_PLEP, U_PLEG = 2, 16
U_IN2 = 16
U_UQ, U_UKV = 3, 2
U_FFN2 = NC2 * 8
UNITS = U_A + U_B + U_C + U_OUT + U_FFN1 + U_PLEP + U_PLEG + U_IN2 + U_UQ + U_UKV + U_OUT + U_FFN2
RAW = 4
HS = 4
LOOK = 3
NMOD = 2 * 6 * KB
MOD_SLOTS = 2

COLS = {}
_n = 0
for _name, _k in (("attn", 16), ("ffn", 16), ("ple", 16), ("attn2", 16), ("mlp2", 16), ("final", 16),
                  ("fq", 1), ("fk", 1), ("mq", 1), ("mk", 1), ("onorm", 1), ("lb", 4),
                  ("qn", 3), ("kvn", 1), ("bf", 1), ("sink", 16), ("bmod", 96), ("conv", 16 * NC1)):
    COLS[_name] = (_n, _k)
    _n += _k
NPAR = _n


def stages(*names):
    return {n: i + 1 for i, n in enumerate(names)}


class Counts:

    def __init__(self, eng, **start):
        self.eng, self.n, self.i, self.per = eng, dict(start), None, {}

    def val(self, name, value):
        step = self.per.get(name, 0)
        return value + self.i * step if step else value

    def loop(self, times, body, **per):
        before = dict(self.n)
        with self.eng.Fori(0, times) as i:
            self.i, self.per = i, per
            body()
        up = {k: self.n[k] - before[k] for k in self.n}
        assert all(up[k] == per.get(k, 0) for k in up), (up, per)
        self.i, self.per = None, {}
        for k in up:
            self.n[k] = before[k] + times * up[k]


HA = stages("exp_f", "exp_nf", "lb_exp", "ln", "exp_nq", "exp_ng", "vtok",
            *[f"exp{m}" for m in LVL + [128]], "at01", "sq", "rstd")
HV = stages("lb_d", "ln_in", "w_free_q", "w_free_g", "silu_g",
            *[x for m in LVL + [128] for x in (f"dec{m}", f"kq{m}")], "var", "done")
HP = stages("vT", "lvl0", *[f"lvl{m}" for m in LVL + [128]], "o", "var")


def build(nc, a):
    ctx = ExitStack()
    with ctx:
        base = [16512]

        def at(name, shape, off_kb, dt=F32):
            return nc.alloc_sbuf_tensor_at(name, shape, dt, offset=base[0] + int(off_kb * 1024))

        def sem(name):
            return ctx.enter_context(nc.semaphore(name))

        raw = at("raw", [P, RAW, 2048], 0)
        wh = at("wh", [P, HS, 1024], 32, F32R)
        wl = at("wl", [P, HS, 1024], 48, F32R)
        modraw = at("modraw", [P, MOD_SLOTS, 1024], 64)
        cb = at("cb", [P, 2048], 72)
        tbias = at("tbias", [P, SWA_H, T], 64)
        x = at("x", [P, KB, T], 80)
        xs = at("xs", [P, KB, 2, T], 96, F32R)
        mix = at("mix", [P, KB, T], 128)
        sec = at("sec", [P, 37, T], 144)
        S0, S1 = 0, 19
        ident = at("ident", [P, P], 181)
        ones = at("ones", [P, P], 181.5)
        dist = at("dist", [P, T], 182)
        causal = at("causal", [P, T], 183)
        par = at("par", [P, NPAR], 184)
        mod = at("mod", [P, 6 * KB], 185.75)
        modt = at("modt", [P, 32], 186.125)
        modp = at("modp", [P, NMOD], 186.25)
        gmod = at("gmod", [P, 2 * KB], 187)
        small = at("small", [P, 64], 187.125)
        gsc = at("gsc", [P, 2], 187.375)
        sil = at("sil", [P, 2048], 144)
        T0 = 187.5
        sq = at("sq", [P, 2, 4, T], T0)
        var = at("var", [P, T], T0 + 8)
        rstd = at("rstd", [P, T], T0 + 9)
        yn = at("yn", [P, 4, T], T0 + 10)
        kk = at("kk", [P, A_H, T], T0)
        kq = at("kq", [P, A_H, T], T0 + 4)
        atd = at("atd", [P, 2, 512], T0 + 8)
        at01 = at("at01", [P, 512], T0 + 12)
        vtok = at("vtok", [P, 2, 512], T0 + 14)
        hmask = at("hmask", [P, 8, P], 128 + 8)
        htmp = at("htmp", [P, 512], T0 + 18)
        logit = at("logit", [P, 3, T], T0)
        prob = at("prob", [P, 3, T], T0 + 3)
        probT = at("probT", [P, 3, T], T0 + 6)
        vt = at("vt", [P, 2, 8 * P], T0 + 9)
        gtmp = at("gtmp", [B_H, T], T0 + 17)
        fnp = at("fnp", [B_H, 2, T], T0 + 18)
        hsq = at("hsq", [P, 2, 512], T0)
        hvr = at("hvr", [P, 2, 512], T0 + 4)
        hsq4 = at("hsq4", [P, 4, T], T0)
        cossin = at("cossin", [P, 2, T], T0)
        perm = at("perm", [P, P], T0 + 2)
        rtmp = at("rtmp", [P, 2, T], T0 + 3)
        relb = at("relb", [REL + 1, SWA_H], T0)
        relh = at("relh", [REL + 1, SWA_H, P], T0 + 0.5)
        oneh = at("oneh", [REL + 1, 384], T0 + 8.5)
        rrow = at("rrow", [P, 4, 384], T0 + 10)
        hg = at("hg", [P, CH, T + 2], 144)
        cv = at("cv", [P, 4, T], 148.25)
        gel = at("gel", [P, CH, T], 152.25)
        up = at("up", [P, 2, T], 156.25)
        yf = at("yf", [P, 2, T], 158.25)
        cvp = at("cvp", [P, 16], 160.25)
        hs = at("hs", [P, 2, CH, 2, T], 161, F32R)

        PS = [ctx.enter_context(nc.psum_tensor(f"ps{i}", [P, 512], F32)) for i in range(8)]
        rel_dram = nc.dram_tensor("rel_rows", [4, P, 4, 384], F32, kind="Internal").ap()

        s_raw = [sem(f"raw_loaded{i}") for i in range(RAW)]
        s_round, s_split, s_used, s_evac = map(sem, ("hi_rounded", "lo_ready", "half_used", "block_taken"))
        s_modl = [sem(f"mod_loaded{i}") for i in range(MOD_SLOTS)]
        s_modu, s_mod = sem("mod_used"), sem("mod_ready")
        s_dch, s_ach = sem("dve_chain"), sem("act_chain")
        s_par, s_x, s_p, s_c, s_hm, s_cs, s_cact = map(sem, (
            "params_loaded", "x_loaded", "p_loaded", "c_loaded", "hmask_loaded", "cossin_loaded", "c_exp_ready"))
        s_ones = sem("ones_ready")
        s_sq, s_ssq, s_var, s_rstd, s_yn, s_yh, s_xs = map(sem, (
            "squares_ready", "square_sums", "inv_var_ready", "rstd_ready", "normed", "x_hi_ready", "x_pair_ready"))
        s_ha, s_hv, s_hp = map(sem, ("hgrn_act", "hgrn_dve", "hgrn_pe"))
        s_hsq, s_hss, s_hvar, s_hr, s_qk = map(sem, (
            "head_squares", "head_square_sums", "head_inv_var", "head_rstd", "qk_ready"))
        s_vT, s_vt, s_fa, s_fv = map(sem, ("v_transposed", "v_tokens", "gate_act", "gate_dve"))
        s_sc, s_lg, s_nm, s_ex, s_pr, s_tr, s_pt, s_pv, s_oe = map(sem, (
            "scores_ready", "scores_taken", "neg_max_ready", "exp_ready", "probs_ready",
            "probs_transposed", "probsT_copied", "pv_ready", "out_taken"))
        s_rl, s_rh, s_rp, s_rr, s_rw, s_rb = map(sem, (
            "rel_loaded", "rel_spread", "rel_rows_psum", "rel_rows_sbuf", "rel_rows_written", "bias_loaded"))
        s_pm, s_kvr = map(sem, ("rope_swapped", "rope_done"))
        s_conv, s_gel, s_hy, s_hh, s_h = map(sem, ("conv_ready", "gelu_ready", "h_ready", "h_hi_ready", "h_pair_ready"))
        s_ps, s_pled = map(sem, ("ple_sigmoid", "ple_added"))
        s_fin, s_out = map(sem, ("final_ready", "out_stored"))

        block = ctx.enter_context(nc.Block())
        cols = lambda name: par[:, COLS[name][0]:COLS[name][0] + COLS[name][1]]
        col = lambda name, k=0: par[:, COLS[name][0] + k:COLS[name][0] + k + 1]

        FIRST = {}
        u0 = b0 = 0
        for name, nu, nb in (("A", U_A, 16), ("B", U_B, 19), ("C", U_C, 18), ("out", U_OUT, 16),
                             ("ffn1", U_FFN1, NC1 * 24), ("plep", U_PLEP, 16), ("pleg", U_PLEG, 16),
                             ("in2", U_IN2, 16), ("uq", U_UQ, 12), ("ukv", U_UKV, 16),
                             ("out2", U_OUT, 16), ("ffn2", U_FFN2, NC2 * 20)):
            FIRST[name] = (u0, b0)
            u0 += nu
            b0 += nb
        FIRST["end"] = (u0, b0)
        assert u0 == UNITS

        J_FOX, J_MOBA, J_SWA, J_MLA = 0, 2 * B_H, 2 * (B_H + C_H), 2 * (B_H + C_H + SWA_H)
        J_END = J_MLA + 2 * MLA_H
        N_ATTN, N_FFN, N_PLE, N_ATTN2, N_MLP2, N_FINAL = range(6)
        XS = {}
        n = 0
        for name, k in (("attn", 16), ("mix", 16), ("ffn", 16), ("p", 2), ("ple", 16), ("attn2", 16),
                        ("cq", 4), ("mix2", 16), ("mlp2", 16)):
            XS[name] = n
            n += k
        DONE = {"out": FIRST["ffn1"][1], "ffn1": FIRST["plep"][1], "out2": FIRST["ffn2"][1], "ffn2": FIRST["end"][1]}
        H0 = CH * NC1

        HN_FOX, HN_MOBA, HN_MLA = 0, 6, 12

        def gemm_blocks(kind, h):
            if kind == "full":
                return [(0, [(t, 8 * h + t) for t in range(8)], h == 0, h == 1)]
            if kind == "quad":
                return [(2 * h + b, [(4 * b + k, k) for k in range(4)], True, True) for b in range(2)]
            if kind == "uq":
                return [(2 * h + b, [(3 * b + k, k) for k in range(3)], True, True) for b in range(2)]
            if kind == "oct":
                return [(4 * h + b, [(2 * b + k, k) for k in range(2)], True, True) for b in range(4)]
            return [(4 * h + b, [(b, 0)], True, True) for b in range(4)]

        NBLK = {"full": 1, "quad": 4, "uq": 4, "oct": 8, "one": 8}
        GAIN_XS = {N_ATTN: "attn", N_FFN: "ffn", N_PLE: "ple", N_ATTN2: "attn2", N_MLP2: "mlp2"}

        qt = lambda t: slice(t * P, (t + 1) * P)

        def fox_job(j):
            h, t = divmod(j, 2)
            nk = P * (t + 1)
            sel = ident[0:B_H, h:h + 1]
            return dict(nk=nk, h=h,
                        scores=[(sec[:, S0 + h, qt(t)], sec[:, S0 + B_H + h, 0:nk]),
                                (fnp[:, 0, qt(t)], sel.to_broadcast([B_H, nk])),
                                (sel.to_broadcast([B_H, P]), fnp[:, 1, 0:nk])],
                        bias=causal[:, T - nk:T], scale=1.0, slope=None, sink=None,
                        v=[vt[:, q, h * P:(h + 1) * P] for q in range(2)],
                        orow=(0, P), out=mix[:, A_H + h, qt(t)])

        def moba_job(j):
            h, t = divmod(j, 2)
            nk = P * (t + 1)
            return dict(nk=nk, h=h, scores=[(sec[:, S1 + h, qt(t)], sec[:, S1 + C_H + h, 0:nk])],
                        bias=dist[:, T - nk:T], scale=None, slope=SLOPES[h], sink=None,
                        v=[vt[:, q, h * P:(h + 1) * P] for q in range(2)],
                        orow=(0, P), out=mix[:, A_H + B_H + h, qt(t)])

        SWA_K, SWA_V, CQ, CKV, KR = 8, 10, 11, 14, 15
        QN, QR, KN, MLA_V0 = 16, 24, 28, 0
        ROPE = [QR, QR + 1, QR + 2, QR + 3, KR]

        def swa_job(j):
            h, t = divmod(j, 2)
            nk = P * (t + 1)
            r = slice(SWA_D * (h % 2), SWA_D * (h % 2) + SWA_D)
            kv = h // (SWA_H // SWA_KV)
            return dict(nk=nk, h=h, scores=[(sec[r, h // 2, qt(t)], sec[r, SWA_K + kv, 0:nk])],
                        bias=tbias[:, h, T - nk:T], scale=SWA_D ** -0.5, slope=None, sink=col("sink", h),
                        v=[vt[:, 0, q * P + kv * SWA_D:q * P + (kv + 1) * SWA_D] for q in range(2)],
                        orow=(SWA_D * (h % 2), SWA_D), out=mix[r, h // 2, qt(t)])

        def mla_job(j):
            h, t = divmod(j, 2)
            nk = P * (t + 1)
            r = slice(MLA_R * (h % 2), MLA_R * (h % 2) + MLA_R)
            return dict(nk=nk, h=h, scores=[(sec[:, QN + h, qt(t)], sec[:, KN + h, 0:nk]),
                                            (sec[r, QR + h // 2, qt(t)], sec[r, KR, 0:nk])],
                        bias=causal[:, T - nk:T], scale=(MLA_N + MLA_R) ** -0.5, slope=None, sink=None,
                        v=[vt[:, q, h * P:(h + 1) * P] for q in range(2)],
                        orow=(0, P), out=mix[:, 8 + h, qt(t)])

        @block.sync
        def _(sp):
            sp.dma_start(x[:, :, :], a["x"]).then_inc(s_x, 16)
            for dst, src in ((par[:, :], a["par"]), (ident[:, :], a["ident"]),
                             (dist[:, :], a["dist"]), (causal[:, :], a["causal"])):
                sp.dma_start(dst, src).then_inc(s_par, 16)
            for u in range(RAW):
                sp.dma_start(raw[:, u, :], a["w"][u, :, :]).then_inc(s_raw[u], 16)
            sp.dma_start(hmask[:, :, :], a["hmask"]).then_inc(s_hm, 16)
            rounds, rest = divmod(UNITS - RAW, RAW)
            with sp.Fori(0, rounds) as i:
                for r in range(RAW):
                    sp.wait_ge(s_split, i * (2 * RAW) + 2 * r + 2)
                    sp.dma_start(raw[:, r:r + 1, :],
                                 a["w"][bass.ds(i * RAW + (RAW + r), 1), :, :].rearrange("a p n -> p a n")
                                 ).then_inc(s_raw[r], 16)
            for r in range(rest):
                u = RAW * (rounds + 1) + r
                sp.wait_ge(s_split, 2 * (u - RAW) + 2)
                sp.dma_start(raw[:, r, :], a["w"][u, :, :]).then_inc(s_raw[r], 16)
            for q in range(4):
                sp.wait_ge(s_fin, 4 * q + 4)
                sp.dma_start(a["out"][:, 4 * q:4 * q + 4, :], mix[:, 4 * q:4 * q + 4, :]).then_inc(s_out, 16)
            sp.wait_ge(s_out, 64)

        @block.gpsimd
        def _(pool):
            pool.dma_start(cb[:, :], a["c"]).then_inc(s_c, 16)
            for n in range(MOD_SLOTS):
                pool.dma_start(modraw[:, n, :], a["wmod"][n, :, :]).then_inc(s_modl[n], 16)
            with pool.Fori(0, NMOD // MOD_SLOTS - 1) as i:
                for n in range(MOD_SLOTS):
                    pool.wait_ge(s_modu, i * MOD_SLOTS + n + 1)
                    pool.dma_start(modraw[:, n:n + 1, :],
                                   a["wmod"][bass.ds(i * MOD_SLOTS + (MOD_SLOTS + n), 1), :, :]
                                   .rearrange("a p n -> p a n")).then_inc(s_modl[n], 16)
            pool.wait_ge(s_xs, XS["attn2"] + 16)
            pool.wait_ge(s_mod, 1)
            pool.dma_start(relb[:, :], a["rel"]).then_inc(s_rl, 16)
            pool.dma_start(oneh[:, :], a["oneh"]).then_inc(s_rl, 16)
            for g in range(4):
                pool.wait_ge(s_rr, g + 1)
                pool.dma_start(rel_dram[g, :, :, :], rrow[:, :, :]).then_inc(s_rw, 16)
                pool.wait_ge(s_rw, 16 * (g + 1))
                for h in range(4):
                    src = bass.AP(tensor=rel_dram.tensor, offset=g * P * 1536 + h * 384 + P - 1,
                                  ap=[[1536 - 1, P], [1, T]])
                    pool.dma_start(tbias[:, 4 * g + h, :], src).then_inc(s_rb, 16)
            pool.wait_ge(s_qk, 3)
            pool.dma_start(cossin[:, :, :], a["cossin"]).then_inc(s_cs, 16)
            pool.dma_start(perm[:, :], a["perm"]).then_inc(s_cs, 16)

        @block.tensor
        def _(pe):
            c = Counts(pe, h=0, b=0, hp=0)

            def unit(kind, src, xwait=None):
                for half in range(2):
                    hh, b = c.n["h"], c.n["b"]
                    pe.wait_ge(s_split, c.val("h", hh + 1))
                    hi, lo = wh[:, hh % HS, :], wl[:, hh % HS, :]
                    for bi, tiles, first, last in gemm_blocks(kind, half):
                        if first and b + bi >= 4:
                            pe.wait_ge(s_evac, c.val("b", b + bi - 3))
                        out = PS[(b + bi) % 4]
                        for n, (t, k) in enumerate(tiles):
                            if xwait and (half == 0 or kind == "full"):
                                pe.wait_ge(s_xs, XS[xwait] + k + 1)
                            w = slice(t * P, (t + 1) * P)
                            s, e = first and n == 0, last and n == len(tiles) - 1
                            pair = src[:, k, :, :].rearrange("p a t -> p (a t)")
                            if e and not s:
                                nc.tensor.matmul(out[:, 0:T], lo[:, w], src[:, k, 0, :], start=False, stop=False)
                                m = nc.tensor.matmul(out[:, :], hi[:, w], pair, start=False, stop=True)
                            else:
                                nc.tensor.matmul(out[:, :], hi[:, w], pair, start=s, stop=e)
                                m = nc.tensor.matmul(out[:, 0:T], lo[:, w], src[:, k, 0, :], start=False,
                                                     stop=e, skip_group_check=e)
                    m.then_inc(s_used, 1)
                    c.n["h"] += 1
                c.n["b"] += NBLK[kind]

            def fulls(n, name):
                unit("full", xs, name)
                for j in range(1, n - (n - 1) // 4 * 4):
                    unit("full", xs)
                c.loop((n - 1) // 4, lambda: [unit("full", xs) for _ in range(4)], h=8, b=4)

            def norm(n):
                for k in range(KB):
                    if k % 4 == 0:
                        pe.wait_ge(s_sq, 4 * n + k // 4 + 1)
                    m = nc.tensor.matmul(PS[4][:, 0:T], ones[:, :], sq[:, (k // 4) % 2, k % 4, :],
                                         start=k == 0, stop=k == KB - 1)
                    if k % 4 == 3:
                        m.then_inc(s_ssq, 1)

            def head_sums(n):
                for j in range(6):
                    pe.wait_ge(s_hsq, n + j + 1)
                    if j >= 2:
                        pe.wait_ge(s_hvar, n + j - 1)
                    nc.tensor.matmul(PS[4 + j % 2][:, :], ones[:, :], hsq[:, j % 2, :],
                                     start=True, stop=True).then_inc(s_hss, 1)

            def v_transposes(n, blocks):
                for g in range(len(blocks) // 2):
                    if g >= 2:
                        pe.wait_ge(s_vt, n + g - 1)
                    for q in range(2):
                        for t in range(2):
                            m = nc.tensor.transpose(PS[6 + g % 2][:, (2 * t + q) * P:(2 * t + q + 1) * P],
                                                    sec[:, blocks[2 * g + q], qt(t)], ident[:, :])
                    m.then_inc(s_vT, 1)

            def jobs(j0, make, n):
                for j in range(n + 3):
                    if j < n:
                        d, J = make(j), j0 + j
                        if j >= 2:
                            pe.wait_ge(s_lg, J - 1)
                        for q, (l, r) in enumerate(d["scores"]):
                            m = nc.tensor.matmul(PS[4 + J % 2][:, 0:d["nk"]], l, r, start=q == 0,
                                                 stop=q == len(d["scores"]) - 1)
                        m.then_inc(s_sc, 1)
                    if 0 <= j - 3 < n:
                        d, J = make(j - 3), j0 + j - 3
                        pe.wait_ge(s_pt, J + 1)
                        if J:
                            pe.wait_ge(s_oe, J)
                        nt, (lo, w) = d["nk"] // P, d["orow"]
                        for t in range(nt):
                            m = nc.tensor.matmul(PS[7][lo:lo + w, 0:P], d["v"][t],
                                                 probT[:, J % 3, qt(t)], start=t == 0, stop=t == nt - 1)
                        m.then_inc(s_pv, 1)
                    if 0 <= j - 2 < n:
                        d, J = make(j - 2), j0 + j - 2
                        pe.wait_ge(s_pr, J + 1)
                        if J:
                            pe.wait_ge(s_pt, J)
                        for t in range(d["nk"] // P):
                            o = t * P
                            m = nc.tensor.transpose(PS[6][:, o:o + P], prob[:, J % 3, qt(t)], ident[:, :])
                        m.then_inc(s_tr, 1)

            pe.wait_ge(s_par, 64)
            pe.wait_ge(s_ones, 1)
            norm(N_ATTN)
            fulls(U_A, "attn")

            pe.wait_ge(s_evac, FIRST["B"][1])
            for t in range(2):
                for h in range(A_H):
                    m = nc.tensor.transpose(PS[6 + t][:, h * P:(h + 1) * P], sec[:, S1 + 8 + h, qt(t)], ident[:, :])
            m.then_inc(s_hp, 1)
            pe.wait_ge(s_hv, HV["silu_g"])
            for lv in [0] + LVL + [128]:
                if lv:
                    pe.wait_ge(s_hv, HV[f"kq{lv}"])
                for t in range(2 if lv < 128 else 1):
                    for h in range(A_H):
                        ks = (kq if lv else kk)[:, h, qt(t)]
                        qs = (kq[:, h, qt(t if lv < 128 else 1)] if lv else sec[:, S1 + h, qt(t)])
                        m = nc.tensor.matmul(PS[4 + t][:, h * P:(h + 1) * P], ks, qs, start=True, stop=True)
                m.then_inc(s_hp, 1)
            pe.wait_ge(s_ha, HA["at01"])
            for h in range(A_H):
                o, q, hc = PS[6 + h // 2], (h % 2) * T, slice(h * P, (h + 1) * P)
                nc.tensor.matmul(o[:, q:q + P], vtok[:, 0, hc], atd[:, 0, hc], start=True, stop=True)
                nc.tensor.matmul(o[:, q + P:q + T], vtok[:, 0, hc], at01[:, hc], start=True, stop=False)
                m = nc.tensor.matmul(o[:, q + P:q + T], vtok[:, 1, hc], atd[:, 1, hc], start=False, stop=True)
            m.then_inc(s_hp, 1)
            pe.wait_ge(s_ha, HA["sq"])
            for g in range(2):
                m = nc.tensor.matmul(PS[4 + g][:, :], ones[:, :],
                                     kq[:, 2 * g:2 * g + 2, :].rearrange("p a t -> p (a t)"), start=True, stop=True)
            m.then_inc(s_hp, 1)

            for _ in range(U_B):
                unit("full", xs)
            pe.wait_ge(s_hv, HV["done"])
            head_sums(HN_FOX)
            pe.wait_ge(s_evac, FIRST["C"][1])
            v_transposes(0, [S0 + 2 * B_H + h for h in range(B_H)])
            pe.wait_ge(s_qk, 1)
            jobs(J_FOX, fox_job, 2 * B_H)

            for _ in range(U_C):
                unit("full", xs)
            head_sums(HN_MOBA)
            pe.wait_ge(s_evac, FIRST["out"][1])
            pe.wait_ge(s_oe, J_MOBA)
            v_transposes(3, [S1 + 2 * C_H + h for h in range(C_H)])
            pe.wait_ge(s_qk, 2)
            jobs(J_MOBA, moba_job, 2 * C_H)

            fulls(U_OUT, "mix")
            norm(N_FFN)

            def down(buf):
                c.n["hp"] += CH
                pe.wait_ge(s_h, c.val("hp", c.n["hp"]))
                for _ in range(4):
                    unit("quad", hs[:, buf, :, :, :])

            def ups(name=None):
                for j in range(CH):
                    unit("full", xs, name if j == 0 else None)

            ups("ffn")
            ups()
            c.loop(NC1 - 1, lambda: (ups(), down(0), ups()), h=24, b=24, hp=CH)
            down(0)

            for j in range(U_PLEP):
                unit("oct", xs, "p" if j == 0 else None)
            norm(N_PLE)
            fulls(U_PLEG, "ple")
            norm(N_ATTN2)

            fulls(U_IN2, "attn2")
            pe.wait_ge(s_rh, 1)
            pe.wait_ge(s_rl, 32)
            for h in range(SWA_H):
                if h >= 4 and h % 4 == 0:
                    pe.wait_ge(s_rr, h // 4)
                nc.tensor.matmul(PS[4 + h % 4][:, 0:384], relh[:, h, :], oneh[:, :], start=True, stop=True).then_inc(s_rp, 1)
            pe.wait_ge(s_rr, 4)
            pe.wait_ge(s_evac, FIRST["uq"][1])
            for t in range(2):
                m = nc.tensor.transpose(PS[7][:, qt(t)], sec[:, SWA_V, qt(t)], ident[:, :])
            m.then_inc(s_vT, 1)
            pe.wait_ge(s_vt, 7)
            jobs(J_SWA, swa_job, 2 * SWA_H)

            pe.wait_ge(s_hsq, HN_MLA + 1)
            for k in range(3):
                m = nc.tensor.matmul(PS[4][:, 0:T], ones[:, :], hsq4[:, k, :], start=k == 0, stop=k == 2)
            m.then_inc(s_hss, 1)
            nc.tensor.matmul(PS[5][:, 0:T], ones[:, :], hsq4[:, 3, :], start=True, stop=True).then_inc(s_hss, 1)
            for j in range(U_UQ):
                unit("uq", xs, "cq" if j == 0 else None)
            pe.wait_ge(s_xs, XS["cq"] + 4)
            for _ in range(U_UKV):
                unit("one", xs[:, 3:4, :, :])
            pe.wait_ge(s_cs, 32)
            pe.wait_ge(s_evac, FIRST["out2"][1])
            for j, b in enumerate(ROPE):
                if j >= 2:
                    pe.wait_ge(s_kvr, j - 1)
                nc.tensor.matmul(PS[4 + j % 2][:, 0:T], perm[:, :], sec[:, b, :], start=True, stop=True).then_inc(s_pm, 1)
            pe.wait_ge(s_oe, J_MLA)
            v_transposes(7, [MLA_V0 + h for h in range(MLA_H)])
            pe.wait_ge(s_kvr, len(ROPE))
            jobs(J_MLA, mla_job, 2 * MLA_H)

            fulls(U_OUT, "mix2")
            norm(N_MLP2)

            ups("mlp2")
            ups()
            c.loop(NC2 // 2 - 1, lambda: (down(0), ups(), down(1), ups()), h=32, b=40, hp=2 * CH)
            down(0)
            down(1)
            assert c.n["h"] == 2 * UNITS and c.n["b"] == FIRST["end"][1]
            norm(N_FINAL)

        @block.scalar
        def _(act):
            c = Counts(act, h=0, g=0, y=0)

            def rnd(h):
                if h < 2 * UNITS:
                    u = h // 2
                    if h % 2 == 0:
                        v = 16 * (u // RAW + 1)
                        act.wait_ge(s_raw[u % RAW], v + c.i * (c.per["h"] * 16 // (2 * RAW)) if c.per else v)
                    if h >= HS:
                        act.wait_ge(s_used, c.val("h", h - HS + 1))
                    nc.scalar.activation(wh[:, h % HS, :], raw[:, u % RAW, (h % 2) * 1024:(h % 2 + 1) * 1024],
                                         ACT.Copy).then_inc(s_round, 1)

            def step(after=None):
                for q in range(2):
                    rnd(c.n["h"] + LOOK)
                    c.n["h"] += 1
                    if after and q == 0:
                        after()

            def steps(n):
                for _ in range(n):
                    step()

            def norm(n, name=None):
                if n:
                    act.wait_ge(s_evac, DONE[name]) if name in DONE else act.wait_ge(s_pled, KB)
                for g in range(4):
                    if 4 * n + g >= 2:
                        act.wait_ge(s_ssq, 4 * n + g - 1)
                    nc.scalar.activation(sq[:, g % 2, :, :], x[:, 4 * g:4 * g + 4, :], ACT.Square).then_inc(s_sq, 1)
                act.wait_ge(s_var, n + 1)
                nc.scalar.activation(rstd[:, :], var[:, :], ACT.Sqrt).then_inc(s_rstd, 1)
                if n != N_FINAL:
                    for k in range(KB):
                        act.wait_ge(s_yn, KB * n + k + 1)
                        nc.scalar.activation(xs[:, k, 0, :], yn[:, k % 4, :], ACT.Copy).then_inc(s_yh, 1)

            def his(phase, srcs):
                act.wait_ge(s_used, 2 * FIRST[phase][0])
                for k, s in enumerate(srcs):
                    nc.scalar.activation(xs[:, k, 0, :], s, ACT.Copy).then_inc(s_yh, 1)

            def head_norms(n, s0):
                for j in range(7):
                    if j < 6:
                        if j >= 2:
                            act.wait_ge(s_hss, n + j - 1)
                        nc.scalar.activation(hsq[:, j % 2, :], sec[:, s0 + 2 * j:s0 + 2 * j + 2, :]
                                             .rearrange("p a t -> p (a t)"), ACT.Square).then_inc(s_hsq, 1)
                    if j:
                        act.wait_ge(s_hvar, n + j)
                        nc.scalar.activation(hvr[:, (j - 1) % 2, :], hvr[:, (j - 1) % 2, :], ACT.Sqrt).then_inc(s_hr, 1)

            def v_copies(n, m):
                for g in range(m):
                    act.wait_ge(s_vT, n + g + 1)
                    nc.scalar.activation(vt[:, :, 2 * g * P:(2 * g + 2) * P],
                                         PS[6 + g % 2][:, :].rearrange("p (t c) -> p t c", t=2), ACT.Copy).then_inc(s_vt, 1)

            def jobs(j0, make, n):
                for j in range(n + 3):
                    if j < n:
                        d, J = make(j), j0 + j
                        act.wait_ge(s_nm, J + 1)
                        if j >= 3:
                            act.wait_ge(s_tr, J - 2)
                        q = J % 3
                        m = nc.scalar.activation(prob[:, q, 0:d["nk"]], logit[:, q, 0:d["nk"]], ACT.Exp,
                                                 bias=small[:, 4 * q:4 * q + 1], accum_out=small[:, 4 * q + 1:4 * q + 2])
                        if d["sink"] is not None:
                            m = nc.scalar.activation(small[:, 4 * q + 2:4 * q + 3], d["sink"], ACT.Exp,
                                                     bias=small[:, 4 * q:4 * q + 1])
                        m.then_inc(s_ex, 1)
                    if 0 <= j - 2 < n:
                        d, J = make(j - 2), j0 + j - 2
                        act.wait_ge(s_tr, J + 1)
                        if j - 2 >= 3:
                            act.wait_ge(s_pv, J - 2)
                        nc.scalar.activation(probT[:, J % 3, 0:d["nk"]], PS[6][:, 0:d["nk"]],
                                             ACT.Copy).then_inc(s_pt, 1)
                    if 0 <= j - 3 < n:
                        d, J = make(j - 3), j0 + j - 3
                        act.wait_ge(s_pv, J + 1)
                        lo, w = d["orow"]
                        nc.scalar.activation(d["out"], PS[7][lo:lo + w, 0:P], ACT.Copy).then_inc(s_oe, 1)

            act.wait_ge(s_x, 16)
            norm(N_ATTN)
            for h in range(LOOK):
                rnd(h)
            act.wait_ge(s_c, 16)
            nc.scalar.activation(sil[:, :], cb[:, :], ACT.Exp, scale=-1.0).then_inc(s_cact, 1)
            steps(U_A)

            q4, f4, g4 = (sec[:, S1 + o:S1 + o + 4, :] for o in (0, 4, 12))
            act.wait_ge(s_evac, FIRST["B"][1])
            nc.scalar.activation(kk[:, :, :], f4, ACT.Exp).then_inc(s_ha, 1)
            nc.scalar.activation(kq[:, :, :], f4, ACT.Exp, scale=-1.0).then_inc(s_ha, 1)
            act.wait_ge(s_hv, HV["lb_d"])
            nc.scalar.activation(small[:, 20:24], small[:, 16:20], ACT.Exp).then_inc(s_ha, 1)
            act.wait_ge(s_hv, HV["ln_in"])
            nc.scalar.activation(f4, f4, ACT.Ln)
            nc.scalar.activation(kq[:, :, :], kq[:, :, :], ACT.Ln, scale=1.0 / LN_SPLIT).then_inc(s_ha, 1)
            act.wait_ge(s_hv, HV["w_free_q"])
            nc.scalar.activation(kq[:, :, :], q4, ACT.Exp, scale=-1.0).then_inc(s_ha, 1)
            act.wait_ge(s_hv, HV["w_free_g"])
            nc.scalar.activation(kq[:, :, :], g4, ACT.Exp, scale=-1.0).then_inc(s_ha, 1)
            act.wait_ge(s_hp, HP["vT"])
            for t in range(2):
                m = nc.scalar.activation(vtok[:, t, :], PS[6 + t][:, :], ACT.Copy)
            m.then_inc(s_ha, 1)
            for lv in LVL + [128]:
                act.wait_ge(s_hv, HV[f"dec{lv}"])
                nc.scalar.activation(kq[:, :, :], kq[:, :, :], ACT.Exp).then_inc(s_ha, 1)
            act.wait_ge(s_hp, HP["lvl128"])
            nc.scalar.activation(at01[:, :], PS[4][:, :], ACT.Copy).then_inc(s_ha, 1)
            act.wait_ge(s_hp, HP["o"])
            for g in range(2):
                m = nc.scalar.activation(kq[:, 2 * g:2 * g + 2, :].rearrange("p a t -> p (a t)"), PS[6 + g][:, :], ACT.Square)
            m.then_inc(s_ha, 1)
            act.wait_ge(s_hv, HV["var"])
            nc.scalar.activation(kk[:, :, :], kk[:, :, :], ACT.Sqrt).then_inc(s_ha, 1)

            steps(U_B)
            act.wait_ge(s_hv, HV["done"])
            act.wait_ge(s_evac, FIRST["C"][1])
            head_norms(HN_FOX, S0)
            v_copies(0, 3)
            act.wait_ge(s_fv, 1)
            nc.scalar.activation(gtmp[:, :], sec[0:B_H, S0 + 18, :], ACT.Abs).then_inc(s_fa, 1)
            act.wait_ge(s_fa, 1)
            nc.scalar.activation(gtmp[:, :], gtmp[:, :], ACT.Exp, scale=-1.0).then_inc(s_fa, 1)
            act.wait_ge(s_fv, 2)
            nc.scalar.activation(gtmp[:, :], gtmp[:, :], ACT.Ln).then_inc(s_fa, 1)
            jobs(J_FOX, fox_job, 2 * B_H)
            steps(U_C)
            act.wait_ge(s_evac, FIRST["out"][1])
            head_norms(HN_MOBA, S1)
            v_copies(3, 3)
            jobs(J_MOBA, moba_job, 2 * C_H)
            act.wait_ge(s_oe, J_SWA)
            his("out", [mix[:, k, :] for k in range(KB)])
            c.loop(U_OUT // 4, lambda: steps(4), h=8)
            act.wait_ge(s_xs, XS["mix"] + 16)
            act.dma_start(mix[:, 0:2, :], a["p"]).then_inc(s_p, 16)
            norm(N_FFN, "out")

            def gelu(j):
                c.n["g"] += 1
                act.wait_ge(s_conv, c.val("g", c.n["g"]))
                nc.scalar.activation(gel[:, j, :], cv[:, j, :], ACT.Gelu_apprx_tanh).then_inc(s_gel, 1)

            def h_hi(buf, j):
                c.n["y"] += 1
                act.wait_ge(s_hy, c.val("y", c.n["y"]))
                nc.scalar.activation(hs[:, buf, j, 0, :], yf[:, (c.n["y"] - 1) % 2, :], ACT.Copy).then_inc(s_hh, 1)

            def gates(first=None):
                for j in range(CH):
                    step((lambda: gelu(j - 1)) if j else first)

            def ups(buf, first=None):
                for j in range(CH):
                    step((lambda: h_hi(buf, j - 1)) if j else first)

            def downs(first):
                step(first)
                steps(3)

            gates()
            ups(0, lambda: gelu(CH - 1))
            c.loop(NC1 - 1, lambda: (gates(lambda: h_hi(0, CH - 1)), downs(lambda: gelu(CH - 1)), ups(0)),
                   h=24, g=CH, y=CH)
            downs(lambda: h_hi(0, CH - 1))

            act.wait_ge(s_p, 16)
            his("plep", [mix[:, k, :] for k in range(2)])
            steps(U_PLEP)
            act.wait_ge(s_used, 2 * FIRST["pleg"][0])
            norm(N_PLE, "ffn1")

            def sigmoid(j):
                act.wait_ge(s_evac, FIRST["pleg"][1] + j + 1)
                nc.scalar.activation(yf[:, j % 2, :], yf[:, j % 2, :], ACT.Sigmoid).then_inc(s_ps, 1)
            for j in range(U_PLEG):
                step((lambda: sigmoid(j - 1)) if j else None)
            sigmoid(U_PLEG - 1)
            norm(N_ATTN2)
            c.loop(U_IN2 // 4, lambda: steps(4), h=8)

            for h in range(SWA_H):
                act.wait_ge(s_rp, h + 1)
                if h % 4 == 0 and h:
                    act.wait_ge(s_rw, 16 * (h // 4))
                m = nc.scalar.activation(rrow[:, h % 4, :], PS[4 + h % 4][:, 0:384], ACT.Copy)
                if h % 4 == 3:
                    m.then_inc(s_rr, 1)
            act.wait_ge(s_rw, 64)
            act.wait_ge(s_vT, 7)
            nc.scalar.activation(vt[:, 0, 0:T], PS[7][:, 0:T], ACT.Copy).then_inc(s_vt, 1)
            jobs(J_SWA, swa_job, 2 * SWA_H)

            act.wait_ge(s_oe, J_MLA)
            nc.scalar.activation(hsq4[:, :, :], sec[:, CQ:CQ + 4, :], ACT.Square).then_inc(s_hsq, 1)
            act.wait_ge(s_hvar, HN_MLA + 2)
            nc.scalar.activation(hvr[:, :, 0:T], hvr[:, :, 0:T], ACT.Sqrt).then_inc(s_hr, 1)
            act.wait_ge(s_qk, 3)
            his("uq", [sec[:, CQ + k, :] for k in range(4)])
            steps(U_UQ + U_UKV)
            v_copies(7, 4)
            jobs(J_MLA, mla_job, 2 * MLA_H)
            act.wait_ge(s_oe, J_END)
            his("out2", [mix[:, k, :] for k in range(KB)])
            c.loop(U_OUT // 4, lambda: steps(4), h=8)
            norm(N_MLP2, "out2")

            ups(0)
            ups(1, lambda: h_hi(0, CH - 1))
            c.loop(NC2 // 2 - 1, lambda: (downs(lambda: h_hi(1, CH - 1)), ups(0), downs(lambda: h_hi(0, CH - 1)), ups(1)),
                   h=32, y=2 * CH)
            downs(lambda: h_hi(1, CH - 1))
            steps(4)
            norm(N_FINAL, "ffn2")

        @block.vector
        def _(dve):
            c = Counts(dve, h=0, b=0, c=0, m=0, g=0, y=0, l=0)

            def link(*ins):
                for i in ins:
                    i.then_inc(s_dch, 1)
                c.n["c"] += len(ins)
                dve.wait_ge(s_dch, c.val("c", c.n["c"]))

            def sub(h):
                if h < 2 * UNITS:
                    dve.wait_ge(s_round, c.val("h", h + 1))
                    nc.vector.tensor_tensor(wl[:, h % HS, :], raw[:, (h // 2) % RAW, (h % 2) * 1024:(h % 2 + 1) * 1024],
                                            wh[:, h % HS, :].bitcast(F32), ALU.subtract).then_inc(s_split, 1)

            def half(before=None, after=None):
                if before:
                    dve.wait_ge(s_used, c.val("h", c.n["h"]))
                    before()
                sub(c.n["h"] + LOOK)
                if after:
                    after()
                c.n["h"] += 1

            def tail(before):
                dve.wait_ge(s_used, c.val("h", c.n["h"]))
                before()

            def bank():
                c.n["b"] += 1
                return PS[(c.n["b"] - 1) % 4]

            def take(dst):
                nc.vector.tensor_reduce(dst, bank()[:, :].rearrange("p (a t) -> p t a", a=2), AX.X, ALU.add
                                        ).then_inc(s_evac, 1)

            def add_blocks(ks, gate=None):
                bs = [bank() for _ in ks]
                for q in range(2):
                    ins = []
                    for k, b in zip(ks, bs):
                        if gate is None:
                            ins.append(nc.vector.tensor_tensor(x[:, k, :], b[:, q * T:(q + 1) * T], x[:, k, :], ALU.add))
                        else:
                            ins.append(nc.vector.scalar_tensor_tensor(x[:, k, :], b[:, q * T:(q + 1) * T],
                                                                      gate[:, k:k + 1], x[:, k, :], ALU.mult, ALU.add))
                    if q == 0:
                        link(*ins)
                    else:
                        for i in ins:
                            i.then_inc(s_evac, 1)

            def mods(n, where=None):
                dst = modp if where is None else modt
                for j in range(n):
                    m = c.n["m"]
                    v = 16 * (m // 2 + 1)
                    dve.wait_ge(s_modl[m % 2], v + c.i * (8 * c.per["m"]) if c.per else v)
                    o = m if where is None else where + j
                    nc.vector.tensor_tensor_reduce(out=modraw[:, m % 2, :], in0=modraw[:, m % 2, :],
                                                   in1=cb[:, (m % 2) * 1024:(m % 2 + 1) * 1024],
                                                   scale=1.0, scalar=0.0, op0=ALU.mult, op1=ALU.add,
                                                   accum_out=dst[:, o:o + 1]).then_inc(s_modu, 1)
                    c.n["m"] += 1

            def fulls(n, ev, nmod=0):
                for j in range(n):
                    half((lambda: ev(j - 1)) if j else None)
                    half(after=lambda: mods(nmod))
                tail(lambda: ev(n - 1))

            def lo(x0, k, src):
                dve.wait_ge(s_yh, x0 + k + 1)
                nc.vector.tensor_tensor(xs[:, k, 1, :], src, xs[:, k, 0, :].bitcast(F32), ALU.subtract).then_inc(s_xs, 1)

            def inv_var(dst, src, n):
                link(nc.vector.tensor_scalar(dst, src, 1.0 / n, EPS, ALU.mult, ALU.add))
                return nc.vector.reciprocal(dst, dst)

            def norm(n, gain, shift=None):
                dve.wait_ge(s_ssq, 4 * n + 4)
                inv_var(var[:, :], PS[4][:, 0:T], DM).then_inc(s_var, 1)
                dve.wait_ge(s_rstd, n + 1)
                for k in range(KB + 2):
                    if k < KB and n == N_FINAL:
                        nc.vector.scalar_tensor_tensor(mix[:, k, :], x[:, k, :], gain[:, k:k + 1], rstd[:, :],
                                                       ALU.mult, ALU.mult).then_inc(s_fin, 1)
                    elif k < KB:
                        if k >= 4:
                            dve.wait_ge(s_xs, XS[GAIN_XS[n]] + k - 3)
                        y = nc.vector.scalar_tensor_tensor(yn[:, k % 4, :], x[:, k, :], gain[:, k:k + 1], rstd[:, :],
                                                           ALU.mult, ALU.mult)
                        if shift is not None:
                            link(y)
                            y = nc.vector.tensor_scalar(yn[:, k % 4, :], yn[:, k % 4, :], shift[:, k:k + 1], None, ALU.add)
                        y.then_inc(s_yn, 1)
                    if k >= 2 and n != N_FINAL:
                        lo(XS[GAIN_XS[n]], k - 2, yn[:, (k - 2) % 4, :])

            def head_norms(n, s0, gq, gk):
                for j in range(7):
                    if j < 6:
                        dve.wait_ge(s_hss, n + j + 1)
                        inv_var(hvr[:, j % 2, :], PS[4 + j % 2][:, :], HD).then_inc(s_hvar, 1)
                    if j:
                        q = j - 1
                        dve.wait_ge(s_hr, n + j)
                        b = sec[:, s0 + 2 * q:s0 + 2 * q + 2, :].rearrange("p a t -> p (a t)")
                        m = nc.vector.scalar_tensor_tensor(b, b, gq if q < 3 else gk, hvr[:, q % 2, :], ALU.mult, ALU.mult)
                        if j < 6:
                            link(m)
                return m

            def jobs(j0, make, n):
                for j in range(n + 1):
                    if j < n:
                        d, J = make(j), j0 + j
                        q, nk = J % 3, d["nk"]
                        s = PS[4 + J % 2][:, 0:nk]
                        dve.wait_ge(s_sc, J + 1)
                        if j >= 3:
                            dve.wait_ge(s_ex, J - 2)
                        if d["slope"] is None:
                            m = nc.vector.scalar_tensor_tensor(logit[:, q, 0:nk], s, d["scale"], d["bias"], ALU.mult, ALU.add)
                        else:
                            m = nc.vector.scalar_tensor_tensor(logit[:, q, 0:nk], d["bias"], d["slope"], s, ALU.mult, ALU.add)
                        m.then_inc(s_lg, 1)
                        dve.wait_ge(s_lg, J + 1)
                        top = small[:, 4 * q + 3:4 * q + 4]
                        if J >= 3:
                            dve.wait_ge(s_nm, J - 2)
                        link(nc.vector.tensor_reduce(top, logit[:, q, 0:nk], AX.X, ALU.max))
                        if d["sink"] is None:
                            m = nc.vector.tensor_scalar(small[:, 4 * q:4 * q + 1], top, -1.0, None, ALU.mult)
                        else:
                            m = nc.vector.tensor_scalar(small[:, 4 * q:4 * q + 1], top, d["sink"], -1.0, ALU.max, ALU.mult)
                        m.then_inc(s_nm, 1)
                    if j:
                        d, J = make(j - 1), j0 + j - 1
                        q, nk = J % 3, d["nk"]
                        den = small[:, 4 * q + 1:4 * q + 2]
                        dve.wait_ge(s_ex, J + 1)
                        if d["sink"] is not None:
                            link(nc.vector.tensor_tensor(den, den, small[:, 4 * q + 2:4 * q + 3], ALU.add))
                        link(nc.vector.reciprocal(den, den))
                        nc.vector.tensor_scalar(prob[:, q, 0:nk], prob[:, q, 0:nk], den, None, ALU.mult).then_inc(s_pr, 1)

            nc.vector.memset(ones[:, :], 1.0).then_inc(s_ones, 1)
            dve.wait_ge(s_ones, 1)
            dve.wait_ge(s_par, 64)
            dve.wait_ge(s_x, 16)
            norm(N_ATTN, cols("attn"))
            for h in range(LOOK):
                sub(h)
            dve.wait_ge(s_cact, 1)
            link(nc.vector.tensor_scalar(sil[:, :], sil[:, :], 1.0, None, ALU.add))
            link(nc.vector.reciprocal(sil[:, :], sil[:, :]))
            link(nc.vector.tensor_tensor(cb[:, :], cb[:, :], sil[:, :], ALU.mult))
            fulls(U_A, lambda j: take(sec[:, S1 + j, :]), 1)

            q4, f4, i4, g4 = (sec[:, S1 + o:S1 + o + 4, :] for o in (0, 4, 8, 12))
            lbd, lbe, lbs, lbc, oml = (small[:, o:o + 4] for o in (16, 20, 24, 28, 32))
            wide = lambda v: v.unsqueeze(2).to_broadcast([P, A_H, T])
            nc.vector.tensor_tensor(lbd, cols("lb"), cols("lb"), ALU.subtract).then_inc(s_hv, 1)
            dve.wait_ge(s_ha, HA["lb_exp"])
            link(nc.vector.reciprocal(lbs, lbe))
            link(nc.vector.tensor_tensor(lbs, lbs, lbe, ALU.mult))
            link(nc.vector.tensor_tensor(lbc, lbs, lbs, ALU.subtract))
            link(nc.vector.tensor_scalar(oml, lbc, -1.0, 1.0, ALU.mult, ALU.add))
            link(nc.vector.tensor_scalar(kk[:, :, :], kk[:, :, :], 1.0, None, ALU.add),
                 nc.vector.tensor_scalar(kq[:, :, :], kq[:, :, :], 1.0, None, ALU.add))
            link(nc.vector.reciprocal(kk[:, :, :], kk[:, :, :]), nc.vector.reciprocal(kq[:, :, :], kq[:, :, :]))
            link(nc.vector.tensor_tensor(kk[:, :, :], kk[:, :, :], wide(oml), ALU.mult),
                 nc.vector.tensor_tensor(kq[:, :, :], kq[:, :, :], wide(oml), ALU.mult))
            link(nc.vector.tensor_tensor(kq[:, :, :], kq[:, :, :], wide(lbc), ALU.add))
            nc.vector.tensor_scalar(f4, kq[:, :, :], LN_SPLIT, None, ALU.max)
            nc.vector.tensor_scalar(kq[:, :, :], kq[:, :, :], TINY, LN_SPLIT, ALU.max, ALU.min).then_inc(s_hv, 1)
            dve.wait_ge(s_ha, HA["ln"])
            nc.vector.tensor_tensor(f4, f4, kq[:, :, :], ALU.add).then_inc(s_hv, 1)
            dve.wait_ge(s_hv, HV["w_free_q"])
            dve.wait_ge(s_hp, HP["vT"])
            for h in range(A_H):
                for t in range(2):
                    m = nc.vector.tensor_tensor_scan(i4[:, h, qt(t)], ones[:, :], f4[:, h, qt(t)], 0.0, ALU.mult, ALU.add)
            link(m)
            for h in range(A_H):
                for t in range(4):
                    r = slice(64 * t, 64 * t + 64)
                    m = nc.vector.tensor_tensor_scan(f4[:, h, r], ones[:, 0:64], f4[:, h, r], 0.0, ALU.mult, ALU.add)
            link(m)
            for name, v in (("q", q4), ("g", g4)):
                dve.wait_ge(s_ha, HA["exp_n" + name])
                link(nc.vector.tensor_scalar(kq[:, :, :], kq[:, :, :], 1.0, None, ALU.add))
                link(nc.vector.reciprocal(kq[:, :, :], kq[:, :, :]))
                nc.vector.tensor_tensor(v, v, kq[:, :, :], ALU.mult).then_inc(s_hv, 1)
            dve.wait_ge(s_hv, HV["silu_g"])
            dve.wait_ge(s_hm, 16)
            prev = 0
            for lv in LVL + [128]:
                b = i4 if lv == 128 else f4
                left = lambda v: v.rearrange("p h (n a m) -> p (h n) a m", a=2, m=lv)[:, :, 0, :]
                right = lambda v: v.rearrange("p h (n a m) -> p (h n) a m", a=2, m=lv)[:, :, 1, :]
                n = A_H * T // (2 * lv)
                end = left(b)[:, :, lv - 1:lv].to_broadcast([P, n, lv])
                dve.wait_ge(s_hp, HP[f"lvl{prev}"])
                if lv < 64:
                    nc.vector.tensor_tensor(right(kq[:, :, :]), right(b), end, ALU.subtract)
                else:
                    nc.vector.tensor_copy(right(kq[:, :, :]), right(b))
                nc.vector.tensor_tensor(left(kq[:, :, :]), end, left(b), ALU.subtract).then_inc(s_hv, 1)
                mask = hmask[:, 0 if prev == 0 else 1 + LVL.index(prev), :].unsqueeze(1).to_broadcast([P, A_H, P])
                for t in range(2):
                    ps = PS[4 + t][:, :].rearrange("p (h s) -> p h s", h=A_H)
                    dst = atd[:, t, :]
                    if prev == 0:
                        link(nc.vector.tensor_tensor(dst.rearrange("p (h s) -> p h s", h=A_H), ps, mask, ALU.mult))
                    else:
                        link(nc.vector.tensor_tensor(htmp[:, :].rearrange("p (h s) -> p h s", h=A_H), ps, mask, ALU.mult))
                        link(nc.vector.tensor_tensor(dst, dst, htmp[:, :], ALU.add))
                dve.wait_ge(s_ha, HA[f"exp{lv}"])
                nc.vector.tensor_tensor(left(kq[:, :, :]), left(kq[:, :, :]), left(kk[:, :, :]), ALU.mult)
                nc.vector.tensor_tensor(right(kq[:, :, :]), right(kq[:, :, :]), right(q4), ALU.mult).then_inc(s_hv, 1)
                prev = lv
            dve.wait_ge(s_hp, HP["var"])
            kkf = kk[:, :, :].rearrange("p h t -> p (h t)")
            link(*[nc.vector.tensor_scalar(kkf[:, 512 * g:512 * (g + 1)], PS[4 + g][:, :], 1.0 / HD, EPS, ALU.mult, ALU.add)
                   for g in range(2)])
            nc.vector.reciprocal(kkf, kkf).then_inc(s_hv, 1)
            dve.wait_ge(s_ha, HA["rstd"])
            mixf = mix[:, 0:4, :].rearrange("p h t -> p (h t)")
            link(*[nc.vector.scalar_tensor_tensor(mixf[:, 512 * g:512 * (g + 1)], PS[6 + g][:, :], cols("onorm"),
                                                  kkf[:, 512 * g:512 * (g + 1)], ALU.mult, ALU.mult) for g in range(2)])
            nc.vector.tensor_tensor(mix[:, 0:4, :], mix[:, 0:4, :], g4, ALU.mult).then_inc(s_hv, 1)

            fulls(U_B, lambda j: take(sec[:, S0 + j, :]), 1)
            link(nc.vector.tensor_scalar(gsc[:, 0:1], cols("fq"), HD ** -0.5, None, ALU.mult),
                 nc.vector.tensor_scalar(gsc[:, 1:2], cols("mq"), HD ** -0.5, None, ALU.mult))
            dve.wait_ge(s_evac, FIRST["C"][1])
            link(head_norms(HN_FOX, S0, gsc[:, 0:1], cols("fk")))
            z = sec[0:B_H, S0 + 18, :]
            nc.vector.tensor_scalar(z, z, cols("bf")[0:B_H, :], None, ALU.add).then_inc(s_fv, 1)
            dve.wait_ge(s_fa, 2)
            link(nc.vector.tensor_scalar(z, z, 0.0, None, ALU.min))
            nc.vector.tensor_scalar(gtmp[:, :], gtmp[:, :], 1.0, None, ALU.add).then_inc(s_fv, 1)
            dve.wait_ge(s_fa, 3)
            link(nc.vector.tensor_tensor(z, z, gtmp[:, :], ALU.subtract))
            link(nc.vector.tensor_tensor_scan(fnp[:, 0, qt(0)], ones[0:B_H, :], z[:, qt(0)], 0.0, ALU.mult, ALU.add))
            link(nc.vector.tensor_tensor_scan(fnp[:, 0, qt(1)], ones[0:B_H, :], z[:, qt(1)], fnp[:, 0, P - 1:P],
                                              ALU.mult, ALU.add))
            nc.vector.tensor_scalar(fnp[:, 1, :], fnp[:, 0, :], -1.0, None, ALU.mult).then_inc(s_qk, 1)
            jobs(J_FOX, fox_job, 2 * B_H)
            fulls(U_C, lambda j: take(sec[:, S1 + j, :]), 1)
            head_norms(HN_MOBA, S1, gsc[:, 1:2], cols("mk")).then_inc(s_qk, 1)
            jobs(J_MOBA, moba_job, 2 * C_H)
            for k in range(KB):
                lo(XS["mix"], k, mix[:, k, :])
            fulls(U_OUT, lambda j: add_blocks([j]), 1)
            norm(N_FFN, cols("ffn"))

            def conv(j):
                if c.n["g"] >= CH:
                    dve.wait_ge(s_conv, c.val("g", c.n["g"] - CH + 1))
                take(hg[:, j, 2:T + 2])
                w = lambda i: cvp[:, 4 * j + i:4 * j + i + 1]
                dve.wait_ge(s_evac, c.val("b", c.n["b"]))
                if c.n["g"] >= CH:
                    dve.wait_ge(s_gel, c.val("g", c.n["g"] - CH + 1))
                link(nc.vector.tensor_scalar(cv[:, j, :], hg[:, j, 2:T + 2], w(2), w(3), ALU.mult, ALU.add))
                link(nc.vector.scalar_tensor_tensor(cv[:, j, :], hg[:, j, 1:T + 1], w(1), cv[:, j, :], ALU.mult, ALU.add))
                nc.vector.scalar_tensor_tensor(cv[:, j, :], hg[:, j, 0:T], w(0), cv[:, j, :], ALU.mult, ALU.add).then_inc(s_conv, 1)
                c.n["g"] += 1

            def product(j):
                y = c.n["y"]
                if y >= 2:
                    dve.wait_ge(s_hy, c.val("y", y - 1))
                take(up[:, j % 2, :])
                dve.wait_ge(s_evac, c.val("b", c.n["b"]))
                dve.wait_ge(s_gel, c.val("y", y + 1))
                if y >= 2:
                    dve.wait_ge(s_h, c.val("y", y - 1))
                nc.vector.tensor_tensor(yf[:, y % 2, :], up[:, j % 2, :], gel[:, j, :], ALU.mult).then_inc(s_hy, 1)
                c.n["y"] += 1

            def h_lo(buf, j):
                l = c.n["l"]
                dve.wait_ge(s_hh, c.val("l", l + 1))
                nc.vector.tensor_tensor(hs[:, buf, j, 1, :], yf[:, l % 2, :], hs[:, buf, j, 0, :].bitcast(F32),
                                        ALU.subtract).then_inc(s_h, 1)
                c.n["l"] += 1

            def units(n, ev, first=None, lo_first=None, h_lo_of=None, nmod=0, m0=None):
                for j in range(n):
                    half((lambda: ev(j - 1)) if j else first,
                         after=(lambda: h_lo_of(j - 1)) if j and h_lo_of else (lo_first if j == 0 else None))
                    half(after=(lambda: mods(nmod, m0 + j * nmod)) if nmod else None)

            def downs(first, lo_first=None, gate=None, nmod=0, m0=None):
                for j in range(4):
                    half((lambda: add_blocks([4 * j - 2, 4 * j - 1], gate)) if j else first,
                         after=lo_first if j == 0 else None)
                    half(lambda: add_blocks([4 * j, 4 * j + 1], gate),
                         after=(lambda: mods(nmod, m0 + j * nmod)) if nmod else None)

            def last_down(gate=None):
                return lambda: add_blocks([14, 15], gate)

            def load_taps(n, dyn=False):
                o = COLS["conv"][0] + 16 * n
                src = par[:, bass.ds(c.i * 16 + o, 16)] if dyn else par[:, o:o + 16]
                link(nc.vector.tensor_copy(cvp[:, :], src))

            link(nc.vector.memset(hg[:, :, 0:2], 0.0))
            load_taps(0)
            units(CH, conv)
            units(CH, product, first=lambda: conv(CH - 1), h_lo_of=lambda j: h_lo(0, j))

            def ffn1_body():
                units(CH, conv, first=lambda: product(CH - 1), lo_first=lambda: (h_lo(0, CH - 1), load_taps(1, True)),
                      nmod=1, m0=0)
                downs(lambda: conv(CH - 1), nmod=1, m0=CH)
                units(CH, product, first=last_down(), h_lo_of=lambda j: h_lo(0, j), nmod=MODS_UP, m0=2 * CH)
                link(nc.vector.tensor_copy(modp[:, bass.ds(c.i * MODS1 + M0, MODS1)], modt[:, 0:MODS1]))
            M0 = c.n["m"]
            MODS_UP, MODS1 = 0, 8
            c.loop(NC1 - 1, ffn1_body, h=24, b=24, c=2 * 8 + 2 * CH + 2, m=MODS1, g=CH, y=CH, l=CH)
            downs(lambda: product(CH - 1), lo_first=lambda: h_lo(0, CH - 1))
            tail(last_down())

            for k in range(2):
                lo(XS["p"], k, mix[:, k, :])
            for u in range(U_PLEP):
                for hf in range(2):
                    o = 8 * u + 4 * hf
                    half((lambda: [take(mix[:, o - 4 + q, :]) for q in range(4)]) if o else None)
            tail(lambda: [take(mix[:, 12 + q, :]) for q in range(4)])
            norm(N_PLE, cols("ple"))

            def ple_in(j):
                take(yf[:, j % 2, :])

            def ple_add(j):
                dve.wait_ge(s_ps, j + 1)
                link(nc.vector.tensor_tensor(up[:, 1, :], yf[:, j % 2, :], mix[:, j, :], ALU.mult))
                nc.vector.tensor_tensor(x[:, j, :], x[:, j, :], up[:, 1, :], ALU.add).then_inc(s_pled, 1)

            rest = NMOD - c.n["m"]
            for j in range(U_PLEG):
                half((lambda: ple_in(j - 1)) if j else None, after=lambda: mods(rest * (j + 1) // U_PLEG - rest * j // U_PLEG))
                half(after=(lambda: ple_add(j - 1)) if j else None)
            tail(lambda: ple_in(U_PLEG - 1))
            ple_add(U_PLEG - 1)
            parts = modp[:, :].rearrange("p (n a) -> p n a", a=2)
            link(nc.vector.tensor_tensor(mod[:, :], parts[:, :, 0], parts[:, :, 1], ALU.add))
            link(nc.vector.tensor_tensor(mod[:, :], mod[:, :], cols("bmod"), ALU.add))
            SH1, SC1, G1, SH2, SC2, G2 = (mod[:, KB * i:KB * (i + 1)] for i in range(6))
            link(nc.vector.tensor_scalar(gmod[:, 0:KB], SC1, 1.0, None, ALU.add),
                 nc.vector.tensor_scalar(gmod[:, KB:2 * KB], SC2, 1.0, None, ALU.add))
            link(nc.vector.tensor_tensor(gmod[:, 0:KB], gmod[:, 0:KB], cols("attn2"), ALU.mult))
            m = nc.vector.tensor_tensor(gmod[:, KB:2 * KB], gmod[:, KB:2 * KB], cols("mlp2"), ALU.mult)
            m.then_inc(s_mod, 1)
            dve.wait_ge(s_mod, 1)
            norm(N_ATTN2, gmod[:, 0:KB], SH1)

            fulls(U_IN2, lambda j: take(sec[:, j, :]))
            dve.wait_ge(s_rl, 32)
            nc.vector.tensor_copy(relh[:, :, :], relb[:, :].unsqueeze(2).to_broadcast([REL + 1, SWA_H, P])).then_inc(s_rh, 1)
            dve.wait_ge(s_rb, 16 * SWA_H)
            jobs(J_SWA, swa_job, 2 * SWA_H)
            for j in range(2):
                dve.wait_ge(s_hss, HN_MLA + j + 1)
                inv_var(hvr[:, j, 0:T], PS[4 + j][:, 0:T], (MLA_QR, MLA_KVR)[j]).then_inc(s_hvar, 1)
            dve.wait_ge(s_hr, HN_MLA + 1)
            for k in range(4):
                g = cols("kvn") if k == 3 else cols("qn")[:, k:k + 1]
                b = sec[:, CQ + k, :]
                m = nc.vector.scalar_tensor_tensor(b, b, g, hvr[:, k // 3, 0:T], ALU.mult, ALU.mult)
            m.then_inc(s_qk, 1)
            dve.wait_ge(s_qk, 3)
            for k in range(4):
                lo(XS["cq"], k, sec[:, CQ + k, :])
            n, groups = 0, []
            dst = [QN + q for q in range(12)] + [KN + q for q in range(MLA_H)] + [MLA_V0 + q for q in range(MLA_H)]
            for size in [2] * (2 * U_UQ) + [4] * (2 * U_UKV):
                groups.append(dst[n:n + size])
                n += size
            for n in range(len(groups)):
                half((lambda: [take(sec[:, b, :]) for b in groups[n - 1]]) if n else None)
            tail(lambda: [take(sec[:, b, :]) for b in groups[-1]])
            dve.wait_ge(s_cs, 32)
            dve.wait_ge(s_evac, FIRST["out2"][1])
            for j, b in enumerate(ROPE):
                dve.wait_ge(s_pm, j + 1)
                if j:
                    dve.wait_ge(s_kvr, j)
                m1 = nc.vector.tensor_tensor(rtmp[:, 0, :], PS[4 + j % 2][:, 0:T], cossin[:, 1, :], ALU.mult)
                link(m1, nc.vector.tensor_tensor(rtmp[:, 1, :], sec[:, b, :], cossin[:, 0, :], ALU.mult))
                nc.vector.tensor_tensor(sec[:, b, :], rtmp[:, 0, :], rtmp[:, 1, :], ALU.add).then_inc(s_kvr, 1)
            dve.wait_ge(s_kvr, len(ROPE))
            jobs(J_MLA, mla_job, 2 * MLA_H)
            for k in range(KB):
                lo(XS["mix2"], k, mix[:, k, :])
            fulls(U_OUT, lambda j: add_blocks([j], G1))
            norm(N_MLP2, gmod[:, KB:2 * KB], SH2)

            def relu2(j):
                y = c.n["y"]
                dve.wait_ge(s_hy, c.val("y", y - 1))
                take(up[:, j % 2, :])
                dve.wait_ge(s_evac, c.val("b", c.n["b"]))
                dve.wait_ge(s_h, c.val("y", y - 1))
                nc.vector.scalar_tensor_tensor(yf[:, y % 2, :], up[:, j % 2, :], 0.0, up[:, j % 2, :],
                                               ALU.max, ALU.mult).then_inc(s_hy, 1)
                c.n["y"] += 1

            units(CH, relu2, h_lo_of=lambda j: h_lo(0, j))
            units(CH, relu2, first=lambda: relu2(CH - 1), lo_first=lambda: h_lo(0, CH - 1), h_lo_of=lambda j: h_lo(1, j))

            def ffn2_body():
                for q in range(2):
                    downs(lambda: relu2(CH - 1), lo_first=lambda: h_lo(1 - q, CH - 1), gate=G2)
                    units(CH, relu2, first=last_down(G2), h_lo_of=lambda j: h_lo(q, j))
            c.loop(NC2 // 2 - 1, ffn2_body, h=32, b=40, c=2 * 2 * 8, y=2 * CH, l=2 * CH)
            downs(lambda: relu2(CH - 1), lo_first=lambda: h_lo(1, CH - 1), gate=G2)
            downs(last_down(G2), gate=G2)
            tail(last_down(G2))
            norm(N_FINAL, cols("final"))


_OUT = "out_0_dram"


def kernel(**inputs):
    import concourse.bacc as bacc
    from concourse.bass_utils import run_bass_kernel_spmd as run

    i = {k: np.asarray(v) for k, v in inputs.items()}
    f32 = np.float32

    def feature_major(m):
        return np.ascontiguousarray(m.T.reshape(-1, P, m.shape[0]).transpose(1, 0, 2))

    def tiles(m):
        k, n = m.shape
        return m.reshape(k // P, P, n // P, P).transpose(2, 1, 0, 3)

    w = np.zeros((UNITS, P, 2, 8, P), f32)
    at = [0]

    def put(t, per_half):
        b, _, k, _ = t.shape
        if per_half == 0:
            w[at[0]:at[0] + b] = t.reshape(b, P, 2, 8, P)
            at[0] += b
        else:
            t = t.reshape(b // (2 * per_half), 2, per_half, P, k, P).transpose(0, 3, 1, 2, 4, 5)
            n = t.shape[0]
            w[at[0]:at[0] + n, :, :, 0:per_half * k] = t.reshape(n, P, 2, per_half * k, P)
            at[0] += n

    w_in = i["w_in"][0]
    a_w, b_w, c_w = A_H * HD, B_H * HD, C_H * HD
    o = 4 * a_w + 3 * b_w
    put(tiles(w_in[:, 0:o]), 0)
    put(tiles(w_in[:, o:o + P]), 0)
    put(tiles(w_in[:, o + B_H:o + B_H + 3 * c_w]), 0)
    put(tiles(i["w_out"][0]), 0)
    gate, up, down = (i[k][0] for k in ("w_gate", "w_up", "w_down"))
    n = CH * P
    for c in range(NC1 + 1):
        if c < NC1:
            put(tiles(gate[:, c * n:(c + 1) * n]), 0)
        if c:
            put(tiles(down[(c - 1) * n:c * n, :]), 2)
        if c < NC1:
            put(tiles(up[:, c * n:(c + 1) * n]), 0)
    put(tiles(i["w_ple_proj"][0]), 4)
    put(tiles(i["w_ple_gate"][0]), 0)
    w2 = i["w_in_2"][0]
    q, kv = SWA_H * SWA_D, SWA_D
    kr = q + 2 * SWA_KV * kv + MLA_QR + MLA_KVR
    put(tiles(np.concatenate([w2[:, 0:q]] + [w2[:, q + g * kv:q + (g + 1) * kv] for g in (0, 0, 1, 1)]
                             + [w2[:, q + SWA_KV * kv:kr], w2[:, kr:], w2[:, kr:]], axis=1)), 0)
    uq = i["w_uq_2"][0].reshape(MLA_QR, MLA_H, MLA_N + MLA_R)
    put(tiles(np.concatenate([uq[:, :, :MLA_N].reshape(MLA_QR, -1), uq[:, :, MLA_N:].reshape(MLA_QR, -1)], axis=1)), 2)
    ukv = i["w_ukv_2"][0].reshape(MLA_KVR, MLA_H, MLA_N + HD)
    put(tiles(np.concatenate([ukv[:, :, :MLA_N].reshape(MLA_KVR, -1), ukv[:, :, MLA_N:].reshape(MLA_KVR, -1)], axis=1)), 4)
    put(tiles(i["w_out_2"][0]), 0)
    ff1, ff2 = i["w_ff1_2"][0], i["w_ff2_2"][0]
    for c in range(NC2 + 2):
        if c >= 2:
            put(tiles(ff2[(c - 2) * n:(c - 1) * n, :]), 2)
        if c < NC2:
            put(tiles(ff1[:, c * n:(c + 1) * n]), 0)
    assert at[0] == UNITS

    par = np.zeros((P, NPAR), f32)

    def param(name, v):
        o, k = COLS[name]
        par[:, o:o + k] = v.reshape(k, P).T
    for name, key in (("attn", "attn_norm"), ("ffn", "ffn_norm"), ("ple", "ple_norm"), ("attn2", "attn_norm_g_2"),
                      ("mlp2", "mlp_norm_g_2"), ("final", "final_norm_g_2"), ("fq", "fox_qnorm"), ("fk", "fox_knorm"),
                      ("mq", "moba_qnorm"), ("mk", "moba_knorm"), ("onorm", "hgrn_onorm"), ("lb", "lb_logits"),
                      ("qn", "mla_q_norm_g_2"), ("kvn", "mla_kv_norm_g_2"), ("bmod", "b_mod_2")):
        param(name, i[key])
    par[0:B_H, COLS["bf"][0]] = i["fox_bf"][0]
    par[:, COLS["sink"][0]:COLS["sink"][0] + SWA_H] = i["swa_sinks_2"]
    taps = np.concatenate([i["conv_w"][0], i["conv_b"]], axis=0).reshape(4, NC1 * CH, P)
    par[:, COLS["conv"][0]:] = taps.transpose(2, 1, 0).reshape(P, -1)

    p_, j_ = np.arange(P)[:, None], np.arange(T)[None, :]
    seen = j_ <= P + p_
    dist = np.where(seen, -(P + p_ - j_), -1e33).astype(f32)
    causal = np.where(seen, 0.0, NEG).astype(f32)
    s_, t_ = np.arange(P)[:, None], np.arange(P)[None, :]
    hmask = np.stack([s_ == t_] + [(s_ // (2 * m) == t_ // (2 * m)) & (s_ // m % 2 == 0) & (t_ // m % 2 == 1)
                                   for m in LVL], axis=1).astype(f32)
    d = 2 * P - 1 - np.arange(3 * P)
    ok = (d >= 0) & (d < P)
    nf = np.maximum(d, 1).astype(f32)
    far = REL // 2 + (np.log(nf / f32(REL // 2)) / f32(np.log(P / (REL // 2))) * f32(REL // 2)).astype(np.int32)
    bucket = np.where(ok, np.where(d < REL // 2, d, np.minimum(far, REL - 1)), REL)
    oneh = (np.arange(REL + 1)[:, None] == bucket[None, :]).astype(f32)
    rel = np.concatenate([i["rel_bias_2"], np.full((1, SWA_H), NEG, f32)], axis=0)
    half = MLA_R // 2
    freq = f32(10000.0) ** (-np.arange(half, dtype=f32) / f32(half))
    ang = (np.arange(T, dtype=f32)[None, :] * freq[:, None])[np.arange(P) % half]
    sign = np.where(np.arange(P) % MLA_R < half, -1.0, 1.0).astype(f32)[:, None]
    cossin = np.stack([np.cos(ang), sign * np.sin(ang)], axis=1).astype(f32)
    swap = np.where(np.arange(P) % MLA_R < half, np.arange(P) + half, np.arange(P) - half)
    perm = (np.arange(P)[:, None] == swap[None, :]).astype(f32)

    arrays = {
        "w": w.reshape(UNITS, P, 2048),
        "wmod": np.ascontiguousarray(i["w_mod_2"][0].T).reshape(6 * KB, P, 2, 1024).transpose(0, 2, 1, 3).reshape(NMOD, P, 1024),
        "x": feature_major(i["x"][0]), "p": feature_major(i["p"][0, 0]),
        "c": np.ascontiguousarray(np.broadcast_to(i["c_2"], (P, DM))),
        "par": par, "ident": np.eye(P, dtype=f32), "dist": dist, "causal": causal, "hmask": hmask,
        "rel": rel, "oneh": oneh, "cossin": cossin, "perm": perm,
    }
    nc = bacc.Bacc("TRN2", target_bir_lowering=False, num_devices=1)
    aps = {}
    for name, v in arrays.items():
        arrays[name] = v = np.ascontiguousarray(v)
        aps[name] = nc.dram_tensor(f"in_{name}", v.shape, mybir.dt.from_np(v.dtype), kind="ExternalInput").ap()
    aps["out"] = nc.dram_tensor(_OUT, (P, KB, T), F32, kind="ExternalOutput").ap()
    build(nc, aps)
    r = run(nc, [{f"in_{k}": v for k, v in arrays.items()}], core_ids=[0])
    got = r.results[0][_OUT]
    return got.transpose(2, 1, 0).reshape(1, T, DM)
```

```python
from contextlib import ExitStack

import numpy as np
import concourse.bass as bass
from concourse import mybir

F32 = mybir.dt.float32
F32R = mybir.dt.float32r
ACT = mybir.ActivationFunctionType
ALU = mybir.AluOpType
AX = mybir.AxisListType

P = 128
T = 256
DM = 2048
KB = DM // P
EPS = 1e-6
TINY = 1e-30
NEG = -1e30
HD = 128
A_H, B_H, C_H = 4, 6, 6
D_FF = 5632
D_FF2 = 8192
SWA_H, SWA_D, SWA_KV = 16, 64, 2
MLA_H, MLA_N, MLA_R = 8, 128, 64
MLA_QR, MLA_KVR = 384, 128
REL = 32
LVL = [1, 2, 4, 8, 16, 32, 64]
LN_SPLIT = 2.0 ** -40
SLOPES = [float(np.float32(2.0) ** np.float32(-8.0 * (i + 1) / C_H)) for i in range(C_H)]

CH = 8
NC1 = D_FF // (CH * P)
CH_LAST = D_FF // P - CH * NC1
NC2 = D_FF2 // (CH * P)
U_A, U_B, U_C = 16, 19, 18
U_OUT = 8
U_FFN1 = 3 * D_FF // P
U_PLEP, U_PLEG = 2, 16
U_IN2 = 16
U_UQ, U_UKV = 3, 2
U_FFN2 = 2 * D_FF2 // P
UNITS = U_A + U_B + U_C + 2 * U_OUT + U_FFN1 + U_PLEP + U_PLEG + U_IN2 + U_UQ + U_UKV + 2 * U_OUT + U_FFN2
RAW = 4
HS = 4
LOOK = 3
NMOD = 2 * 6 * KB
MOD_SLOTS = 2

COLS = {}
_n = 0
for _name, _k in (("attn", 16), ("ffn", 16), ("ple", 16), ("attn2", 16), ("mlp2", 16), ("final", 16),
                  ("fq", 1), ("fk", 1), ("mq", 1), ("mk", 1), ("onorm", 1), ("lb", 4),
                  ("qn", 3), ("kvn", 1), ("bf", 1), ("sink", 16), ("bmod", 96), ("conv", 4 * (D_FF // P))):
    COLS[_name] = (_n, _k)
    _n += _k
NPAR = _n


def stages(*names):
    return {n: i + 1 for i, n in enumerate(names)}


class Counts:

    def __init__(self, eng, **start):
        self.eng, self.n, self.i, self.per = eng, dict(start), None, {}

    def val(self, name, value):
        step = self.per.get(name, 0)
        return value + self.i * step if step else value

    def loop(self, times, body, **per):
        before = dict(self.n)
        with self.eng.Fori(0, times) as i:
            self.i, self.per = i, per
            body()
        up = {k: self.n[k] - before[k] for k in self.n}
        assert all(up[k] == per.get(k, 0) for k in up), (up, per)
        self.i, self.per = None, {}
        for k in up:
            self.n[k] = before[k] + times * up[k]


HA = stages("exp_f", "exp_nf", "lb_exp", "vtok", "ln", "sig_q", "sig_g",
            *[f"exp{m}" for m in LVL + [128]], "at01", "sq", "rstd")
HV = stages("lb_d", "ln_in", "w_free_q", "w_free_g", "silu_g",
            *[x for m in LVL + [128] for x in (f"dec{m}", f"kq{m}")], "var", "done")
HP = stages("vT", "lvl0", *[f"lvl{m}" for m in LVL + [128]], "o", "var")


def build(nc, a):
    ctx = ExitStack()
    with ctx:
        base = [16512]

        def at(name, shape, off_kb, dt=F32):
            return nc.alloc_sbuf_tensor_at(name, shape, dt, offset=base[0] + int(off_kb * 1024))

        def sem(name):
            return ctx.enter_context(nc.semaphore(name))

        raw = at("raw", [P, RAW, 2048], 0)
        wh = at("wh", [P, HS, 1024], 32, F32R)
        wl = at("wl", [P, HS, 1024], 48, F32R)
        modraw = at("modraw", [P, MOD_SLOTS, 1024], 64)
        cb = at("cb", [P, 2048], 72)
        tbias = at("tbias", [P, SWA_H, T], 64)
        x = at("x", [P, KB, T], 80)
        xs = at("xs", [P, KB, 2, T], 96, F32R)
        mix = at("mix", [P, KB, T], 128)
        sec = at("sec", [P, 37, T], 144)
        S0, S1 = 0, 19
        ident = at("ident", [P, P], 181)
        ones = at("ones", [P, P], 181.5)
        dist = at("dist", [P, T], 182)
        causal = at("causal", [P, T], 183)
        par = at("par", [P, NPAR], 184)
        mod = at("mod", [P, 6 * KB], 185.75)
        modt = at("modt", [P, 3 * CH], 186.125)
        modp = at("modp", [P, NMOD], 186.25)
        gmod = at("gmod", [P, 2 * KB], 187)
        small = at("small", [P, 64], 187.125)
        gsc = at("gsc", [P, 2], 187.375)
        sil = at("sil", [P, 2048], 144)
        T0 = 187.5
        sq = at("sq", [P, 2, 4, T], T0)
        var = at("var", [P, T], T0 + 8)
        rstd = at("rstd", [P, T], T0 + 9)
        yn = at("yn", [P, 4, T], T0 + 10)
        kk = at("kk", [P, A_H, T], T0)
        kq = at("kq", [P, A_H, T], T0 + 4)
        atd = at("atd", [P, 2, 512], T0 + 8)
        at01 = at("at01", [P, 512], T0 + 12)
        vtok = at("vtok", [P, 2, 512], T0 + 14)
        hmask = at("hmask", [P, 8, P], 128 + 8)
        htmp = at("htmp", [P, 512], T0 + 18)
        logit = at("logit", [P, 3, T], T0)
        prob = at("prob", [P, 3, T], T0 + 3)
        probT = at("probT", [P, 3, T], T0 + 6)
        vt = at("vt", [P, 2, 8 * P], T0 + 9)
        gtmp = at("gtmp", [B_H, T], T0 + 17)
        fnp = at("fnp", [B_H, 2, T], T0 + 18)
        hsq = at("hsq", [P, 2, 512], T0)
        hvr = at("hvr", [P, 2, 512], T0 + 4)
        hsq4 = at("hsq4", [P, 4, T], T0)
        cossin = at("cossin", [P, 2, T], T0 + 17)
        perm = at("perm", [P, P], T0 + 19)
        rtmp = at("rtmp", [P, 2, T], T0 + 3)
        relb = at("relb", [REL + 1, SWA_H], T0)
        relh = at("relh", [REL + 1, SWA_H, P], T0 + 0.5)
        oneh = at("oneh", [REL + 1, 384], T0 + 8.5)
        rrow = at("rrow", [P, 4, 384], T0 + 10)
        up = at("up", [P, 2, T], 144)
        yf = at("yf", [P, 2, T], 146)
        hs = at("hs", [P, 2, CH, 2, T], 148, F32R)
        hg = at("hg", [P, 2, T + 2], 164)
        cv = at("cv", [P, 2, T], 166.25)
        gel = at("gel", [P, CH, T], 168.25)
        cvp = at("cvp", [P, 4 * CH], 176.25)

        PS = [ctx.enter_context(nc.psum_tensor(f"ps{i}", [P, 512], F32)) for i in range(8)]
        rel_dram = nc.dram_tensor("rel_rows", [4, P, 4, 384], F32, kind="Internal").ap()

        s_raw = [sem(f"raw_loaded{i}") for i in range(RAW)]
        s_round, s_split, s_used, s_evac = map(sem, ("hi_rounded", "lo_ready", "half_used", "block_taken"))
        s_modl = [sem(f"mod_loaded{i}") for i in range(MOD_SLOTS)]
        s_modu, s_mod = sem("mod_used"), sem("mod_ready")
        s_dch, s_ach = sem("dve_chain"), sem("act_chain")
        s_par, s_x, s_p, s_c, s_hm, s_cs, s_cact = map(sem, (
            "params_loaded", "x_loaded", "p_loaded", "c_loaded", "hmask_loaded", "cossin_loaded", "c_exp_ready"))
        s_ones = sem("ones_ready")
        s_sq, s_ssq, s_var, s_rstd, s_yn, s_yh, s_xs = map(sem, (
            "squares_ready", "square_sums", "inv_var_ready", "rstd_ready", "normed", "x_hi_ready", "x_pair_ready"))
        s_ha, s_hv, s_hp = map(sem, ("hgrn_act", "hgrn_dve", "hgrn_pe"))
        s_hsq, s_hss, s_hvar, s_hr, s_qk = map(sem, (
            "head_squares", "head_square_sums", "head_inv_var", "head_rstd", "qk_ready"))
        s_vT, s_vt, s_fa, s_fv = map(sem, ("v_transposed", "v_tokens", "gate_act", "gate_dve"))
        s_sc, s_lg, s_nm, s_ex, s_pr, s_tr, s_pt, s_pv, s_oe = map(sem, (
            "scores_ready", "scores_taken", "neg_max_ready", "exp_ready", "probs_ready",
            "probs_transposed", "probsT_copied", "pv_ready", "out_taken"))
        s_rl, s_rh, s_rp, s_rr, s_rw, s_rb = map(sem, (
            "rel_loaded", "rel_spread", "rel_rows_psum", "rel_rows_sbuf", "rel_rows_written", "bias_loaded"))
        s_pm, s_kvr = map(sem, ("rope_swapped", "rope_done"))
        s_conv, s_gel, s_hy, s_hh, s_h = map(sem, ("conv_ready", "gelu_ready", "h_ready", "h_hi_ready", "h_pair_ready"))
        s_ps, s_pled = map(sem, ("ple_sigmoid", "ple_added"))
        s_fin, s_out = map(sem, ("final_ready", "out_stored"))

        block = ctx.enter_context(nc.Block())
        cols = lambda name: par[:, COLS[name][0]:COLS[name][0] + COLS[name][1]]
        col = lambda name, k=0: par[:, COLS[name][0] + k:COLS[name][0] + k + 1]

        FIRST = {}
        u0 = b0 = 0
        for name, nu, nb in (("A", U_A, 16), ("B", U_B, 19), ("C", U_C, 18), ("out", U_OUT, 16), ("outb", U_OUT, 16),
                             ("ffn1", U_FFN1, 2 * (D_FF // P) + KB * (NC1 + 1)), ("plep", U_PLEP, 16), ("pleg", U_PLEG, 16),
                             ("in2", U_IN2, 16), ("uq", U_UQ, 12), ("ukv", U_UKV, 16),
                             ("out2", U_OUT, 16), ("out2b", U_OUT, 16), ("ffn2", U_FFN2, NC2 * (CH + KB))):
            FIRST[name] = (u0, b0)
            u0 += nu
            b0 += nb
        FIRST["end"] = (u0, b0)
        assert u0 == UNITS

        J_FOX, J_MOBA, J_SWA, J_MLA = 0, 2 * B_H, 2 * (B_H + C_H), 2 * (B_H + C_H + SWA_H)
        J_END = J_MLA + 2 * MLA_H
        N_ATTN, N_FFN, N_PLE, N_ATTN2, N_MLP2, N_FINAL = range(6)
        XS = {}
        n = 0
        for name, k in (("attn", 16), ("mix", 16), ("ffn", 16), ("p", 2), ("ple", 16), ("attn2", 16),
                        ("cq", 4), ("mix2", 16), ("mlp2", 16)):
            XS[name] = n
            n += k
        DONE = {"out": FIRST["ffn1"][1], "ffn1": FIRST["plep"][1], "out2": FIRST["ffn2"][1], "ffn2": FIRST["end"][1]}

        HN_FOX, HN_MOBA, HN_MLA = 0, 6, 12

        def gemm_blocks(kind, h):
            if kind == "full":
                return [(0, [(t, 8 * h + t) for t in range(8)], h == 0, h == 1)]
            if kind == "eight":
                return [(h, [(t, t) for t in range(8)], True, True)]
            if kind == "quad":
                return [(2 * h + b, [(4 * b + k, k) for k in range(4)], True, True) for b in range(2)]
            if kind == "uq":
                return [(2 * h + b, [(3 * b + k, k) for k in range(3)], True, True) for b in range(2)]
            if kind == "oct":
                return [(4 * h + b, [(2 * b + k, k) for k in range(2)], True, True) for b in range(4)]
            return [(4 * h + b, [(b, 0)], True, True) for b in range(4)]

        NBLK = {"full": 1, "eight": 2, "quad": 4, "uq": 4, "oct": 8, "one": 8}
        GAIN_XS = {N_ATTN: "attn", N_FFN: "ffn", N_PLE: "ple", N_ATTN2: "attn2", N_MLP2: "mlp2"}

        JOB_LAG = 3
        LEVELS = LVL + [128]
        LV0 = 10
        FOX_V, FOX_J = 7, 12
        MOBA_N = FOX_J + 2 * B_H + JOB_LAG + 1
        MOBA_J = 1
        assert MOBA_N + 7 <= 2 * U_C and MOBA_J + 2 * C_H + JOB_LAG <= 2 * U_OUT
        REL_C, REL_G, LAT, SWA_J = 4, (5, 8, 11, 14), 16, 20
        IN2_HALVES = 2 * (U_IN2 + U_UQ + U_UKV)
        MLA_J = 5

        def share(n, i, first, end):
            i, m = i - first, end - first
            return range(n * i // m, n * (i + 1) // m) if 0 <= i < m else ()

        def swa_steps(i):
            return share(2 * SWA_H + JOB_LAG, i, SWA_J, IN2_HALVES)

        def mla_steps(i):
            return share(2 * MLA_H + JOB_LAG, i, MLA_J, 2 * U_OUT)

        qt = lambda t: slice(t * P, (t + 1) * P)

        def fox_job(j):
            h, t = divmod(j, 2)
            nk = P * (t + 1)
            sel = ident[0:B_H, h:h + 1]
            return dict(nk=nk, h=h,
                        scores=[(sec[:, S0 + h, qt(t)], sec[:, S0 + B_H + h, 0:nk]),
                                (fnp[:, 0, qt(t)], sel.to_broadcast([B_H, nk])),
                                (sel.to_broadcast([B_H, P]), fnp[:, 1, 0:nk])],
                        bias=causal[:, T - nk:T], scale=1.0, slope=None, sink=None,
                        v=[vt[:, q, h * P:(h + 1) * P] for q in range(2)],
                        orow=(0, P), out=mix[:, A_H + h, qt(t)])

        def moba_job(j):
            h, t = divmod(j, 2)
            nk = P * (t + 1)
            return dict(nk=nk, h=h, scores=[(sec[:, S1 + h, qt(t)], sec[:, S1 + C_H + h, 0:nk])],
                        bias=dist[:, T - nk:T], scale=None, slope=SLOPES[h], sink=None,
                        v=[vt[:, q, h * P:(h + 1) * P] for q in range(2)],
                        orow=(0, P), out=mix[:, A_H + B_H + h, qt(t)])

        CQ, CKV, KR, SWA_K, SWA_V, SWA_Q = 0, 3, 4, 5, 7, 8
        QN, QR, KN = 16, 24, 28
        ROPE = [QR, QR + 1, QR + 2, QR + 3, KR]

        def swa_job(j):
            h, t = divmod(j, 2)
            nk = P * (t + 1)
            r = slice(SWA_D * (h % 2), SWA_D * (h % 2) + SWA_D)
            kv = h // (SWA_H // SWA_KV)
            return dict(nk=nk, h=h, scores=[(sec[r, SWA_Q + h // 2, qt(t)], sec[r, SWA_K + kv, 0:nk])],
                        bias=tbias[:, h, T - nk:T], scale=SWA_D ** -0.5, slope=None, sink=col("sink", h),
                        v=[vt[:, 0, q * P + kv * SWA_D:q * P + (kv + 1) * SWA_D] for q in range(2)],
                        orow=(SWA_D * (h % 2), SWA_D), out=mix[r, h // 2, qt(t)])

        def mla_job(j):
            h, t = divmod(j, 2)
            nk = P * (t + 1)
            r = slice(MLA_R * (h % 2), MLA_R * (h % 2) + MLA_R)
            return dict(nk=nk, h=h, scores=[(sec[:, QN + h, qt(t)], sec[:, KN + h, 0:nk]),
                                            (sec[r, QR + h // 2, qt(t)], sec[r, KR, 0:nk])],
                        bias=causal[:, T - nk:T], scale=(MLA_N + MLA_R) ** -0.5, slope=None, sink=None,
                        v=[vt[:, q, h * P:(h + 1) * P] for q in range(2)],
                        orow=(0, P), out=mix[:, 8 + h, qt(t)])

        @block.sync
        def _(sp):
            sp.dma_start(x[:, :, :], a["x"]).then_inc(s_x, 16)
            for dst, src in ((par[:, :], a["par"]), (ident[:, :], a["ident"]),
                             (dist[:, :], a["dist"]), (causal[:, :], a["causal"])):
                sp.dma_start(dst, src).then_inc(s_par, 16)
            for u in range(RAW):
                sp.dma_start(raw[:, u, :], a["w"][u, :, :]).then_inc(s_raw[u], 16)
            sp.dma_start(hmask[:, :, :], a["hmask"]).then_inc(s_hm, 16)
            rounds, rest = divmod(UNITS - RAW, RAW)
            with sp.Fori(0, rounds) as i:
                for r in range(RAW):
                    sp.wait_ge(s_split, i * (2 * RAW) + 2 * r + 2)
                    sp.dma_start(raw[:, r:r + 1, :],
                                 a["w"][bass.ds(i * RAW + (RAW + r), 1), :, :].rearrange("a p n -> p a n")
                                 ).then_inc(s_raw[r], 16)
            for r in range(rest):
                u = RAW * (rounds + 1) + r
                sp.wait_ge(s_split, 2 * (u - RAW) + 2)
                sp.dma_start(raw[:, r, :], a["w"][u, :, :]).then_inc(s_raw[r], 16)
            for q in range(4):
                sp.wait_ge(s_fin, 4 * q + 4)
                sp.dma_start(a["out"][:, 4 * q:4 * q + 4, :], mix[:, 4 * q:4 * q + 4, :]).then_inc(s_out, 16)
            sp.wait_ge(s_out, 64)

        @block.gpsimd
        def _(pool):
            pool.dma_start(cb[:, :], a["c"]).then_inc(s_c, 16)
            for n in range(MOD_SLOTS):
                pool.dma_start(modraw[:, n, :], a["wmod"][n, :, :]).then_inc(s_modl[n], 16)
            with pool.Fori(0, NMOD // MOD_SLOTS - 1) as i:
                for n in range(MOD_SLOTS):
                    pool.wait_ge(s_modu, i * MOD_SLOTS + n + 1)
                    pool.dma_start(modraw[:, n:n + 1, :],
                                   a["wmod"][bass.ds(i * MOD_SLOTS + (MOD_SLOTS + n), 1), :, :]
                                   .rearrange("a p n -> p a n")).then_inc(s_modl[n], 16)
            pool.wait_ge(s_xs, XS["attn2"] + 16)
            pool.wait_ge(s_mod, 1)
            pool.dma_start(relb[:, :], a["rel"]).then_inc(s_rl, 16)
            pool.dma_start(oneh[:, :], a["oneh"]).then_inc(s_rl, 16)
            for g in range(4):
                pool.wait_ge(s_rr, g + 1)
                pool.dma_start(rel_dram[g, :, :, :], rrow[:, :, :]).then_inc(s_rw, 16)
                pool.wait_ge(s_rw, 16 * (g + 1))
                for h in range(4):
                    src = bass.AP(tensor=rel_dram.tensor, offset=g * P * 1536 + h * 384 + P - 1,
                                  ap=[[1536 - 1, P], [1, T]])
                    pool.dma_start(tbias[:, 4 * g + h, :], src).then_inc(s_rb, 16)
            pool.dma_start(cossin[:, :, :], a["cossin"]).then_inc(s_cs, 16)
            pool.dma_start(perm[:, :], a["perm"]).then_inc(s_cs, 16)

        @block.tensor
        def _(pe):
            c = Counts(pe, h=0, b=0, hp=0)

            def unit(kind, src, xwait=None, between=None):
                for half in range(2):
                    if between:
                        between(half)
                    hh, b = c.n["h"], c.n["b"]
                    pe.wait_ge(s_split, c.val("h", hh + 1))
                    hi, lo = wh[:, hh % HS, :], wl[:, hh % HS, :]
                    for bi, tiles, first, last in gemm_blocks(kind, half):
                        if first and b + bi >= 4:
                            pe.wait_ge(s_evac, c.val("b", b + bi - 3))
                        out = PS[(b + bi) % 4]
                        for n, (t, k) in enumerate(tiles):
                            if xwait is not None and (half == 0 or kind == "full"):
                                pe.wait_ge(s_xs, xwait + k + 1)
                            w = slice(t * P, (t + 1) * P)
                            s, e = first and n == 0, last and n == len(tiles) - 1
                            pair = src[:, k, :, :].rearrange("p a t -> p (a t)")
                            if e and not s:
                                nc.tensor.matmul(out[:, 0:T], lo[:, w], src[:, k, 0, :], start=False, stop=False)
                                m = nc.tensor.matmul(out[:, :], hi[:, w], pair, start=False, stop=True)
                            else:
                                nc.tensor.matmul(out[:, :], hi[:, w], pair, start=s, stop=e)
                                m = nc.tensor.matmul(out[:, 0:T], lo[:, w], src[:, k, 0, :], start=False,
                                                     stop=e, skip_group_check=e)
                    m.then_inc(s_used, 1)
                    c.n["h"] += 1
                c.n["b"] += NBLK[kind]

            def fulls(n, name):
                unit("full", xs, XS[name])
                for j in range(1, n - (n - 1) // 4 * 4):
                    unit("full", xs)
                c.loop((n - 1) // 4, lambda: [unit("full", xs) for _ in range(4)], h=8, b=4)

            def norm(n):
                for k in range(KB):
                    if k % 4 == 0:
                        pe.wait_ge(s_sq, 4 * n + k // 4 + 1)
                    m = nc.tensor.matmul(PS[4][:, 0:T], ones[:, :], sq[:, (k // 4) % 2, k % 4, :],
                                         start=k == 0, stop=k == KB - 1)
                    if k % 4 == 3:
                        m.then_inc(s_ssq, 1)

            def head_sums(n, j):
                if 0 <= j < 6:
                    pe.wait_ge(s_hsq, n + j + 1)
                    if j >= 2:
                        pe.wait_ge(s_hvar, n + j - 1)
                    nc.tensor.matmul(PS[4 + j % 2][:, :], ones[:, :], hsq[:, j % 2, :],
                                     start=True, stop=True).then_inc(s_hss, 1)

            def v_transposes(n, v, g):
                if g >= 2:
                    pe.wait_ge(s_vt, n + g - 1)
                for q in range(2):
                    for t in range(2):
                        m = nc.tensor.transpose(PS[6 + g % 2][:, (2 * t + q) * P:(2 * t + q + 1) * P],
                                                v[:, 2 * g + q, qt(t)], ident[:, :])
                m.then_inc(s_vT, 1)

            def job_step(j0, make, n, j):
                if j < n:
                    d, J = make(j), j0 + j
                    if j >= 2:
                        pe.wait_ge(s_lg, J - 1)
                    for q, (l, r) in enumerate(d["scores"]):
                        m = nc.tensor.matmul(PS[4 + J % 2][:, 0:d["nk"]], l, r, start=q == 0,
                                             stop=q == len(d["scores"]) - 1)
                    m.then_inc(s_sc, 1)
                if 0 <= j - 3 < n:
                    d, J = make(j - 3), j0 + j - 3
                    pe.wait_ge(s_pt, J + 1)
                    if J:
                        pe.wait_ge(s_oe, J)
                    nt, (lo, w) = d["nk"] // P, d["orow"]
                    for t in range(nt):
                        m = nc.tensor.matmul(PS[7][lo:lo + w, 0:P], d["v"][t],
                                             probT[:, J % 3, qt(t)], start=t == 0, stop=t == nt - 1)
                    m.then_inc(s_pv, 1)
                if 0 <= j - 2 < n:
                    d, J = make(j - 2), j0 + j - 2
                    pe.wait_ge(s_pr, J + 1)
                    if J:
                        pe.wait_ge(s_pt, J)
                    for t in range(d["nk"] // P):
                        o = t * P
                        m = nc.tensor.transpose(PS[6][:, o:o + P], prob[:, J % 3, qt(t)], ident[:, :])
                    m.then_inc(s_tr, 1)

            pe.wait_ge(s_par, 64)
            pe.wait_ge(s_ones, 1)
            norm(N_ATTN)
            fulls(U_A, "attn")

            def level(lv):
                pe.wait_ge(s_hv, HV[f"kq{lv}"] if lv else HV["silu_g"])
                for t in range(2 if lv < 128 else 1):
                    for h in range(A_H):
                        ks = (kq if lv else kk)[:, h, qt(t)]
                        qs = (kq[:, h, qt(t if lv < 128 else 1)] if lv else sec[:, S1 + h, qt(t)])
                        m = nc.tensor.matmul(PS[4 + t][:, h * P:(h + 1) * P], ks, qs, start=True, stop=True)
                m.then_inc(s_hp, 1)

            def hgrn(i):
                k, r = divmod(i - LV0, 3)
                if i == 0:
                    pe.wait_ge(s_evac, FIRST["B"][1])
                    for t in range(2):
                        for h in range(A_H):
                            m = nc.tensor.transpose(PS[6 + t][:, h * P:(h + 1) * P], sec[:, S1 + 8 + h, qt(t)],
                                                    ident[:, :])
                    m.then_inc(s_hp, 1)
                if r == 0 and 0 <= k <= len(LEVELS):
                    level(([0] + LEVELS)[k])
                if i == LV0 + 3 * len(LEVELS) + 1:
                    pe.wait_ge(s_ha, HA["at01"])
                    for h in range(A_H):
                        o, q, hc = PS[6 + h // 2], (h % 2) * T, slice(h * P, (h + 1) * P)
                        nc.tensor.matmul(o[:, q:q + P], vtok[:, 0, hc], atd[:, 0, hc], start=True, stop=True)
                        nc.tensor.matmul(o[:, q + P:q + T], vtok[:, 0, hc], at01[:, hc], start=True, stop=False)
                        m = nc.tensor.matmul(o[:, q + P:q + T], vtok[:, 1, hc], atd[:, 1, hc], start=False, stop=True)
                    m.then_inc(s_hp, 1)
                if i == LV0 + 3 * len(LEVELS) + 2:
                    pe.wait_ge(s_ha, HA["sq"])
                    for g in range(2):
                        m = nc.tensor.matmul(PS[4 + g][:, :], ones[:, :],
                                             kq[:, 2 * g:2 * g + 2, :].rearrange("p a t -> p (a t)"), start=True, stop=True)
                    m.then_inc(s_hp, 1)

            for u in range(U_B):
                unit("full", xs, between=lambda q: hgrn(2 * u + q))

            def fox(i):
                head_sums(HN_FOX, i)
                if 0 <= i - FOX_V < B_H // 2:
                    pe.wait_ge(s_evac, FIRST["C"][1])
                    v_transposes(0, sec[:, S0 + 2 * B_H:S0 + 3 * B_H, :], i - FOX_V)
                if 0 <= i - FOX_J < 2 * B_H + JOB_LAG:
                    if i == FOX_J:
                        pe.wait_ge(s_qk, 1)
                    job_step(J_FOX, fox_job, 2 * B_H, i - FOX_J)
                head_sums(HN_MOBA, i - MOBA_N)

            for u in range(U_C):
                unit("full", xs, between=lambda q: fox(2 * u + q))

            def moba(i):
                if i == 0:
                    pe.wait_ge(s_evac, FIRST["out"][1])
                    pe.wait_ge(s_oe, J_MOBA)
                    for g in range(C_H // 2):
                        v_transposes(3, sec[:, S1 + 2 * C_H:S1 + 3 * C_H, :], g)
                    pe.wait_ge(s_qk, 2)
                if i >= MOBA_J:
                    job_step(J_MOBA, moba_job, 2 * C_H, i - MOBA_J)

            def eights(name, between):
                for u in range(U_OUT):
                    unit("eight", xs[:, 0:8, :, :], XS[name] if u == 0 else None, lambda q: between(2 * u + q))
                unit("eight", xs[:, 8:16, :, :], XS[name] + 8)
                for u in range(1, U_OUT):
                    unit("eight", xs[:, 8:16, :, :])

            eights("mix", moba)
            norm(N_FFN)

            def down(buf):
                c.n["hp"] += CH
                pe.wait_ge(s_h, c.val("hp", c.n["hp"]))
                for _ in range(KB // 2):
                    unit("eight", hs[:, buf, :, :, :])

            def ups(n=CH, name=None):
                for j in range(n):
                    unit("full", xs, XS[name] if name and j == 0 else None)

            ups(name="ffn")
            ups()
            c.loop(NC1 - 1, lambda: (ups(), down(0), ups()), h=6 * CH, b=2 * CH + KB, hp=CH)
            ups(CH_LAST)
            down(0)
            ups(CH_LAST)
            pe.wait_ge(s_h, CH * NC1 + CH_LAST)
            c.n["hp"] += CH_LAST
            for _ in range(KB // 4):
                unit("quad", hs[:, 0, 0:CH_LAST, :, :])

            for j in range(U_PLEP):
                unit("oct", xs, XS["p"] if j == 0 else None)
            norm(N_PLE)
            fulls(U_PLEG, "ple")
            norm(N_ATTN2)

            def swa(i):
                if i in REL_G:
                    g = REL_G.index(i)
                    if g:
                        pe.wait_ge(s_rr, g)
                    else:
                        pe.wait_ge(s_rh, 1)
                        pe.wait_ge(s_rl, 32)
                    for q in range(4):
                        m = nc.tensor.matmul(PS[4 + q][:, 0:384], relh[:, 4 * g + q, :], oneh[:, :], start=True, stop=True)
                    m.then_inc(s_rp, 1)
                if i == LAT:
                    pe.wait_ge(s_rr, 4)
                    pe.wait_ge(s_hsq, HN_MLA + 1)
                    for k in range(3):
                        m = nc.tensor.matmul(PS[4][:, 0:T], ones[:, :], hsq4[:, k, :], start=k == 0, stop=k == 2)
                    m.then_inc(s_hss, 1)
                    nc.tensor.matmul(PS[5][:, 0:T], ones[:, :], hsq4[:, 3, :], start=True, stop=True).then_inc(s_hss, 1)
                    pe.wait_ge(s_evac, FIRST["in2"][1] + SWA_V + 1)
                    for t in range(2):
                        m = nc.tensor.transpose(PS[7][:, qt(t)], sec[:, SWA_V, qt(t)], ident[:, :])
                    m.then_inc(s_vT, 1)
                for j in swa_steps(i):
                    if j == 0:
                        pe.wait_ge(s_vt, 7)
                        pe.wait_ge(s_hvar, HN_MLA + 2)
                    if j % 4 == 0 and j < 2 * SWA_H:
                        pe.wait_ge(s_evac, FIRST["in2"][1] + SWA_Q + j // 4 + 1)
                    job_step(J_SWA, swa_job, 2 * SWA_H, j)

            for u in range(U_IN2):
                unit("full", xs, XS["attn2"] if u == 0 else None, lambda q: swa(2 * u + q))
            for u in range(U_UQ):
                unit("uq", xs, XS["cq"] if u == 0 else None, lambda q: swa(2 * (U_IN2 + u) + q))
            pe.wait_ge(s_xs, XS["cq"] + 4)
            for u in range(U_UKV):
                unit("one", xs[:, 3:4, :, :], between=lambda q: swa(2 * (U_IN2 + U_UQ + u) + q))

            def mla(i):
                if i == 0:
                    pe.wait_ge(s_cs, 32)
                    pe.wait_ge(s_evac, FIRST["out2"][1])
                    pe.wait_ge(s_oe, J_MLA)
                if i < len(ROPE):
                    if i >= 2:
                        pe.wait_ge(s_kvr, i - 1)
                    nc.tensor.matmul(PS[4 + i % 2][:, 0:T], perm[:, :], sec[:, ROPE[i], :],
                                     start=True, stop=True).then_inc(s_pm, 1)
                if i < MLA_H // 2:
                    v_transposes(7, mix[:, 8:16, :], i)
                for j in mla_steps(i):
                    if j == 0:
                        pe.wait_ge(s_kvr, len(ROPE))
                    job_step(J_MLA, mla_job, 2 * MLA_H, j)

            eights("mix2", mla)
            norm(N_MLP2)

            ups(name="mlp2")
            ups()
            c.loop(NC2 // 2 - 1, lambda: (down(0), ups(), down(1), ups()), h=8 * CH, b=2 * (CH + KB), hp=2 * CH)
            down(0)
            down(1)
            assert c.n["h"] == 2 * UNITS and c.n["b"] == FIRST["end"][1]
            norm(N_FINAL)

        @block.scalar
        def _(act):
            c = Counts(act, h=0, g=0, y=0)

            def rnd(h):
                if h < 2 * UNITS:
                    u = h // 2
                    if h % 2 == 0:
                        v = 16 * (u // RAW + 1)
                        act.wait_ge(s_raw[u % RAW], v + c.i * (c.per["h"] * 16 // (2 * RAW)) if c.per else v)
                    if h >= HS:
                        act.wait_ge(s_used, c.val("h", h - HS + 1))
                    nc.scalar.activation(wh[:, h % HS, :], raw[:, u % RAW, (h % 2) * 1024:(h % 2 + 1) * 1024],
                                         ACT.Copy).then_inc(s_round, 1)

            def step(after=None, between=None):
                for q in range(2):
                    rnd(c.n["h"] + LOOK)
                    c.n["h"] += 1
                    if after and q == 0:
                        after()
                    if between:
                        between(q)

            def steps(n):
                for _ in range(n):
                    step()

            def norm(n, name=None):
                if n:
                    act.wait_ge(s_evac, DONE[name]) if name in DONE else act.wait_ge(s_pled, KB)
                for g in range(4):
                    if 4 * n + g >= 2:
                        act.wait_ge(s_ssq, 4 * n + g - 1)
                    nc.scalar.activation(sq[:, g % 2, :, :], x[:, 4 * g:4 * g + 4, :], ACT.Square).then_inc(s_sq, 1)
                act.wait_ge(s_var, n + 1)
                nc.scalar.activation(rstd[:, :], var[:, :], ACT.Sqrt).then_inc(s_rstd, 1)
                if n != N_FINAL:
                    for k in range(KB):
                        act.wait_ge(s_yn, KB * n + k + 1)
                        nc.scalar.activation(xs[:, k, 0, :], yn[:, k % 4, :], ACT.Copy).then_inc(s_yh, 1)

            def his(phase, srcs, k0=0):
                act.wait_ge(s_used, 2 * FIRST[phase][0])
                for k, s in enumerate(srcs):
                    nc.scalar.activation(xs[:, k0 + k, 0, :], s, ACT.Copy).then_inc(s_yh, 1)

            def head_norm(n, s0, j):
                if 0 < j <= 6:
                    act.wait_ge(s_hvar, n + j)
                    nc.scalar.activation(hvr[:, (j - 1) % 2, :], hvr[:, (j - 1) % 2, :], ACT.Sqrt).then_inc(s_hr, 1)
                if 0 <= j < 6:
                    if j >= 2:
                        act.wait_ge(s_hss, n + j - 1)
                    nc.scalar.activation(hsq[:, j % 2, :], sec[:, s0 + 2 * j:s0 + 2 * j + 2, :]
                                         .rearrange("p a t -> p (a t)"), ACT.Square).then_inc(s_hsq, 1)

            def v_copy(n, g):
                act.wait_ge(s_vT, n + g + 1)
                nc.scalar.activation(vt[:, :, 2 * g * P:(2 * g + 2) * P],
                                     PS[6 + g % 2][:, :].rearrange("p (t c) -> p t c", t=2), ACT.Copy).then_inc(s_vt, 1)

            def job_step(j0, make, n, j):
                if j < n:
                    d, J = make(j), j0 + j
                    act.wait_ge(s_nm, J + 1)
                    if j >= 3:
                        act.wait_ge(s_tr, J - 2)
                    q = J % 3
                    m = nc.scalar.activation(prob[:, q, 0:d["nk"]], logit[:, q, 0:d["nk"]], ACT.Exp,
                                             bias=small[:, 4 * q:4 * q + 1], accum_out=small[:, 4 * q + 1:4 * q + 2])
                    if d["sink"] is not None:
                        m = nc.scalar.activation(small[:, 4 * q + 2:4 * q + 3], d["sink"], ACT.Exp,
                                                 bias=small[:, 4 * q:4 * q + 1])
                    m.then_inc(s_ex, 1)
                if 0 <= j - 2 < n:
                    d, J = make(j - 2), j0 + j - 2
                    act.wait_ge(s_tr, J + 1)
                    if j - 2 >= 3:
                        act.wait_ge(s_pv, J - 2)
                    nc.scalar.activation(probT[:, J % 3, 0:d["nk"]], PS[6][:, 0:d["nk"]],
                                         ACT.Copy).then_inc(s_pt, 1)
                if 0 <= j - 3 < n:
                    d, J = make(j - 3), j0 + j - 3
                    act.wait_ge(s_pv, J + 1)
                    lo, w = d["orow"]
                    nc.scalar.activation(d["out"], PS[7][lo:lo + w, 0:P], ACT.Copy).then_inc(s_oe, 1)

            act.wait_ge(s_x, 16)
            norm(N_ATTN)
            for h in range(LOOK):
                rnd(h)
            act.wait_ge(s_c, 16)
            nc.scalar.activation(sil[:, :], cb[:, :], ACT.Exp, scale=-1.0).then_inc(s_cact, 1)
            steps(U_A)

            q4, f4, g4 = (sec[:, S1 + o:S1 + o + 4, :] for o in (0, 4, 12))

            def hgrn(i):
                k, r = divmod(i - LV0, 3)
                if i == 0:
                    act.wait_ge(s_evac, FIRST["B"][1])
                    nc.scalar.activation(kk[:, :, :], f4, ACT.Exp).then_inc(s_ha, 1)
                    nc.scalar.activation(kq[:, :, :], f4, ACT.Exp, scale=-1.0).then_inc(s_ha, 1)
                    act.wait_ge(s_hv, HV["lb_d"])
                    nc.scalar.activation(small[:, 20:24], small[:, 16:20], ACT.Exp).then_inc(s_ha, 1)
                if i == 2:
                    act.wait_ge(s_hp, HP["vT"])
                    for t in range(2):
                        m = nc.scalar.activation(vtok[:, t, :], PS[6 + t][:, :], ACT.Copy)
                    m.then_inc(s_ha, 1)
                if i == 4:
                    act.wait_ge(s_hv, HV["ln_in"])
                    nc.scalar.activation(f4, f4, ACT.Ln)
                    nc.scalar.activation(kq[:, :, :], kq[:, :, :], ACT.Ln, scale=1.0 / LN_SPLIT).then_inc(s_ha, 1)
                if i == 6:
                    act.wait_ge(s_hv, HV["w_free_q"])
                    nc.scalar.activation(kq[:, :, :], q4, ACT.Sigmoid).then_inc(s_ha, 1)
                if i == 8:
                    act.wait_ge(s_hv, HV["w_free_g"])
                    nc.scalar.activation(kq[:, :, :], g4, ACT.Sigmoid).then_inc(s_ha, 1)
                if r == 1 and 0 <= k < len(LEVELS):
                    act.wait_ge(s_hv, HV[f"dec{LEVELS[k]}"])
                    nc.scalar.activation(kq[:, :, :], kq[:, :, :], ACT.Exp).then_inc(s_ha, 1)
                if i == LV0 + 3 * len(LEVELS):
                    act.wait_ge(s_hp, HP["lvl128"])
                    nc.scalar.activation(at01[:, :], PS[4][:, :], ACT.Copy).then_inc(s_ha, 1)
                if i == LV0 + 3 * len(LEVELS) + 1:
                    act.wait_ge(s_hp, HP["o"])
                    for g in range(2):
                        m = nc.scalar.activation(kq[:, 2 * g:2 * g + 2, :].rearrange("p a t -> p (a t)"),
                                                 PS[6 + g][:, :], ACT.Square)
                    m.then_inc(s_ha, 1)
                if i == LV0 + 3 * len(LEVELS) + 3:
                    act.wait_ge(s_hv, HV["var"])
                    nc.scalar.activation(kk[:, :, :], kk[:, :, :], ACT.Sqrt).then_inc(s_ha, 1)

            for u in range(U_B):
                step(between=lambda q: hgrn(2 * u + q))

            def fox(i):
                if i == 0:
                    act.wait_ge(s_hv, HV["done"])
                    act.wait_ge(s_evac, FIRST["C"][1])
                head_norm(HN_FOX, S0, i)
                if 0 <= i - FOX_V < B_H // 2:
                    v_copy(0, i - FOX_V)
                if i == FOX_V + 1:
                    act.wait_ge(s_fv, 1)
                    nc.scalar.activation(gtmp[:, :], sec[0:B_H, S0 + 18, :], ACT.Abs).then_inc(s_fa, 1)
                    act.wait_ge(s_fa, 1)
                    nc.scalar.activation(gtmp[:, :], gtmp[:, :], ACT.Exp, scale=-1.0).then_inc(s_fa, 1)
                if i == FOX_V + 3:
                    act.wait_ge(s_fv, 2)
                    nc.scalar.activation(gtmp[:, :], gtmp[:, :], ACT.Ln).then_inc(s_fa, 1)
                if 0 <= i - FOX_J < 2 * B_H + JOB_LAG:
                    job_step(J_FOX, fox_job, 2 * B_H, i - FOX_J)
                if i == MOBA_N:
                    act.wait_ge(s_oe, J_MOBA)
                    act.wait_ge(s_evac, FIRST["C"][1] + 2 * C_H)
                head_norm(HN_MOBA, S1, i - MOBA_N)

            for u in range(U_C):
                step(between=lambda q: fox(2 * u + q))

            def moba(i):
                if i == 0:
                    for g in range(C_H // 2):
                        v_copy(3, g)
                if i >= MOBA_J:
                    job_step(J_MOBA, moba_job, 2 * C_H, i - MOBA_J)

            def eights(phase, first_done, jobs_done, between):
                act.wait_ge(s_oe, first_done)
                his(phase, [mix[:, k, :] for k in range(8)])
                for u in range(U_OUT):
                    step(between=lambda q: between(2 * u + q))
                act.wait_ge(s_oe, jobs_done)
                his(phase, [mix[:, k, :] for k in range(8, KB)], 8)
                c.loop(U_OUT // 4, lambda: steps(4), h=8)

            eights("out", J_MOBA, J_SWA, moba)
            act.wait_ge(s_xs, XS["mix"] + 16)
            act.dma_start(mix[:, 0:2, :], a["p"]).then_inc(s_p, 16)
            norm(N_FFN, "out")

            def gelu(j):
                c.n["g"] += 1
                act.wait_ge(s_conv, c.val("g", c.n["g"]))
                nc.scalar.activation(gel[:, j, :], cv[:, j % 2, :], ACT.Gelu_apprx_tanh).then_inc(s_gel, 1)

            def h_hi(buf, j):
                c.n["y"] += 1
                act.wait_ge(s_hy, c.val("y", c.n["y"]))
                nc.scalar.activation(hs[:, buf, j, 0, :], yf[:, (c.n["y"] - 1) % 2, :], ACT.Copy).then_inc(s_hh, 1)

            def gates(n=CH, first=None):
                for j in range(n):
                    step((lambda: gelu(j - 1)) if j else first)

            def ups(buf, n=CH, first=None):
                for j in range(n):
                    step((lambda: h_hi(buf, j - 1)) if j else first)

            def downs(first, n=KB // 2):
                step(first)
                steps(n - 1)

            gates()
            ups(0, first=lambda: gelu(CH - 1))
            c.loop(NC1 - 1, lambda: (gates(first=lambda: h_hi(0, CH - 1)), downs(lambda: gelu(CH - 1)), ups(0)),
                   h=6 * CH, g=CH, y=CH)
            gates(CH_LAST, lambda: h_hi(0, CH - 1))
            downs(lambda: gelu(CH_LAST - 1))
            ups(0, CH_LAST)
            downs(lambda: h_hi(0, CH_LAST - 1), KB // 4)

            act.wait_ge(s_p, 16)
            his("plep", [mix[:, k, :] for k in range(2)])
            steps(U_PLEP)
            act.wait_ge(s_used, 2 * FIRST["pleg"][0])
            norm(N_PLE, "ffn1")

            def sigmoid(j):
                act.wait_ge(s_evac, FIRST["pleg"][1] + j + 1)
                nc.scalar.activation(yf[:, j % 2, :], yf[:, j % 2, :], ACT.Sigmoid).then_inc(s_ps, 1)
            for j in range(U_PLEG):
                step((lambda: sigmoid(j - 1)) if j else None)
            sigmoid(U_PLEG - 1)
            norm(N_ATTN2)

            def swa(i):
                if i in REL_G:
                    g = REL_G.index(i)
                    act.wait_ge(s_rp, g + 1)
                    if g:
                        act.wait_ge(s_rw, 16 * g)
                    for q in range(4):
                        m = nc.scalar.activation(rrow[:, q, :], PS[4 + q][:, 0:384], ACT.Copy)
                    m.then_inc(s_rr, 1)
                if i == LAT:
                    act.wait_ge(s_evac, FIRST["in2"][1] + CKV + 1)
                    nc.scalar.activation(hsq4[:, :, :], sec[:, CQ:CQ + 4, :], ACT.Square).then_inc(s_hsq, 1)
                if i == LAT + 1:
                    act.wait_ge(s_rw, 64)
                    act.wait_ge(s_vT, 7)
                    nc.scalar.activation(vt[:, 0, 0:T], PS[7][:, 0:T], ACT.Copy).then_inc(s_vt, 1)
                if i == LAT + 2:
                    act.wait_ge(s_hvar, HN_MLA + 2)
                    nc.scalar.activation(hvr[:, :, 0:T], hvr[:, :, 0:T], ACT.Sqrt).then_inc(s_hr, 1)
                for j in swa_steps(i):
                    if j == 0:
                        act.wait_ge(s_qk, 3)
                    job_step(J_SWA, swa_job, 2 * SWA_H, j)

            for u in range(U_IN2):
                step(between=lambda q: swa(2 * u + q))
            his("uq", [sec[:, CQ + k, :] for k in range(4)])
            for u in range(U_IN2, U_IN2 + U_UQ + U_UKV):
                step(between=lambda q: swa(2 * u + q))

            def mla(i):
                if i < MLA_H // 2:
                    v_copy(7, i)
                for j in mla_steps(i):
                    job_step(J_MLA, mla_job, 2 * MLA_H, j)

            eights("out2", J_MLA, J_END, mla)
            norm(N_MLP2, "out2")

            ups(0)
            ups(1, first=lambda: h_hi(0, CH - 1))
            c.loop(NC2 // 2 - 1, lambda: (downs(lambda: h_hi(1, CH - 1)), ups(0), downs(lambda: h_hi(0, CH - 1)), ups(1)),
                   h=8 * CH, y=2 * CH)
            downs(lambda: h_hi(1, CH - 1))
            steps(KB // 2)
            norm(N_FINAL, "ffn2")

        @block.vector
        def _(dve):
            c = Counts(dve, h=0, b=0, c=0, m=0, g=0, y=0, l=0)

            def link(*ins):
                for i in ins:
                    i.then_inc(s_dch, 1)
                c.n["c"] += len(ins)
                dve.wait_ge(s_dch, c.val("c", c.n["c"]))

            def sub(h):
                if h < 2 * UNITS:
                    dve.wait_ge(s_round, c.val("h", h + 1))
                    nc.vector.tensor_tensor(wl[:, h % HS, :], raw[:, (h // 2) % RAW, (h % 2) * 1024:(h % 2 + 1) * 1024],
                                            wh[:, h % HS, :].bitcast(F32), ALU.subtract).then_inc(s_split, 1)

            def half(before=None, after=None):
                if before:
                    dve.wait_ge(s_used, c.val("h", c.n["h"]))
                    before()
                sub(c.n["h"] + LOOK)
                if after:
                    after()
                c.n["h"] += 1

            def tail(before):
                dve.wait_ge(s_used, c.val("h", c.n["h"]))
                before()

            def bank():
                c.n["b"] += 1
                return PS[(c.n["b"] - 1) % 4]

            def take(dst):
                nc.vector.tensor_reduce(dst, bank()[:, :].rearrange("p (a t) -> p t a", a=2), AX.X, ALU.add
                                        ).then_inc(s_evac, 1)

            def add_blocks(ks, gate=None):
                bs = [bank() for _ in ks]
                for q in range(2):
                    ins = []
                    for k, b in zip(ks, bs):
                        if gate is None:
                            ins.append(nc.vector.tensor_tensor(x[:, k, :], b[:, q * T:(q + 1) * T], x[:, k, :], ALU.add))
                        else:
                            ins.append(nc.vector.scalar_tensor_tensor(x[:, k, :], b[:, q * T:(q + 1) * T],
                                                                      gate[:, k:k + 1], x[:, k, :], ALU.mult, ALU.add))
                    if q == 0:
                        link(*ins)
                    else:
                        for i in ins:
                            i.then_inc(s_evac, 1)

            def mods(n, where=None):
                dst = modp if where is None else modt
                for j in range(n):
                    m = c.n["m"]
                    v = 16 * (m // 2 + 1)
                    dve.wait_ge(s_modl[m % 2], v + c.i * (8 * c.per["m"]) if c.per else v)
                    o = m if where is None else where + j
                    nc.vector.tensor_tensor_reduce(out=modraw[:, m % 2, :], in0=modraw[:, m % 2, :],
                                                   in1=cb[:, (m % 2) * 1024:(m % 2 + 1) * 1024],
                                                   scale=1.0, scalar=0.0, op0=ALU.mult, op1=ALU.add,
                                                   accum_out=dst[:, o:o + 1]).then_inc(s_modu, 1)
                    c.n["m"] += 1

            def fulls(n, ev, nmod=lambda j: 0, between=lambda i: None):
                for j in range(n):
                    half((lambda: ev(j - 1)) if j else None, after=lambda: between(2 * j))
                    half(after=lambda: (between(2 * j + 1), mods(nmod(j))))
                tail(lambda: ev(n - 1))

            def eights(name, jobs_done, between, gate=None, nmod=0):
                for part in range(2):
                    if part:
                        dve.wait_ge(s_oe, jobs_done)
                    for k in range(8 * part, 8 * part + 8):
                        lo(XS[name], k, mix[:, k, :])
                    for i in range(2 * U_OUT):
                        half((lambda: add_blocks([i - 1], gate)) if i else None,
                             after=lambda: (mods(nmod * (i % 2)) if part else between(i)))
                    tail(lambda: add_blocks([KB - 1], gate))

            def lo(x0, k, src):
                dve.wait_ge(s_yh, x0 + k + 1)
                nc.vector.tensor_tensor(xs[:, k, 1, :], src, xs[:, k, 0, :].bitcast(F32), ALU.subtract).then_inc(s_xs, 1)

            def inv_var(dst, src, n):
                link(nc.vector.tensor_scalar(dst, src, 1.0 / n, EPS, ALU.mult, ALU.add))
                return nc.vector.reciprocal(dst, dst)

            def norm(n, gain, shift=None):
                dve.wait_ge(s_ssq, 4 * n + 4)
                inv_var(var[:, :], PS[4][:, 0:T], DM).then_inc(s_var, 1)
                dve.wait_ge(s_rstd, n + 1)
                for k in range(KB + 2):
                    if k < KB and n == N_FINAL:
                        nc.vector.scalar_tensor_tensor(mix[:, k, :], x[:, k, :], gain[:, k:k + 1], rstd[:, :],
                                                       ALU.mult, ALU.mult).then_inc(s_fin, 1)
                    elif k < KB:
                        if k >= 4:
                            dve.wait_ge(s_xs, XS[GAIN_XS[n]] + k - 3)
                        y = nc.vector.scalar_tensor_tensor(yn[:, k % 4, :], x[:, k, :], gain[:, k:k + 1], rstd[:, :],
                                                           ALU.mult, ALU.mult)
                        if shift is not None:
                            link(y)
                            y = nc.vector.tensor_scalar(yn[:, k % 4, :], yn[:, k % 4, :], shift[:, k:k + 1], None, ALU.add)
                        y.then_inc(s_yn, 1)
                    if k >= 2 and n != N_FINAL:
                        lo(XS[GAIN_XS[n]], k - 2, yn[:, (k - 2) % 4, :])

            def head_norm(n, s0, gq, gk, j):
                if 0 <= j < 6:
                    dve.wait_ge(s_hss, n + j + 1)
                    inv_var(hvr[:, j % 2, :], PS[4 + j % 2][:, :], HD).then_inc(s_hvar, 1)
                if 0 < j <= 6:
                    q = j - 1
                    dve.wait_ge(s_hr, n + j)
                    b = sec[:, s0 + 2 * q:s0 + 2 * q + 2, :].rearrange("p a t -> p (a t)")
                    m = nc.vector.scalar_tensor_tensor(b, b, gq if q < 3 else gk, hvr[:, q % 2, :], ALU.mult, ALU.mult)
                    if (n, j) == (HN_MOBA, 6):
                        m.then_inc(s_qk, 1)
                    else:
                        link(m)

            def job_step(j0, make, n, j):
                if j < n:
                    d, J = make(j), j0 + j
                    q, nk = J % 3, d["nk"]
                    s = PS[4 + J % 2][:, 0:nk]
                    dve.wait_ge(s_sc, J + 1)
                    if j >= 3:
                        dve.wait_ge(s_ex, J - 2)
                    if d["slope"] is None:
                        m = nc.vector.scalar_tensor_tensor(logit[:, q, 0:nk], s, d["scale"], d["bias"], ALU.mult, ALU.add)
                    else:
                        m = nc.vector.scalar_tensor_tensor(logit[:, q, 0:nk], d["bias"], d["slope"], s, ALU.mult, ALU.add)
                    m.then_inc(s_lg, 1)
                    dve.wait_ge(s_lg, J + 1)
                    top = small[:, 4 * q + 3:4 * q + 4]
                    if J >= 3:
                        dve.wait_ge(s_nm, J - 2)
                    link(nc.vector.tensor_reduce(top, logit[:, q, 0:nk], AX.X, ALU.max))
                    if d["sink"] is None:
                        m = nc.vector.tensor_scalar(small[:, 4 * q:4 * q + 1], top, -1.0, None, ALU.mult)
                    else:
                        m = nc.vector.tensor_scalar(small[:, 4 * q:4 * q + 1], top, d["sink"], -1.0, ALU.max, ALU.mult)
                    m.then_inc(s_nm, 1)
                if 0 < j <= n:
                    d, J = make(j - 1), j0 + j - 1
                    q, nk = J % 3, d["nk"]
                    den = small[:, 4 * q + 1:4 * q + 2]
                    dve.wait_ge(s_ex, J + 1)
                    if d["sink"] is not None:
                        link(nc.vector.tensor_tensor(den, den, small[:, 4 * q + 2:4 * q + 3], ALU.add))
                    link(nc.vector.reciprocal(den, den))
                    nc.vector.tensor_scalar(prob[:, q, 0:nk], prob[:, q, 0:nk], den, None, ALU.mult).then_inc(s_pr, 1)

            nc.vector.memset(ones[:, :], 1.0).then_inc(s_ones, 1)
            dve.wait_ge(s_ones, 1)
            dve.wait_ge(s_par, 64)
            dve.wait_ge(s_x, 16)
            norm(N_ATTN, cols("attn"))
            for h in range(LOOK):
                sub(h)
            dve.wait_ge(s_cact, 1)
            link(nc.vector.tensor_scalar(sil[:, :], sil[:, :], 1.0, None, ALU.add))
            link(nc.vector.reciprocal(sil[:, :], sil[:, :]))
            link(nc.vector.tensor_tensor(cb[:, :], cb[:, :], sil[:, :], ALU.mult))
            fulls(U_A, lambda j: take(sec[:, S1 + j, :]), lambda j: 1 + j % 2)

            q4, f4, i4, g4 = (sec[:, S1 + o:S1 + o + 4, :] for o in (0, 4, 8, 12))
            lbd, lbe, lbs, lbc, oml = (small[:, o:o + 4] for o in (16, 20, 24, 28, 32))
            wide = lambda v: v.unsqueeze(2).to_broadcast([P, A_H, T])

            def decays(k):
                lv, prev = LEVELS[k], ([0] + LEVELS)[k]
                b = i4 if lv == 128 else f4
                n = A_H * T // (2 * lv)
                end = left(b, lv)[:, :, lv - 1:lv].to_broadcast([P, n, lv])
                dve.wait_ge(s_hp, HP[f"lvl{prev}"])
                if lv < 64:
                    nc.vector.tensor_tensor(right(kq[:, :, :], lv), right(b, lv), end, ALU.subtract)
                else:
                    nc.vector.tensor_copy(right(kq[:, :, :], lv), right(b, lv))
                nc.vector.tensor_tensor(left(kq[:, :, :], lv), end, left(b, lv), ALU.subtract).then_inc(s_hv, 1)
                mask = hmask[:, 0 if prev == 0 else 1 + LVL.index(prev), :].unsqueeze(1).to_broadcast([P, A_H, P])
                for t in range(2):
                    ps = PS[4 + t][:, :].rearrange("p (h s) -> p h s", h=A_H)
                    dst = atd[:, t, :].rearrange("p (h s) -> p h s", h=A_H)
                    if prev == 0:
                        m = nc.vector.tensor_tensor(dst, ps, mask, ALU.mult)
                    else:
                        m = nc.vector.copy_predicated(dst, mask.bitcast(mybir.dt.uint32), ps)
                link(m)

            def left(v, m):
                return v.rearrange("p h (n a m) -> p (h n) a m", a=2, m=m)[:, :, 0, :]

            def right(v, m):
                return v.rearrange("p h (n a m) -> p (h n) a m", a=2, m=m)[:, :, 1, :]

            kkf = kk[:, :, :].rearrange("p h t -> p (h t)")
            mixf = mix[:, 0:4, :].rearrange("p h t -> p (h t)")

            def hgrn(i):
                k, r = divmod(i - LV0, 3)
                if i == 0:
                    nc.vector.tensor_tensor(lbd, cols("lb"), cols("lb"), ALU.subtract).then_inc(s_hv, 1)
                    dve.wait_ge(s_ha, HA["lb_exp"])
                    link(nc.vector.reciprocal(lbs, lbe))
                    link(nc.vector.tensor_tensor(lbs, lbs, lbe, ALU.mult))
                    link(nc.vector.tensor_tensor(lbc, lbs, lbs, ALU.subtract))
                    link(nc.vector.tensor_scalar(oml, lbc, -1.0, 1.0, ALU.mult, ALU.add))
                    link(nc.vector.tensor_scalar(kk[:, :, :], kk[:, :, :], 1.0, None, ALU.add),
                         nc.vector.tensor_scalar(kq[:, :, :], kq[:, :, :], 1.0, None, ALU.add))
                if i == 1:
                    link(nc.vector.reciprocal(kk[:, :, :], kk[:, :, :]), nc.vector.reciprocal(kq[:, :, :], kq[:, :, :]))
                if i == 2:
                    link(nc.vector.tensor_tensor(kk[:, :, :], kk[:, :, :], wide(oml), ALU.mult),
                         nc.vector.tensor_tensor(kq[:, :, :], kq[:, :, :], wide(oml), ALU.mult))
                if i == 3:
                    link(nc.vector.tensor_tensor(kq[:, :, :], kq[:, :, :], wide(lbc), ALU.add))
                    nc.vector.tensor_scalar(f4, kq[:, :, :], LN_SPLIT, None, ALU.max)
                    nc.vector.tensor_scalar(kq[:, :, :], kq[:, :, :], TINY, LN_SPLIT, ALU.max, ALU.min).then_inc(s_hv, 1)
                if i == 5:
                    dve.wait_ge(s_ha, HA["ln"])
                    nc.vector.tensor_tensor(f4, f4, kq[:, :, :], ALU.add).then_inc(s_hv, 1)
                    dve.wait_ge(s_hv, HV["w_free_q"])
                    dve.wait_ge(s_hp, HP["vT"])
                    for h in range(A_H):
                        for t in range(2):
                            m = nc.vector.tensor_tensor_scan(i4[:, h, qt(t)], ones[:, :], f4[:, h, qt(t)], 0.0,
                                                             ALU.mult, ALU.add)
                    link(m)
                if i == 6:
                    for h in range(A_H):
                        for t in range(4):
                            s = slice(64 * t, 64 * t + 64)
                            m = nc.vector.tensor_tensor_scan(f4[:, h, s], ones[:, 0:64], f4[:, h, s], 0.0,
                                                             ALU.mult, ALU.add)
                    link(m)
                if i in (7, 9):
                    name, v = ("q", q4) if i == 7 else ("g", g4)
                    dve.wait_ge(s_ha, HA["sig_" + name])
                    nc.vector.tensor_tensor(v, v, kq[:, :, :], ALU.mult).then_inc(s_hv, 1)
                    dve.wait_ge(s_hv, HV["w_free_g" if i == 7 else "silu_g"])
                if r == 0 and 0 <= k < len(LEVELS):
                    if k == 0:
                        dve.wait_ge(s_hm, 16)
                    decays(k)
                if r == 2 and 0 <= k < len(LEVELS):
                    lv = LEVELS[k]
                    dve.wait_ge(s_ha, HA[f"exp{lv}"])
                    nc.vector.tensor_tensor(left(kq[:, :, :], lv), left(kq[:, :, :], lv), left(kk[:, :, :], lv), ALU.mult)
                    nc.vector.tensor_tensor(right(kq[:, :, :], lv), right(kq[:, :, :], lv), right(q4, lv),
                                            ALU.mult).then_inc(s_hv, 1)
                if i == LV0 + 3 * len(LEVELS) + 2:
                    dve.wait_ge(s_hp, HP["var"])
                    link(*[nc.vector.tensor_scalar(kkf[:, 512 * g:512 * (g + 1)], PS[4 + g][:, :], 1.0 / HD, EPS,
                                                   ALU.mult, ALU.add) for g in range(2)])
                    nc.vector.reciprocal(kkf, kkf).then_inc(s_hv, 1)
                if i == LV0 + 3 * len(LEVELS) + 3:
                    dve.wait_ge(s_ha, HA["rstd"])
                    link(*[nc.vector.scalar_tensor_tensor(mixf[:, 512 * g:512 * (g + 1)], PS[6 + g][:, :], cols("onorm"),
                                                          kkf[:, 512 * g:512 * (g + 1)], ALU.mult, ALU.mult)
                           for g in range(2)])
                    nc.vector.tensor_tensor(mix[:, 0:4, :], mix[:, 0:4, :], g4, ALU.mult).then_inc(s_hv, 1)

            fulls(U_B, lambda j: take(sec[:, S0 + j, :]), between=hgrn)

            link(nc.vector.tensor_scalar(gsc[:, 0:1], cols("fq"), HD ** -0.5, None, ALU.mult),
                 nc.vector.tensor_scalar(gsc[:, 1:2], cols("mq"), HD ** -0.5, None, ALU.mult))
            z = sec[0:B_H, S0 + 18, :]

            def fox(i):
                head_norm(HN_FOX, S0, gsc[:, 0:1], cols("fk"), i)
                if i == FOX_V:
                    nc.vector.tensor_scalar(z, z, cols("bf")[0:B_H, :], None, ALU.add).then_inc(s_fv, 1)
                if i == FOX_V + 2:
                    dve.wait_ge(s_fa, 2)
                    link(nc.vector.tensor_scalar(z, z, 0.0, None, ALU.min))
                    nc.vector.tensor_scalar(gtmp[:, :], gtmp[:, :], 1.0, None, ALU.add).then_inc(s_fv, 1)
                if i == FOX_V + 4:
                    dve.wait_ge(s_fa, 3)
                    link(nc.vector.tensor_tensor(z, z, gtmp[:, :], ALU.subtract))
                    link(nc.vector.tensor_tensor_scan(fnp[:, 0, qt(0)], ones[0:B_H, :], z[:, qt(0)], 0.0, ALU.mult, ALU.add))
                    link(nc.vector.tensor_tensor_scan(fnp[:, 0, qt(1)], ones[0:B_H, :], z[:, qt(1)], fnp[:, 0, P - 1:P],
                                                      ALU.mult, ALU.add))
                    nc.vector.tensor_scalar(fnp[:, 1, :], fnp[:, 0, :], -1.0, None, ALU.mult).then_inc(s_qk, 1)
                if 0 <= i - FOX_J < 2 * B_H + JOB_LAG:
                    job_step(J_FOX, fox_job, 2 * B_H, i - FOX_J)
                head_norm(HN_MOBA, S1, gsc[:, 1:2], cols("mk"), i - MOBA_N)

            fulls(U_C, lambda j: take(sec[:, S1 + j, :]), lambda j: 1, fox)

            def moba(i):
                if i >= MOBA_J:
                    job_step(J_MOBA, moba_job, 2 * C_H, i - MOBA_J)

            dve.wait_ge(s_oe, J_MOBA)
            eights("mix", J_SWA, moba, nmod=1)
            norm(N_FFN, cols("ffn"))

            def conv(j):
                q = j % 2
                if c.n["g"] >= 2:
                    dve.wait_ge(s_conv, c.val("g", c.n["g"] - 1))
                take(hg[:, q, 2:T + 2])
                w = lambda i: cvp[:, 4 * j + i:4 * j + i + 1]
                dve.wait_ge(s_evac, c.val("b", c.n["b"]))
                if c.n["g"] >= 2:
                    dve.wait_ge(s_gel, c.val("g", c.n["g"] - 1))
                link(nc.vector.tensor_scalar(cv[:, q, :], hg[:, q, 2:T + 2], w(2), w(3), ALU.mult, ALU.add))
                link(nc.vector.scalar_tensor_tensor(cv[:, q, :], hg[:, q, 1:T + 1], w(1), cv[:, q, :], ALU.mult, ALU.add))
                nc.vector.scalar_tensor_tensor(cv[:, q, :], hg[:, q, 0:T], w(0), cv[:, q, :], ALU.mult, ALU.add).then_inc(s_conv, 1)
                c.n["g"] += 1

            def product(j):
                y = c.n["y"]
                if y >= 2:
                    dve.wait_ge(s_hy, c.val("y", y - 1))
                take(up[:, j % 2, :])
                dve.wait_ge(s_evac, c.val("b", c.n["b"]))
                dve.wait_ge(s_gel, c.val("y", y + 1))
                if y >= 2:
                    dve.wait_ge(s_h, c.val("y", y - 1))
                nc.vector.tensor_tensor(yf[:, y % 2, :], up[:, j % 2, :], gel[:, j, :], ALU.mult).then_inc(s_hy, 1)
                c.n["y"] += 1

            def h_lo(buf, j):
                l = c.n["l"]
                dve.wait_ge(s_hh, c.val("l", l + 1))
                nc.vector.tensor_tensor(hs[:, buf, j, 1, :], yf[:, l % 2, :], hs[:, buf, j, 0, :].bitcast(F32),
                                        ALU.subtract).then_inc(s_h, 1)
                c.n["l"] += 1

            def units(n, ev, first=None, lo_first=None, h_lo_of=None, nmod=0, m0=None):
                for j in range(n):
                    half((lambda: ev(j - 1)) if j else first,
                         after=(lambda: h_lo_of(j - 1)) if j and h_lo_of else (lo_first if j == 0 else None))
                    half(after=(lambda: mods(nmod, m0 if m0 is None else m0 + j * nmod)) if nmod else None)

            def downs(first, lo_first=None, gate=None, nmod=0, m0=None):
                for i in range(KB):
                    half((lambda: add_blocks([i - 1], gate)) if i else first,
                         after=lo_first if i == 0 else
                         ((lambda: mods(nmod, m0 + (i // 2) * nmod)) if nmod and i % 2 else None))

            def last_down(gate=None):
                return lambda: add_blocks([KB - 1], gate)

            def load_taps(n, blocks=CH, dyn=False):
                o = COLS["conv"][0] + 4 * CH * n
                src = par[:, bass.ds(c.i * (4 * CH) + o, 4 * CH)] if dyn else par[:, o:o + 4 * blocks]
                link(nc.vector.tensor_copy(cvp[:, 0:4 * blocks], src))

            link(nc.vector.memset(hg[:, :, 0:2], 0.0))
            load_taps(0)
            units(CH, conv, nmod=1)
            units(CH, product, first=lambda: conv(CH - 1), h_lo_of=lambda j: h_lo(0, j), nmod=1)

            def ffn1_body():
                units(CH, conv, first=lambda: product(CH - 1), lo_first=lambda: (h_lo(0, CH - 1), load_taps(1, dyn=True)),
                      nmod=1, m0=0)
                downs(lambda: conv(CH - 1), nmod=1, m0=CH)
                units(CH, product, first=last_down(), h_lo_of=lambda j: h_lo(0, j), nmod=1, m0=2 * CH)
                dve.wait_ge(s_modu, c.val("m", c.n["m"]))
                link(nc.vector.tensor_copy(modp[:, bass.ds(c.i * MODS + M0, MODS)], modt[:, 0:MODS]))
            MODS, M0 = 3 * CH, c.n["m"]
            c.loop(NC1 - 1, ffn1_body, h=6 * CH, b=2 * CH + KB, c=KB + 2 * CH + 2, m=MODS, g=CH, y=CH, l=CH)
            units(CH_LAST, conv, first=lambda: product(CH - 1),
                  lo_first=lambda: (h_lo(0, CH - 1), load_taps(NC1, CH_LAST)))
            downs(lambda: conv(CH_LAST - 1))
            units(CH_LAST, product, first=last_down(), h_lo_of=lambda j: h_lo(0, j))
            for j in range(KB // 4):
                half((lambda: add_blocks([4 * j - 2, 4 * j - 1])) if j else (lambda: product(CH_LAST - 1)),
                     after=None if j else (lambda: h_lo(0, CH_LAST - 1)))
                half(lambda: add_blocks([4 * j, 4 * j + 1]))
            tail(lambda: add_blocks([KB - 2, KB - 1]))

            for k in range(2):
                lo(XS["p"], k, mix[:, k, :])
            for u in range(U_PLEP):
                for hf in range(2):
                    o = 8 * u + 4 * hf
                    half((lambda: [take(mix[:, o - 4 + q, :]) for q in range(4)]) if o else None)
            tail(lambda: [take(mix[:, 12 + q, :]) for q in range(4)])
            norm(N_PLE, cols("ple"))

            def ple_in(j):
                take(yf[:, j % 2, :])

            def ple_add(j):
                dve.wait_ge(s_ps, j + 1)
                link(nc.vector.tensor_tensor(up[:, 1, :], yf[:, j % 2, :], mix[:, j, :], ALU.mult))
                nc.vector.tensor_tensor(x[:, j, :], x[:, j, :], up[:, 1, :], ALU.add).then_inc(s_pled, 1)

            rest = NMOD - c.n["m"]
            for j in range(U_PLEG):
                half((lambda: ple_in(j - 1)) if j else None, after=lambda: mods(rest * (j + 1) // U_PLEG - rest * j // U_PLEG))
                half(after=(lambda: ple_add(j - 1)) if j else None)
            tail(lambda: ple_in(U_PLEG - 1))
            ple_add(U_PLEG - 1)
            parts = modp[:, :].rearrange("p (n a) -> p n a", a=2)
            link(nc.vector.tensor_tensor(mod[:, :], parts[:, :, 0], parts[:, :, 1], ALU.add))
            link(nc.vector.tensor_tensor(mod[:, :], mod[:, :], cols("bmod"), ALU.add))
            SH1, SC1, G1, SH2, SC2, G2 = (mod[:, KB * i:KB * (i + 1)] for i in range(6))
            link(nc.vector.tensor_scalar(gmod[:, 0:KB], SC1, 1.0, None, ALU.add),
                 nc.vector.tensor_scalar(gmod[:, KB:2 * KB], SC2, 1.0, None, ALU.add))
            link(nc.vector.tensor_tensor(gmod[:, 0:KB], gmod[:, 0:KB], cols("attn2"), ALU.mult))
            m = nc.vector.tensor_tensor(gmod[:, KB:2 * KB], gmod[:, KB:2 * KB], cols("mlp2"), ALU.mult)
            m.then_inc(s_mod, 1)
            dve.wait_ge(s_mod, 1)
            norm(N_ATTN2, gmod[:, 0:KB], SH1)

            def swa(i):
                if i == REL_C:
                    dve.wait_ge(s_rl, 32)
                    nc.vector.tensor_copy(relh[:, :, :], relb[:, :].unsqueeze(2).to_broadcast([REL + 1, SWA_H, P])
                                          ).then_inc(s_rh, 1)
                if i == LAT + 1:
                    for j in range(2):
                        dve.wait_ge(s_hss, HN_MLA + j + 1)
                        inv_var(hvr[:, j, 0:T], PS[4 + j][:, 0:T], (MLA_QR, MLA_KVR)[j]).then_inc(s_hvar, 1)
                if i == LAT + 3:
                    dve.wait_ge(s_hr, HN_MLA + 1)
                    for k in range(4):
                        g = cols("kvn") if k == 3 else cols("qn")[:, k:k + 1]
                        b = sec[:, CQ + k, :]
                        m = nc.vector.scalar_tensor_tensor(b, b, g, hvr[:, k // 3, 0:T], ALU.mult, ALU.mult)
                    m.then_inc(s_qk, 1)
                    dve.wait_ge(s_qk, 3)
                for j in swa_steps(i):
                    if j == 0:
                        dve.wait_ge(s_rb, 16 * SWA_H)
                    job_step(J_SWA, swa_job, 2 * SWA_H, j)

            fulls(U_IN2, lambda j: take(sec[:, j, :]), between=swa)
            for k in range(4):
                lo(XS["cq"], k, sec[:, CQ + k, :])
            n, groups = 0, []
            dst = ([sec[:, QN + q, :] for q in range(12)] + [sec[:, KN + q, :] for q in range(MLA_H)]
                   + [mix[:, 8 + q, :] for q in range(MLA_H)])
            for size in [2] * (2 * U_UQ) + [4] * (2 * U_UKV):
                groups.append(dst[n:n + size])
                n += size
            for n in range(len(groups)):
                half((lambda: [take(b) for b in groups[n - 1]]) if n else None, after=lambda: swa(2 * U_IN2 + n))
            tail(lambda: [take(b) for b in groups[-1]])

            def mla(i):
                if i == 0:
                    dve.wait_ge(s_cs, 32)
                    dve.wait_ge(s_evac, FIRST["out2"][1])
                if i < len(ROPE):
                    dve.wait_ge(s_pm, i + 1)
                    if i:
                        dve.wait_ge(s_kvr, i)
                    b = sec[:, ROPE[i], :]
                    m1 = nc.vector.tensor_tensor(rtmp[:, 0, :], PS[4 + i % 2][:, 0:T], cossin[:, 1, :], ALU.mult)
                    link(m1, nc.vector.tensor_tensor(rtmp[:, 1, :], b, cossin[:, 0, :], ALU.mult))
                    nc.vector.tensor_tensor(b, rtmp[:, 0, :], rtmp[:, 1, :], ALU.add).then_inc(s_kvr, 1)
                for j in mla_steps(i):
                    if j == 0:
                        dve.wait_ge(s_kvr, len(ROPE))
                    job_step(J_MLA, mla_job, 2 * MLA_H, j)

            dve.wait_ge(s_oe, J_MLA)
            eights("mix2", J_END, mla, G1)
            norm(N_MLP2, gmod[:, KB:2 * KB], SH2)

            def relu2(j):
                y = c.n["y"]
                dve.wait_ge(s_hy, c.val("y", y - 1))
                take(up[:, j % 2, :])
                dve.wait_ge(s_evac, c.val("b", c.n["b"]))
                dve.wait_ge(s_h, c.val("y", y - 1))
                nc.vector.scalar_tensor_tensor(yf[:, y % 2, :], up[:, j % 2, :], 0.0, up[:, j % 2, :],
                                               ALU.max, ALU.mult).then_inc(s_hy, 1)
                c.n["y"] += 1

            units(CH, relu2, h_lo_of=lambda j: h_lo(0, j))
            units(CH, relu2, first=lambda: relu2(CH - 1), lo_first=lambda: h_lo(0, CH - 1), h_lo_of=lambda j: h_lo(1, j))

            def ffn2_body():
                for q in range(2):
                    downs(lambda: relu2(CH - 1), lo_first=lambda: h_lo(1 - q, CH - 1), gate=G2)
                    units(CH, relu2, first=last_down(G2), h_lo_of=lambda j: h_lo(q, j))
            c.loop(NC2 // 2 - 1, ffn2_body, h=8 * CH, b=2 * (CH + KB), c=2 * KB, y=2 * CH, l=2 * CH)
            downs(lambda: relu2(CH - 1), lo_first=lambda: h_lo(1, CH - 1), gate=G2)
            downs(last_down(G2), gate=G2)
            tail(last_down(G2))
            norm(N_FINAL, cols("final"))


_OUT = "out_0_dram"


def kernel(**inputs):
    import concourse.bacc as bacc
    from concourse.bass_utils import run_bass_kernel_spmd as run

    i = {k: np.asarray(v) for k, v in inputs.items()}
    f32 = np.float32

    def feature_major(m):
        return np.ascontiguousarray(m.T.reshape(-1, P, m.shape[0]).transpose(1, 0, 2))

    def tiles(m):
        k, n = m.shape
        return m.reshape(k // P, P, n // P, P).transpose(2, 1, 0, 3)

    w = np.zeros((UNITS, P, 2, 8, P), f32)
    at = [0]

    def put(t, per_half):
        b, _, k, _ = t.shape
        if per_half == 0:
            w[at[0]:at[0] + b] = t.reshape(b, P, 2, 8, P)
            at[0] += b
        else:
            t = t.reshape(b // (2 * per_half), 2, per_half, P, k, P).transpose(0, 3, 1, 2, 4, 5)
            n = t.shape[0]
            w[at[0]:at[0] + n, :, :, 0:per_half * k] = t.reshape(n, P, 2, per_half * k, P)
            at[0] += n

    w_in = i["w_in"][0]
    a_w, b_w, c_w = A_H * HD, B_H * HD, C_H * HD
    o = 4 * a_w + 3 * b_w
    put(tiles(w_in[:, 0:o]), 0)
    put(tiles(w_in[:, o:o + P]), 0)
    put(tiles(w_in[:, o + B_H:o + B_H + 3 * c_w]), 0)
    for k in (0, KB // 2):
        put(tiles(i["w_out"][0])[:, :, k:k + KB // 2, :], 1)
    gate, up, down = (i[k][0] for k in ("w_gate", "w_up", "w_down"))
    n = CH * P
    for c in range(NC1 + 1):
        put(tiles(gate[:, c * n:(c + 1) * n]), 0)
        if c:
            put(tiles(down[(c - 1) * n:c * n, :]), 1)
        put(tiles(up[:, c * n:(c + 1) * n]), 0)
    put(tiles(down[NC1 * n:, :]), 2)
    put(tiles(i["w_ple_proj"][0]), 4)
    put(tiles(i["w_ple_gate"][0]), 0)
    w2 = i["w_in_2"][0]
    q, kv = SWA_H * SWA_D, SWA_D
    kr = q + 2 * SWA_KV * kv + MLA_QR + MLA_KVR
    lat = q + 2 * SWA_KV * kv
    put(tiles(np.concatenate([w2[:, lat:kr], w2[:, kr:], w2[:, kr:]]
                             + [w2[:, q + g * kv:q + (g + 1) * kv] for g in (0, 0, 1, 1)]
                             + [w2[:, q + SWA_KV * kv:lat], w2[:, 0:q]], axis=1)), 0)
    uq = i["w_uq_2"][0].reshape(MLA_QR, MLA_H, MLA_N + MLA_R)
    put(tiles(np.concatenate([uq[:, :, :MLA_N].reshape(MLA_QR, -1), uq[:, :, MLA_N:].reshape(MLA_QR, -1)], axis=1)), 2)
    ukv = i["w_ukv_2"][0].reshape(MLA_KVR, MLA_H, MLA_N + HD)
    put(tiles(np.concatenate([ukv[:, :, :MLA_N].reshape(MLA_KVR, -1), ukv[:, :, MLA_N:].reshape(MLA_KVR, -1)], axis=1)), 4)
    for k in (0, KB // 2):
        put(tiles(i["w_out_2"][0])[:, :, k:k + KB // 2, :], 1)
    ff1, ff2 = i["w_ff1_2"][0], i["w_ff2_2"][0]
    for c in range(NC2 + 2):
        if c >= 2:
            put(tiles(ff2[(c - 2) * n:(c - 1) * n, :]), 1)
        if c < NC2:
            put(tiles(ff1[:, c * n:(c + 1) * n]), 0)
    assert at[0] == UNITS

    par = np.zeros((P, NPAR), f32)

    def param(name, v):
        o, k = COLS[name]
        par[:, o:o + k] = v.reshape(k, P).T
    for name, key in (("attn", "attn_norm"), ("ffn", "ffn_norm"), ("ple", "ple_norm"), ("attn2", "attn_norm_g_2"),
                      ("mlp2", "mlp_norm_g_2"), ("final", "final_norm_g_2"), ("fq", "fox_qnorm"), ("fk", "fox_knorm"),
                      ("mq", "moba_qnorm"), ("mk", "moba_knorm"), ("onorm", "hgrn_onorm"), ("lb", "lb_logits"),
                      ("qn", "mla_q_norm_g_2"), ("kvn", "mla_kv_norm_g_2"), ("bmod", "b_mod_2")):
        param(name, i[key])
    par[0:B_H, COLS["bf"][0]] = i["fox_bf"][0]
    par[:, COLS["sink"][0]:COLS["sink"][0] + SWA_H] = i["swa_sinks_2"]
    taps = np.concatenate([i["conv_w"][0], i["conv_b"]], axis=0).reshape(4, -1, P)
    par[:, COLS["conv"][0]:] = taps.transpose(2, 1, 0).reshape(P, -1)

    p_, j_ = np.arange(P)[:, None], np.arange(T)[None, :]
    seen = j_ <= P + p_
    dist = np.where(seen, -(P + p_ - j_), -1e33).astype(f32)
    causal = np.where(seen, 0.0, NEG).astype(f32)
    s_, t_ = np.arange(P)[:, None], np.arange(P)[None, :]
    hmask = np.stack([s_ == t_] + [(s_ // (2 * m) == t_ // (2 * m)) & (s_ // m % 2 == 0) & (t_ // m % 2 == 1)
                                   for m in LVL], axis=1).astype(f32)
    d = 2 * P - 1 - np.arange(3 * P)
    ok = (d >= 0) & (d < P)
    nf = np.maximum(d, 1).astype(f32)
    far = REL // 2 + (np.log(nf / f32(REL // 2)) / f32(np.log(P / (REL // 2))) * f32(REL // 2)).astype(np.int32)
    bucket = np.where(ok, np.where(d < REL // 2, d, np.minimum(far, REL - 1)), REL)
    oneh = (np.arange(REL + 1)[:, None] == bucket[None, :]).astype(f32)
    rel = np.concatenate([i["rel_bias_2"], np.full((1, SWA_H), NEG, f32)], axis=0)
    half = MLA_R // 2
    freq = f32(10000.0) ** (-np.arange(half, dtype=f32) / f32(half))
    ang = (np.arange(T, dtype=f32)[None, :] * freq[:, None])[np.arange(P) % half]
    sign = np.where(np.arange(P) % MLA_R < half, -1.0, 1.0).astype(f32)[:, None]
    cossin = np.stack([np.cos(ang), sign * np.sin(ang)], axis=1).astype(f32)
    swap = np.where(np.arange(P) % MLA_R < half, np.arange(P) + half, np.arange(P) - half)
    perm = (np.arange(P)[:, None] == swap[None, :]).astype(f32)

    arrays = {
        "w": w.reshape(UNITS, P, 2048),
        "wmod": np.ascontiguousarray(i["w_mod_2"][0].T).reshape(6 * KB, P, 2, 1024).transpose(0, 2, 1, 3).reshape(NMOD, P, 1024),
        "x": feature_major(i["x"][0]), "p": feature_major(i["p"][0, 0]),
        "c": np.ascontiguousarray(np.broadcast_to(i["c_2"], (P, DM))),
        "par": par, "ident": np.eye(P, dtype=f32), "dist": dist, "causal": causal, "hmask": hmask,
        "rel": rel, "oneh": oneh, "cossin": cossin, "perm": perm,
    }
    nc = bacc.Bacc("TRN2", target_bir_lowering=False, num_devices=1)
    aps = {}
    for name, v in arrays.items():
        arrays[name] = v = np.ascontiguousarray(v)
        aps[name] = nc.dram_tensor(f"in_{name}", v.shape, mybir.dt.from_np(v.dtype), kind="ExternalInput").ap()
    aps["out"] = nc.dram_tensor(_OUT, (P, KB, T), F32, kind="ExternalOutput").ap()
    build(nc, aps)
    r = run(nc, [{f"in_{k}": v for k, v in arrays.items()}], core_ids=[0])
    got = r.results[0][_OUT]
    return got.transpose(2, 1, 0).reshape(1, T, DM)
```

```python
from contextlib import ExitStack

import numpy as np
import concourse.bass as bass
from concourse import mybir

F32 = mybir.dt.float32
F32R = mybir.dt.float32r
ACT = mybir.ActivationFunctionType
ALU = mybir.AluOpType
AX = mybir.AxisListType

P = 128
T = 256
DM = 2048
KB = DM // P
EPS = 1e-6
TINY = 1e-30
NEG = -1e30
HD = 128
A_H, B_H, C_H = 4, 6, 6
D_FF = 5632
D_FF2 = 8192
SWA_H, SWA_D, SWA_KV = 16, 64, 2
MLA_H, MLA_N, MLA_R = 8, 128, 64
MLA_QR, MLA_KVR = 384, 128
REL = 32
LVL = [1, 2, 4, 8, 16, 32, 64]
LN_SPLIT = 2.0 ** -40
SLOPES = [float(np.float32(2.0) ** np.float32(-8.0 * (i + 1) / C_H)) for i in range(C_H)]

CH = 8
NC1 = D_FF // (CH * P)
CH_LAST = D_FF // P - CH * NC1
NC2 = D_FF2 // (CH * P)
U_A, U_B, U_C = 16, 19, 18
U_OUT = 8
U_FFN1 = 3 * D_FF // P
U_PLEP, U_PLEG = 2, 16
U_IN2 = 16
U_UQ, U_UKV = 3, 2
U_FFN2 = 2 * D_FF2 // P
UNITS = U_A + U_B + U_C + 2 * U_OUT + U_FFN1 + U_PLEP + U_PLEG + U_IN2 + U_UQ + U_UKV + 2 * U_OUT + U_FFN2
RAW = 4
HS = 4
LOOK = 3
NMOD = 2 * 6 * KB
MOD_SLOTS = 2

COLS = {}
_n = 0
for _name, _k in (("attn", 16), ("ffn", 16), ("ple", 16), ("attn2", 16), ("mlp2", 16), ("final", 16),
                  ("fq", 1), ("fk", 1), ("mq", 1), ("mk", 1), ("onorm", 1), ("lb", 4),
                  ("qn", 3), ("kvn", 1), ("bf", 1), ("sink", 16), ("eps", 1), ("bmod", 96), ("conv", 4 * (D_FF // P))):
    COLS[_name] = (_n, _k)
    _n += _k
NPAR = _n


def stages(*names):
    return {n: i + 1 for i, n in enumerate(names)}


class Counts:

    def __init__(self, eng, **start):
        self.eng, self.n, self.i, self.per = eng, dict(start), None, {}

    def val(self, name, value):
        step = self.per.get(name, 0)
        return value + self.i * step if step else value

    def loop(self, times, body, **per):
        before = dict(self.n)
        with self.eng.Fori(0, times) as i:
            self.i, self.per = i, per
            body()
        up = {k: self.n[k] - before[k] for k in self.n}
        assert all(up[k] == per.get(k, 0) for k in up), (up, per)
        self.i, self.per = None, {}
        for k in up:
            self.n[k] = before[k] + times * up[k]


HA = stages("exp_nf", "lb_exp", "vtok", "ln", "sig_q", "sig_g",
            *[f"exp{m}" for m in LVL + [128]], "at01", "sq", "rms")
HV = stages("lb_d", "ln_in", "w_free_q", "w_free_g", "silu_g",
            *[x for m in LVL + [128] for x in (f"dec{m}", f"kq{m}")], "rstd", "done")
HP = stages("vT", "lvl0", *[f"lvl{m}" for m in LVL + [128]], "o", "var", "rstd")


def build(nc, a):
    ctx = ExitStack()
    with ctx:
        base = [16512]

        def at(name, shape, off_kb, dt=F32):
            return nc.alloc_sbuf_tensor_at(name, shape, dt, offset=base[0] + int(off_kb * 1024))

        def sem(name):
            return ctx.enter_context(nc.semaphore(name))

        raw = at("raw", [P, RAW, 2048], 0)
        wh = at("wh", [P, HS, 1024], 32, F32R)
        wl = at("wl", [P, HS, 1024], 48, F32R)
        modraw = at("modraw", [P, MOD_SLOTS, 1024], 64)
        cb = at("cb", [P, 2048], 72)
        tbias = at("tbias", [P, SWA_H, T], 64)
        x = at("x", [P, KB, T], 80)
        xs = at("xs", [P, KB, 2, T], 96, F32R)
        mix = at("mix", [P, KB, T], 128)
        sec = at("sec", [P, 37, T], 144)
        S0, S1 = 0, 19
        ident = at("ident", [P, P], 181)
        ones = at("ones", [P, P], 181.5)
        dist = at("dist", [P, T], 182)
        causal = at("causal", [P, T], 183)
        par = at("par", [P, NPAR], 184)
        mod = at("mod", [P, 6 * KB], 185.75)
        modt = at("modt", [P, 3 * CH], 186.125)
        modp = at("modp", [P, NMOD], 186.25)
        gmod = at("gmod", [P, 2 * KB], 187)
        small = at("small", [P, 64], 187.125)
        stat = lambda J, n: small[:, 8 * (J % 3) + 2 * n:8 * (J % 3) + 2 * n + 2]
        strip = small[:, 40:40 + 4 * B_H - 1]
        gsc = at("gsc", [P, 2], 187.375)
        T0 = 187.5
        sq = at("sq", [P, 2, 4, T], T0)
        rstd = at("rstd", [P, T], T0 + 9)
        yn = at("yn", [P, 4, T], T0 + 10)
        crow = at("crow", [KB, P], T0 + 14)
        cexp = at("cexp", [KB, P], T0 + 14.5)
        kk = at("kk", [P, A_H, T], T0)
        kq = at("kq", [P, A_H, T], T0 + 4)
        atd = at("atd", [P, 2, 512], T0 + 8)
        at01 = at("at01", [P, 512], T0 + 12)
        vtok = at("vtok", [P, 2, 512], T0 + 14)
        hmask = at("hmask", [P, 8, P], 128 + 8)
        prob = at("prob", [P, 3, 3 * P], T0)
        probT = at("probT", [P, 2, 3 * P], T0 + 4.5)
        vt = at("vt", [P, 2, 8 * P], T0 + 9)
        gtmp = at("gtmp", [B_H, T], T0 + 17)
        fnp = at("fnp", [B_H, 2, T], T0 + 18)
        hsq = at("hsq", [P, 2, 512], T0)
        hrs = at("hrs", [2 * B_H, T], T0 + 4)
        hsq4 = at("hsq4", [P, 4, T], T0)
        hvr = at("hvr", [P, 2, T], T0 + 4)
        cossin = at("cossin", [P, 2, T], T0 + 17)
        perm = at("perm", [P, P], T0 + 19)
        rtmp = at("rtmp", [P, 2, T], T0 + 3)
        relb = at("relb", [REL + 1, SWA_H], T0)
        relh = at("relh", [REL + 1, SWA_H, P], T0 + 0.5)
        oneh = at("oneh", [REL + 1, 384], T0 + 8.5)
        rrow = at("rrow", [P, 4, 384], T0 + 10)
        up = at("up", [P, 2, T], 144)
        yf = at("yf", [P, 2, T], 146)
        hs = at("hs", [P, 2, CH, 2, T], 148, F32R)
        hg = at("hg", [P, 2, T + 2], 164)
        cv = at("cv", [P, 2, T], 166.25)
        gel = at("gel", [P, CH, T], 168.25)
        cvp = at("cvp", [P, 4 * CH], 176.25)

        PS = [ctx.enter_context(nc.psum_tensor(f"ps{i}", [P, 512], F32)) for i in range(8)]
        rel_dram = nc.dram_tensor("rel_rows", [4, P, 4, 384], F32, kind="Internal").ap()

        s_raw = [sem(f"raw_loaded{i}") for i in range(RAW)]
        s_round, s_split, s_used, s_evac = map(sem, ("hi_rounded", "lo_ready", "half_used", "block_taken"))
        s_modl = [sem(f"mod_loaded{i}") for i in range(MOD_SLOTS)]
        s_modu, s_mod = sem("mod_used"), sem("mod_ready")
        s_dch = sem("dve_chain")
        s_par, s_p, s_c, s_hm, s_cs, s_cact = map(sem, (
            "params_loaded", "p_loaded", "c_loaded", "hmask_loaded", "cossin_loaded", "c_exp_ready"))
        s_crow, s_cps, s_cb = map(sem, ("c_silu_ready", "c_spread", "c_copied"))
        s_x = [sem(f"x_loaded{g}") for g in range(4)]
        s_ones = sem("ones_ready")
        s_sq, s_ssq, s_rms, s_yn, s_yh, s_xs = map(sem, (
            "squares_ready", "square_sums", "rms_ready", "normed", "x_hi_ready", "x_pair_ready"))
        s_ha, s_hv, s_hp = map(sem, ("hgrn_act", "hgrn_dve", "hgrn_pe"))
        s_hsq, s_hss, s_hrms, s_hr, s_hb, s_hn, s_qk = map(sem, (
            "head_squares", "head_square_sums", "head_rms", "head_rstd", "head_rstd_spread",
            "head_normed", "qk_ready"))
        s_vT, s_vt, s_fa, s_fv = map(sem, ("v_transposed", "v_tokens", "gate_act", "gate_dve"))
        s_sc, s_lg, s_nm, s_ex, s_pr, s_tr, s_pt, s_pv, s_oe = map(sem, (
            "scores_ready", "scores_taken", "neg_max_ready", "exp_ready", "probs_ready",
            "probs_transposed", "probsT_copied", "pv_ready", "out_taken"))
        s_rl, s_rh, s_rp, s_rr, s_rw, s_rb = map(sem, (
            "rel_loaded", "rel_spread", "rel_rows_psum", "rel_rows_sbuf", "rel_rows_written", "bias_loaded"))
        s_pm, s_kvr = map(sem, ("rope_swapped", "rope_done"))
        s_conv, s_gel, s_hy, s_hh, s_h = map(sem, ("conv_ready", "gelu_ready", "h_ready", "h_hi_ready", "h_pair_ready"))
        s_ps, s_pled = map(sem, ("ple_sigmoid", "ple_added"))
        s_fin, s_out = map(sem, ("final_ready", "out_stored"))

        block = ctx.enter_context(nc.Block())
        cols = lambda name: par[:, COLS[name][0]:COLS[name][0] + COLS[name][1]]
        col = lambda name, k=0: par[:, COLS[name][0] + k:COLS[name][0] + k + 1]

        FIRST = {}
        u0 = b0 = 0
        for name, nu, nb in (("A", U_A, 16), ("B", U_B, 19), ("C", U_C, 18), ("out", U_OUT, 16), ("outb", U_OUT, 16),
                             ("ffn1", U_FFN1, 2 * (D_FF // P) + KB * (NC1 + 1)), ("plep", U_PLEP, 16), ("pleg", U_PLEG, 16),
                             ("in2", U_IN2, 16), ("uq", U_UQ, 12), ("ukv", U_UKV, 16),
                             ("out2", U_OUT, 16), ("out2b", U_OUT, 16), ("ffn2", U_FFN2, NC2 * (CH + KB))):
            FIRST[name] = (u0, b0)
            u0 += nu
            b0 += nb
        FIRST["end"] = (u0, b0)
        assert u0 == UNITS

        J_FOX, J_MOBA, J_SWA, J_MLA = 0, B_H, B_H + C_H, B_H + C_H + SWA_H
        J_END = J_MLA + MLA_H
        N_ATTN, N_FFN, N_PLE, N_ATTN2, N_MLP2, N_FINAL = range(6)
        XS = {}
        n = 0
        for name, k in (("attn", 16), ("mix", 16), ("ffn", 16), ("p", 2), ("ple", 16), ("attn2", 16),
                        ("cq", 4), ("mix2", 16), ("mlp2", 16)):
            XS[name] = n
            n += k

        def gemm_blocks(kind, h):
            if kind == "full":
                return [(0, [(t, 8 * h + t) for t in range(8)], h == 0, h == 1)]
            if kind == "eight":
                return [(h, [(t, t) for t in range(8)], True, True)]
            if kind == "quad":
                return [(2 * h + b, [(4 * b + k, k) for k in range(4)], True, True) for b in range(2)]
            if kind == "uq":
                return [(2 * h + b, [(3 * b + k, k) for k in range(3)], True, True) for b in range(2)]
            if kind == "oct":
                return [(4 * h + b, [(2 * b + k, k) for k in range(2)], True, True) for b in range(4)]
            return [(4 * h + b, [(b, 0)], True, True) for b in range(4)]

        NBLK = {"full": 1, "eight": 2, "quad": 4, "uq": 4, "oct": 8, "one": 8}
        GAIN_XS = {N_ATTN: "attn", N_FFN: "ffn", N_PLE: "ple", N_ATTN2: "attn2", N_MLP2: "mlp2"}

        C_AT, MOD_UNIT = (2, 3, 4, 5), 3
        JOB_LAG = 3
        LEVELS = LVL + [128]
        LV0 = 10
        FOX_V, FOX_J, MOBA_N = 8, 13, 2 * U_C - 8
        MOBA_J = 1
        REL_C, REL_G, LAT, SWA_J = 4, (5, 8, 11, 14), 16, 20
        IN2_HALVES = 2 * (U_IN2 + U_UQ + U_UKV)
        MLA_J = 5

        SQ_EIGHT, SQ_QUAD, SQ_PLE = 5, 3, 10

        def share(n, i, first, end):
            i, m = i - first, end - first
            return range(n * i // m, n * (i + 1) // m) if 0 <= i < m else ()

        fox_steps = lambda i: share(B_H + JOB_LAG, i, FOX_J, MOBA_N)
        moba_steps = lambda i: share(C_H + JOB_LAG, i, MOBA_J, 2 * U_OUT)
        swa_steps = lambda i: share(SWA_H + JOB_LAG, i, SWA_J, IN2_HALVES)
        mla_steps = lambda i: share(MLA_H + JOB_LAG, i, MLA_J, 2 * U_OUT)

        qt = lambda t: slice(t * P, (t + 1) * P)
        into = lambda j, n: strip[:, 2 * B_H - 1 - j:2 * B_H - 1 - j + n]
        spread = lambda j, n: ident[0:n, j:j + 1].to_broadcast([n, P])

        part = lambda t: slice(P * t, P * (2 * t + 1))
        keys = lambda t: P * (t + 1)

        def fox_job(h):
            sel = ident[0:B_H, h:h + 1]
            return dict(scores=lambda t: [(sec[:, S0 + h, qt(t)], sec[:, S0 + B_H + h, 0:keys(t)]),
                                          (fnp[:, 0, qt(t)], sel.to_broadcast([B_H, keys(t)])),
                                          (sel.to_broadcast([B_H, P]), fnp[:, 1, 0:keys(t)])],
                        bias=causal, scale=1.0, slope=None, sink=None,
                        v=[vt[:, q, h * P:(h + 1) * P] for q in range(2)], rows=slice(0, P), out=mix[:, A_H + h, :])

        def moba_job(h):
            return dict(scores=lambda t: [(sec[:, S1 + h, qt(t)], sec[:, S1 + C_H + h, 0:keys(t)])],
                        bias=dist, scale=None, slope=SLOPES[h], sink=None,
                        v=[vt[:, q, h * P:(h + 1) * P] for q in range(2)], rows=slice(0, P), out=mix[:, A_H + B_H + h, :])

        CQ, CKV, KR, SWA_K, SWA_V, SWA_Q = 0, 3, 4, 5, 7, 8
        QN, QR, KN = 16, 24, 28
        _dst = ([sec[:, QN + q, :] for q in range(12)] + [sec[:, KN + q, :] for q in range(MLA_H)]
                + [mix[:, 8 + q, :] for q in range(MLA_H)])
        LATENT_DST = [_dst[2 * n:2 * n + 2] for n in range(6)] + [_dst[12 + 4 * n:16 + 4 * n] for n in range(4)]
        ROPE = [QR, QR + 1, QR + 2, QR + 3, KR]

        def swa_job(h):
            r = slice(SWA_D * (h % 2), SWA_D * (h % 2) + SWA_D)
            kv = h // (SWA_H // SWA_KV)
            return dict(scores=lambda t: [(sec[r, SWA_Q + h // 2, qt(t)], sec[r, SWA_K + kv, 0:keys(t)])],
                        bias=tbias[:, h, :], scale=SWA_D ** -0.5, slope=None, sink=col("sink", h),
                        v=[vt[:, 0, q * P + kv * SWA_D:q * P + (kv + 1) * SWA_D] for q in range(2)],
                        rows=r, out=mix[r, h // 2, :])

        def mla_job(h):
            r = slice(MLA_R * (h % 2), MLA_R * (h % 2) + MLA_R)
            return dict(scores=lambda t: [(sec[:, QN + h, qt(t)], sec[:, KN + h, 0:keys(t)]),
                                          (sec[r, QR + h // 2, qt(t)], sec[r, KR, 0:keys(t)])],
                        bias=causal, scale=(MLA_N + MLA_R) ** -0.5, slope=None, sink=None,
                        v=[vt[:, q, h * P:(h + 1) * P] for q in range(2)], rows=slice(0, P), out=mix[:, 8 + h, :])

        @block.sync
        def _(sp):
            for g in range(4):
                sp.dma_start(x[:, 4 * g:4 * g + 4, :], a["x"][:, 4 * g:4 * g + 4, :]).then_inc(s_x[g], 16)
            for dst, src in ((par[:, :], a["par"]), (ident[:, :], a["ident"]),
                             (dist[:, :], a["dist"]), (causal[:, :], a["causal"])):
                sp.dma_start(dst, src).then_inc(s_par, 16)
            for u in range(RAW):
                sp.dma_start(raw[:, u, :], a["w"][u, :, :]).then_inc(s_raw[u], 16)
            sp.dma_start(hmask[:, :, :], a["hmask"]).then_inc(s_hm, 16)
            rounds, rest = divmod(UNITS - RAW, RAW)
            with sp.Fori(0, rounds) as i:
                for r in range(RAW):
                    sp.wait_ge(s_split, i * (2 * RAW) + 2 * r + 2)
                    sp.dma_start(raw[:, r:r + 1, :],
                                 a["w"][bass.ds(i * RAW + (RAW + r), 1), :, :].rearrange("a p n -> p a n")
                                 ).then_inc(s_raw[r], 16)
            for r in range(rest):
                u = RAW * (rounds + 1) + r
                sp.wait_ge(s_split, 2 * (u - RAW) + 2)
                sp.dma_start(raw[:, r, :], a["w"][u, :, :]).then_inc(s_raw[r], 16)
            for q in range(4):
                sp.wait_ge(s_fin, 4 * q + 4)
                sp.dma_start(a["out"][:, 4 * q:4 * q + 4, :], mix[:, 4 * q:4 * q + 4, :]).then_inc(s_out, 16)
            sp.wait_ge(s_out, 64)

        @block.gpsimd
        def _(pool):
            pool.dma_start(crow[:, :], a["c"]).then_inc(s_c, 16)
            for n in range(MOD_SLOTS):
                pool.dma_start(modraw[:, n, :], a["wmod"][n, :, :]).then_inc(s_modl[n], 16)
            with pool.Fori(0, NMOD // MOD_SLOTS - 1) as i:
                for n in range(MOD_SLOTS):
                    pool.wait_ge(s_modu, i * MOD_SLOTS + n + 1)
                    pool.dma_start(modraw[:, n:n + 1, :],
                                   a["wmod"][bass.ds(i * MOD_SLOTS + (MOD_SLOTS + n), 1), :, :]
                                   .rearrange("a p n -> p a n")).then_inc(s_modl[n], 16)
            pool.wait_ge(s_xs, XS["attn2"] + 16)
            pool.wait_ge(s_mod, 1)
            pool.dma_start(relb[:, :], a["rel"]).then_inc(s_rl, 16)
            pool.dma_start(oneh[:, :], a["oneh"]).then_inc(s_rl, 16)
            for g in range(4):
                pool.wait_ge(s_rr, g + 1)
                pool.dma_start(rel_dram[g, :, :, :], rrow[:, :, :]).then_inc(s_rw, 16)
                pool.wait_ge(s_rw, 16 * (g + 1))
                for h in range(4):
                    src = bass.AP(tensor=rel_dram.tensor, offset=g * P * 1536 + h * 384 + P - 1,
                                  ap=[[1536 - 1, P], [1, T]])
                    pool.dma_start(tbias[:, 4 * g + h, :], src).then_inc(s_rb, 16)
            pool.dma_start(cossin[:, :, :], a["cossin"]).then_inc(s_cs, 16)
            pool.dma_start(perm[:, :], a["perm"]).then_inc(s_cs, 16)

        @block.tensor
        def _(pe):
            c = Counts(pe, h=0, b=0, hp=0)

            def unit(kind, src, xwait=None, between=None, joined=False):
                for half in range(2):
                    if between:
                        between(half)
                    hh, b = c.n["h"], c.n["b"]
                    pe.wait_ge(s_split, c.val("h", hh + 1))
                    hi, lo = wh[:, hh % HS, :], wl[:, hh % HS, :]
                    for bi, tiles, first, last in gemm_blocks(kind, half):
                        if first and b + bi >= 4:
                            pe.wait_ge(s_evac, c.val("b", b + bi - 3))
                        out = PS[(b + bi) % 4]
                        for n, (t, k) in enumerate(tiles):
                            if xwait is not None and (half == 0 or kind == "full"):
                                pe.wait_ge(s_xs, xwait + k + 1)
                            w = slice(t * P, (t + 1) * P)
                            s, e = first and n == 0, last and n == len(tiles) - 1
                            pair = src[:, k, :, :].rearrange("p a t -> p (a t)")
                            if joined:
                                nc.tensor.matmul(out[:, 0:T], hi[:, w], src[:, k, 0, :], start=s, stop=False)
                                nc.tensor.matmul(out[:, 0:T], hi[:, w], src[:, k, 1, :], start=False, stop=False)
                                m = nc.tensor.matmul(out[:, 0:T], lo[:, w], src[:, k, 0, :], start=False, stop=e)
                            elif e and not s:
                                nc.tensor.matmul(out[:, 0:T], lo[:, w], src[:, k, 0, :], start=False, stop=False)
                                m = nc.tensor.matmul(out[:, :], hi[:, w], pair, start=False, stop=True)
                            else:
                                nc.tensor.matmul(out[:, :], hi[:, w], pair, start=s, stop=e)
                                m = nc.tensor.matmul(out[:, 0:T], lo[:, w], src[:, k, 0, :], start=False,
                                                     stop=e, skip_group_check=e)
                    m.then_inc(s_used, 1)
                    c.n["h"] += 1
                c.n["b"] += NBLK[kind]

            def fulls(n, name):
                unit("full", xs, XS[name])
                for j in range(1, n - (n - 1) // 4 * 4):
                    unit("full", xs)
                c.loop((n - 1) // 4, lambda: [unit("full", xs) for _ in range(4)], h=8, b=4)

            def square_sums(n, g):
                pe.wait_ge(s_sq, 4 * n + g + 1)
                for k in range(4):
                    m = nc.tensor.matmul(PS[4][:, 0:T], ones[:, :], sq[:, g % 2, k, :],
                                         start=g == k == 0, stop=g == k == 3)
                m.then_inc(s_ssq, 1)

            def early_sums(n, i, first, every):
                g, r = divmod(i - first, every)
                if r == 0 and 0 <= g < 3:
                    square_sums(n, g)

            def head_norm(m, i):
                if 1 <= i < 4:
                    for j in (2 * i - 2, 2 * i - 1):
                        pe.wait_ge(s_hsq, 6 * m + j + 1)
                        for q in range(2):
                            mm = nc.tensor.matmul(PS[6][0:2 * B_H, 0:T], into(2 * j + q, 2 * B_H), hsq[:, j % 2, q * T:(q + 1) * T],
                                                  start=j == q == 0, stop=j == 5 and q == 1)
                        mm.then_inc(s_hss, 1)
                if 5 <= i < 8:
                    pe.wait_ge(s_hr, m + 1)
                    for j in (2 * i - 10, 2 * i - 9):
                        if j >= 2:
                            pe.wait_ge(s_hn, 6 * m + j - 1)
                        for q in range(2):
                            mm = nc.tensor.matmul(PS[4 + j % 2][:, q * T:(q + 1) * T], spread(2 * j + q, 2 * B_H),
                                                  hrs[:, :], start=True, stop=True)
                        mm.then_inc(s_hb, 1)

            def v_transposes(n, v, g):
                if g >= 2:
                    pe.wait_ge(s_vt, n + g - 1)
                for q in range(2):
                    for t in range(2):
                        m = nc.tensor.transpose(PS[6 + g % 2][:, (2 * t + q) * P:(2 * t + q + 1) * P],
                                                v[:, 2 * g + q, qt(t)], ident[:, :])
                m.then_inc(s_vT, 1)

            def job_step(j0, make, n, j):
                if j < n:
                    d, J = make(j), j0 + j
                    if J >= 2:
                        pe.wait_ge(s_lg, J - 1)
                    for t in range(2):
                        pairs = d["scores"](t)
                        for q, (l, r) in enumerate(pairs):
                            m = nc.tensor.matmul(PS[4 + J % 2][:, part(t)], l, r, start=q == 0, stop=q == len(pairs) - 1)
                    m.then_inc(s_sc, 1)
                if 0 <= j - 3 < n:
                    d, J = make(j - 3), j0 + j - 3
                    pe.wait_ge(s_pt, J + 1)
                    if J:
                        pe.wait_ge(s_oe, J)
                    for t in range(2):
                        for q in range(t + 1):
                            m = nc.tensor.matmul(PS[7][d["rows"], qt(t)], d["v"][q], probT[:, J % 2, qt(t + q)],
                                                 start=q == 0, stop=q == t)
                    m.then_inc(s_pv, 1)
                if 0 <= j - 2 < n:
                    J = j0 + j - 2
                    pe.wait_ge(s_pr, J + 1)
                    if J:
                        pe.wait_ge(s_pt, J)
                    for q in range(3):
                        m = nc.tensor.transpose(PS[6][:, qt(q)], prob[:, J % 3, qt(q)], ident[:, :])
                    m.then_inc(s_tr, 1)

            pe.wait_ge(s_par, 64)
            pe.wait_ge(s_ones, 2)
            for g in range(4):
                square_sums(N_ATTN, g)
            def spread_c(i):
                if i in C_AT:
                    g = C_AT.index(i)
                    pe.wait_ge(s_crow, 1)
                    if g == 3:
                        pe.wait_ge(s_cb, 1)
                    for j in range(4):
                        m = nc.tensor.matmul(PS[5 + g % 3][:, j * P:(j + 1) * P], spread(4 * g + j, KB), crow[:, :],
                                             start=True, stop=True)
                    m.then_inc(s_cps, 1)

            for u in range(U_A):
                unit("full", xs, XS["attn"] if u == 0 else None, lambda q: spread_c(2 * u + q))

            def level(lv):
                pe.wait_ge(s_hv, HV[f"kq{lv}"] if lv else HV["silu_g"])
                for t in range(2 if lv < 128 else 1):
                    for h in range(A_H):
                        ks = (kq if lv else kk)[:, h, qt(t)]
                        qs = (kq[:, h, qt(t if lv < 128 else 1)] if lv else sec[:, S1 + h, qt(t)])
                        m = nc.tensor.matmul(PS[4 + t][:, h * P:(h + 1) * P], ks, qs, start=True, stop=True)
                m.then_inc(s_hp, 1)

            def hgrn(i):
                k, r = divmod(i - LV0, 3)
                if i == 0:
                    pe.wait_ge(s_evac, FIRST["B"][1])
                    for t in range(2):
                        for h in range(A_H):
                            m = nc.tensor.transpose(PS[6 + t][:, h * P:(h + 1) * P], sec[:, S1 + 8 + h, qt(t)],
                                                    ident[:, :])
                    m.then_inc(s_hp, 1)
                if r == 0 and 0 <= k <= len(LEVELS):
                    level(([0] + LEVELS)[k])
                if i == LV0 + 3 * len(LEVELS) + 1:
                    pe.wait_ge(s_ha, HA["at01"])
                    for h in range(A_H):
                        o, q, hc = PS[6 + h // 2], (h % 2) * T, slice(h * P, (h + 1) * P)
                        nc.tensor.matmul(o[:, q:q + P], vtok[:, 0, hc], atd[:, 0, hc], start=True, stop=True)
                        nc.tensor.matmul(o[:, q + P:q + T], vtok[:, 0, hc], at01[:, hc], start=True, stop=False)
                        m = nc.tensor.matmul(o[:, q + P:q + T], vtok[:, 1, hc], atd[:, 1, hc], start=False, stop=True)
                    m.then_inc(s_hp, 1)
                if i == LV0 + 3 * len(LEVELS) + 2:
                    pe.wait_ge(s_ha, HA["sq"])
                    for h in range(A_H):
                        m = nc.tensor.matmul(PS[4][0:A_H, 0:T], into(h, A_H), kq[:, h, :], start=h == 0, stop=h == A_H - 1)
                    m.then_inc(s_hp, 1)
                if i == LV0 + 3 * len(LEVELS) + 3:
                    pe.wait_ge(s_hv, HV["rstd"])
                    for h in range(A_H):
                        m = nc.tensor.matmul(PS[4 + h // 2][:, (h % 2) * T:(h % 2 + 1) * T], spread(h, A_H),
                                             kk[0:A_H, 0, :], start=True, stop=True)
                    m.then_inc(s_hp, 1)

            for u in range(U_B):
                unit("full", xs, between=lambda q: hgrn(2 * u + q))

            def fox(i):
                head_norm(0, i)
                if 0 <= i - FOX_V < B_H // 2:
                    pe.wait_ge(s_evac, FIRST["C"][1])
                    v_transposes(0, sec[:, S0 + 2 * B_H:S0 + 3 * B_H, :], i - FOX_V)
                for j in fox_steps(i):
                    if j == 0:
                        pe.wait_ge(s_hn, 6)
                        pe.wait_ge(s_qk, 1)
                    job_step(J_FOX, fox_job, B_H, j)
                head_norm(1, i - MOBA_N)

            for u in range(U_C):
                unit("full", xs, between=lambda q: fox(2 * u + q))

            def moba(i):
                if i == 0:
                    pe.wait_ge(s_evac, FIRST["out"][1])
                    pe.wait_ge(s_oe, J_MOBA)
                    for g in range(C_H // 2):
                        v_transposes(3, sec[:, S1 + 2 * C_H:S1 + 3 * C_H, :], g)
                    pe.wait_ge(s_hn, 12)
                for j in moba_steps(i):
                    job_step(J_MOBA, moba_job, C_H, j)

            def eights(name, between, n):
                for u in range(U_OUT):
                    unit("eight", xs[:, 0:8, :, :], XS[name] if u == 0 else None, lambda q: between(2 * u + q))
                for u in range(U_OUT):
                    unit("eight", xs[:, 8:16, :, :], XS[name] + 8 if u == 0 else None,
                         lambda q: early_sums(n, 2 * u + q, SQ_EIGHT + 1, 4))
                square_sums(n, 3)

            eights("mix", moba, N_FFN)

            def down(buf):
                c.n["hp"] += CH
                pe.wait_ge(s_h, c.val("hp", c.n["hp"]))
                for _ in range(KB // 2):
                    unit("eight", hs[:, buf, :, :, :])

            def ups(n=CH, name=None):
                for j in range(n):
                    unit("full", xs, XS[name] if name and j == 0 else None)

            ups(name="ffn")
            ups()
            c.loop(NC1 - 1, lambda: (ups(), down(0), ups()), h=6 * CH, b=2 * CH + KB, hp=CH)
            ups(CH_LAST)
            down(0)
            ups(CH_LAST)
            pe.wait_ge(s_h, CH * NC1 + CH_LAST)
            c.n["hp"] += CH_LAST
            for u in range(KB // 4):
                unit("quad", hs[:, 0, 0:CH_LAST, :, :], between=lambda q: early_sums(N_PLE, 2 * u + q, SQ_QUAD + 1, 2))

            for j in range(U_PLEP):
                unit("oct", xs, XS["p"] if j == 0 else None, joined=True)
            square_sums(N_PLE, 2)
            square_sums(N_PLE, 3)
            for u in range(U_PLEG):
                unit("full", xs, XS["ple"] if u == 0 else None, lambda q: early_sums(N_ATTN2, 2 * u + q, SQ_PLE + 1, 8))
            square_sums(N_ATTN2, 3)

            def swa(i):
                if i in REL_G:
                    g = REL_G.index(i)
                    if g:
                        pe.wait_ge(s_rr, g)
                    else:
                        pe.wait_ge(s_rh, 1)
                        pe.wait_ge(s_rl, 32)
                    for q in range(4):
                        m = nc.tensor.matmul(PS[4 + q][:, 0:384], relh[:, 4 * g + q, :], oneh[:, :], start=True, stop=True)
                    m.then_inc(s_rp, 1)
                if i == LAT:
                    pe.wait_ge(s_rr, 4)
                    pe.wait_ge(s_hsq, 13)
                    for k in range(3):
                        m = nc.tensor.matmul(PS[4][:, 0:T], ones[:, :], hsq4[:, k, :], start=k == 0, stop=k == 2)
                    m.then_inc(s_hss, 1)
                    nc.tensor.matmul(PS[5][:, 0:T], ones[:, :], hsq4[:, 3, :], start=True, stop=True).then_inc(s_hss, 1)
                    pe.wait_ge(s_evac, FIRST["in2"][1] + SWA_V + 1)
                    for t in range(2):
                        m = nc.tensor.transpose(PS[7][:, qt(t)], sec[:, SWA_V, qt(t)], ident[:, :])
                    m.then_inc(s_vT, 1)
                for j in swa_steps(i):
                    if j == 0:
                        pe.wait_ge(s_vt, 7)
                        pe.wait_ge(s_hrms, 4)
                    if j % 2 == 0 and j < SWA_H:
                        pe.wait_ge(s_evac, FIRST["in2"][1] + SWA_Q + j // 2 + 1)
                    job_step(J_SWA, swa_job, SWA_H, j)

            for u in range(U_IN2):
                unit("full", xs, XS["attn2"] if u == 0 else None, lambda q: swa(2 * u + q))
            for u in range(U_UQ):
                unit("uq", xs, XS["cq"] if u == 0 else None, lambda q: swa(2 * (U_IN2 + u) + q), True)
            pe.wait_ge(s_xs, XS["cq"] + 4)
            for u in range(U_UKV):
                unit("one", xs[:, 3:4, :, :], between=lambda q: swa(2 * (U_IN2 + U_UQ + u) + q), joined=True)

            def mla(i):
                if i == 0:
                    pe.wait_ge(s_cs, 32)
                    pe.wait_ge(s_evac, FIRST["out2"][1])
                    pe.wait_ge(s_oe, J_MLA)
                if i < len(ROPE):
                    if i >= 2:
                        pe.wait_ge(s_kvr, i - 1)
                    nc.tensor.matmul(PS[4 + i % 2][:, 0:T], perm[:, :], sec[:, ROPE[i], :],
                                     start=True, stop=True).then_inc(s_pm, 1)
                if i < MLA_H // 2:
                    v_transposes(7, mix[:, 8:16, :], i)
                for j in mla_steps(i):
                    if j == 0:
                        pe.wait_ge(s_kvr, len(ROPE))
                    job_step(J_MLA, mla_job, MLA_H, j)

            eights("mix2", mla, N_MLP2)

            ups(name="mlp2")
            ups()
            c.loop(NC2 // 2 - 1, lambda: (down(0), ups(), down(1), ups()), h=8 * CH, b=2 * (CH + KB), hp=2 * CH)
            down(0)
            c.n["hp"] += CH
            pe.wait_ge(s_h, c.n["hp"])
            for u in range(KB // 2):
                unit("eight", hs[:, 1, :, :, :], between=lambda q: early_sums(N_FINAL, 2 * u + q, SQ_EIGHT + 1, 4))
            assert c.n["h"] == 2 * UNITS and c.n["b"] == FIRST["end"][1]
            square_sums(N_FINAL, 3)

        @block.scalar
        def _(act):
            c = Counts(act, h=0, g=0, y=0)

            def rnd(h):
                if h < 2 * UNITS:
                    u = h // 2
                    if h % 2 == 0:
                        v = 16 * (u // RAW + 1)
                        act.wait_ge(s_raw[u % RAW], v + c.i * (c.per["h"] * 16 // (2 * RAW)) if c.per else v)
                    if h >= HS:
                        act.wait_ge(s_used, c.val("h", h - HS + 1))
                    nc.scalar.activation(wh[:, h % HS, :], raw[:, u % RAW, (h % 2) * 1024:(h % 2 + 1) * 1024],
                                         ACT.Copy).then_inc(s_round, 1)

            def step(after=None, between=None):
                for q in range(2):
                    rnd(c.n["h"] + LOOK)
                    c.n["h"] += 1
                    if after and q == 0:
                        after()
                    if between:
                        between(q)

            def steps(n):
                for _ in range(n):
                    step()

            def takes(b, dsts):
                act.wait_ge(s_used, c.n["h"])
                act.wait_ge(s_evac, b)
                for n, dst in enumerate(dsts):
                    nc.scalar.activation(dst, PS[(b + n) % 4][:, 0:T], ACT.Copy).then_inc(s_evac, 1)

            def squares(n, g):
                if 4 * n + g >= 2:
                    act.wait_ge(s_ssq, 4 * n + g - 1)
                nc.scalar.activation(sq[:, g % 2, :, :], x[:, 4 * g:4 * g + 4, :], ACT.Square).then_inc(s_sq, 1)

            def early_squares(n, i, first, every, ready):
                g, r = divmod(i - first, every)
                if r == 0 and 0 <= g < 3:
                    ready(g)
                    squares(n, g)

            def root_table():
                nc.scalar.activation(small[:, 36:37], col("eps"), ACT.Sqrt)

            def norm(n, shift=None):
                act.wait_ge(s_ssq, 4 * n + 4)
                nc.scalar.activation(rstd[:, :], PS[4][:, 0:T], ACT.Sqrt, scale=1.0 / DM, bias=col("eps")).then_inc(s_rms, 1)
                if n != N_FINAL:
                    for k in range(KB):
                        act.wait_ge(s_yn, KB * n + k + 1)
                        if shift is None:
                            m = nc.scalar.activation(xs[:, k, 0, :], yn[:, k % 4, :], ACT.Copy)
                        else:
                            m = nc.scalar.activation(xs[:, k, 0, :], yn[:, k % 4, :], ACT.Identity, bias=shift[:, k:k + 1])
                        m.then_inc(s_yh, 1)

            def his(phase, srcs, k0=0):
                act.wait_ge(s_used, 2 * FIRST[phase][0])
                for k, s in enumerate(srcs):
                    nc.scalar.activation(xs[:, k0 + k, 0, :], s, ACT.Copy).then_inc(s_yh, 1)

            def head_norm(m, s0, i):
                if 0 <= i < 3:
                    for j in (2 * i, 2 * i + 1):
                        if j >= 2:
                            act.wait_ge(s_hss, 6 * m + j - 1)
                        nc.scalar.activation(hsq[:, j % 2, :], sec[:, s0 + 2 * j:s0 + 2 * j + 2, :]
                                             .rearrange("p a t -> p (a t)"), ACT.Square).then_inc(s_hsq, 1)
                if i == 3:
                    act.wait_ge(s_hss, 6 * m + 6)
                    nc.scalar.activation(hrs[:, :], PS[6][0:2 * B_H, 0:T], ACT.Sqrt, scale=1.0 / HD,
                                         bias=col("eps")[0:2 * B_H, :]).then_inc(s_hrms, 1)

            def v_copy(n, g):
                act.wait_ge(s_vT, n + g + 1)
                nc.scalar.activation(vt[:, :, 2 * g * P:(2 * g + 2) * P],
                                     PS[6 + g % 2][:, :].rearrange("p (t c) -> p t c", t=2), ACT.Copy).then_inc(s_vt, 1)

            def job_step(j0, make, n, j):
                if 0 <= j - 3 < n:
                    d, J = make(j - 3), j0 + j - 3
                    act.wait_ge(s_pv, J + 1)
                    nc.scalar.activation(d["out"], PS[7][d["rows"], 0:T], ACT.Copy).then_inc(s_oe, 1)
                if 0 <= j - 2 < n:
                    J = j0 + j - 2
                    act.wait_ge(s_tr, J + 1)
                    if J >= 2:
                        act.wait_ge(s_pv, J - 1)
                    nc.scalar.activation(probT[:, J % 2, :], PS[6][:, 0:3 * P], ACT.Copy).then_inc(s_pt, 1)
                if j < n:
                    d, J = make(j), j0 + j
                    act.wait_ge(s_nm, J + 1)
                    for t in range(2):
                        p, top = prob[:, J % 3, part(t)], stat(J, 0)[:, t:t + 1]
                        m = nc.scalar.activation(p, p, ACT.Exp, bias=top, accum_out=stat(J, 1)[:, t:t + 1])
                        if d["sink"] is not None:
                            m = nc.scalar.activation(stat(J, 2)[:, t:t + 1], d["sink"], ACT.Exp, bias=top)
                    m.then_inc(s_ex, 1)

            for g in range(4):
                act.wait_ge(s_x[g], 16)
                squares(N_ATTN, g)
            act.wait_ge(s_par, 64)
            for h in range(LOOK):
                rnd(h)
            norm(N_ATTN)
            act.wait_ge(s_c, 16)
            nc.scalar.activation(cexp[:, :], crow[:, :], ACT.Exp, scale=-1.0).then_inc(s_cact, 1)

            def copy_c(i):
                if i in C_AT:
                    g = C_AT.index(i)
                    act.wait_ge(s_cps, g + 1)
                    nc.scalar.activation(cb[:, 512 * g:512 * (g + 1)], PS[5 + g % 3][:, :], ACT.Copy).then_inc(s_cb, 1)

            for u in range(U_A):
                step(between=lambda q: copy_c(2 * u + q))

            q4, f4, g4 = (sec[:, S1 + o:S1 + o + 4, :] for o in (0, 4, 12))

            def hgrn(i):
                k, r = divmod(i - LV0, 3)
                if i == 0:
                    act.wait_ge(s_evac, FIRST["B"][1])
                    nc.scalar.activation(kq[:, :, :], f4, ACT.Exp, scale=-1.0).then_inc(s_ha, 1)
                    act.wait_ge(s_hv, HV["lb_d"])
                    nc.scalar.activation(small[:, 20:24], small[:, 16:20], ACT.Exp).then_inc(s_ha, 1)
                if i == 2:
                    act.wait_ge(s_hp, HP["vT"])
                    for t in range(2):
                        m = nc.scalar.activation(vtok[:, t, :], PS[6 + t][:, :], ACT.Copy)
                    m.then_inc(s_ha, 1)
                if i == 5:
                    act.wait_ge(s_hv, HV["ln_in"])
                    nc.scalar.activation(f4, f4, ACT.Ln)
                    nc.scalar.activation(kq[:, :, :], kq[:, :, :], ACT.Ln, scale=1.0 / LN_SPLIT).then_inc(s_ha, 1)
                if i == 7:
                    act.wait_ge(s_hv, HV["w_free_q"])
                    nc.scalar.activation(kq[:, :, :], q4, ACT.Sigmoid).then_inc(s_ha, 1)
                if i == 9:
                    act.wait_ge(s_hv, HV["w_free_g"])
                    nc.scalar.activation(kq[:, :, :], g4, ACT.Sigmoid).then_inc(s_ha, 1)
                if r == 1 and 0 <= k < len(LEVELS):
                    act.wait_ge(s_hv, HV[f"dec{LEVELS[k]}"])
                    nc.scalar.activation(kq[:, :, :], kq[:, :, :], ACT.Exp).then_inc(s_ha, 1)
                if i == LV0 + 3 * len(LEVELS):
                    act.wait_ge(s_hp, HP["lvl128"])
                    nc.scalar.activation(at01[:, :], PS[4][:, :], ACT.Copy).then_inc(s_ha, 1)
                if i == LV0 + 3 * len(LEVELS) + 1:
                    act.wait_ge(s_hp, HP["o"])
                    for g in range(2):
                        m = nc.scalar.activation(kq[:, 2 * g:2 * g + 2, :].rearrange("p a t -> p (a t)"),
                                                 PS[6 + g][:, :], ACT.Square)
                    m.then_inc(s_ha, 1)
                if i == LV0 + 3 * len(LEVELS) + 2:
                    act.wait_ge(s_hp, HP["var"])
                    nc.scalar.activation(kk[0:A_H, 0, :], PS[4][0:A_H, 0:T], ACT.Sqrt, scale=1.0 / HD,
                                         bias=col("eps")[0:A_H, :]).then_inc(s_ha, 1)

            for u in range(U_B):
                step(between=lambda q: hgrn(2 * u + q))

            def fox(i):
                if i == 0:
                    act.wait_ge(s_hv, HV["done"])
                    act.wait_ge(s_evac, FIRST["C"][1])
                head_norm(0, S0, i)
                if 0 <= i - FOX_V < B_H // 2:
                    v_copy(0, i - FOX_V)
                if i == FOX_V + 1:
                    act.wait_ge(s_fv, 1)
                    nc.scalar.activation(gtmp[:, :], sec[0:B_H, S0 + 18, :], ACT.Abs).then_inc(s_fa, 1)
                    act.wait_ge(s_fa, 1)
                    nc.scalar.activation(gtmp[:, :], gtmp[:, :], ACT.Exp, scale=-1.0).then_inc(s_fa, 1)
                if i == FOX_V + 3:
                    act.wait_ge(s_fv, 2)
                    nc.scalar.activation(gtmp[:, :], gtmp[:, :], ACT.Ln).then_inc(s_fa, 1)
                for j in fox_steps(i):
                    job_step(J_FOX, fox_job, B_H, j)
                if i == MOBA_N:
                    act.wait_ge(s_oe, J_MOBA)
                    act.wait_ge(s_evac, FIRST["C"][1] + 2 * C_H)
                head_norm(1, S1, i - MOBA_N)

            for u in range(U_C):
                step(between=lambda q: fox(2 * u + q))

            def moba(i):
                if i == 0:
                    for g in range(C_H // 2):
                        v_copy(3, g)
                for j in moba_steps(i):
                    job_step(J_MOBA, moba_job, C_H, j)

            def eights(phase, first_done, jobs_done, between, n):
                act.wait_ge(s_oe, first_done)
                his(phase, [mix[:, k, :] for k in range(8)])
                for u in range(U_OUT):
                    step(between=lambda q: between(2 * u + q))
                act.wait_ge(s_oe, jobs_done)
                his(phase, [mix[:, k, :] for k in range(8, KB)], 8)
                b = FIRST[phase][1] + KB
                for u in range(U_OUT):
                    step(between=lambda q: early_squares(n, 2 * u + q, SQ_EIGHT, 4,
                                                         lambda g: act.wait_ge(s_evac, b + 4 * g + 4)))
                root_table()
                act.wait_ge(s_evac, b + KB)
                squares(n, 3)

            eights("out", J_MOBA, J_SWA, moba, N_FFN)
            act.wait_ge(s_xs, XS["mix"] + 16)
            act.dma_start(mix[:, 0:2, :], a["p"]).then_inc(s_p, 16)
            norm(N_FFN)

            def gelu(j):
                c.n["g"] += 1
                act.wait_ge(s_conv, c.val("g", c.n["g"]))
                nc.scalar.activation(gel[:, j, :], cv[:, j % 2, :], ACT.Gelu_apprx_tanh).then_inc(s_gel, 1)

            def h_hi(buf, j):
                c.n["y"] += 1
                act.wait_ge(s_hy, c.val("y", c.n["y"]))
                nc.scalar.activation(hs[:, buf, j, 0, :], yf[:, (c.n["y"] - 1) % 2, :], ACT.Copy).then_inc(s_hh, 1)

            def gates(n=CH, first=None):
                for j in range(n):
                    step((lambda: gelu(j - 1)) if j else first)

            def ups(buf, n=CH, first=None):
                for j in range(n):
                    step((lambda: h_hi(buf, j - 1)) if j else first)

            def downs(first, n=KB // 2):
                step(first)
                steps(n - 1)

            gates()
            ups(0, first=lambda: gelu(CH - 1))
            c.loop(NC1 - 1, lambda: (gates(first=lambda: h_hi(0, CH - 1)), downs(lambda: gelu(CH - 1)), ups(0)),
                   h=6 * CH, g=CH, y=CH)
            gates(CH_LAST, lambda: h_hi(0, CH - 1))
            downs(lambda: gelu(CH_LAST - 1))
            ups(0, CH_LAST)
            for u in range(KB // 4):
                step(None if u else (lambda: h_hi(0, CH_LAST - 1)),
                     lambda q: early_squares(N_PLE, 2 * u + q, SQ_QUAD, 2,
                                             lambda g: act.wait_ge(s_evac, FIRST["plep"][1] - KB + 4 * g + 4)))

            act.wait_ge(s_p, 16)
            his("plep", [mix[:, k, :] for k in range(2)])
            for n in range(2 * U_PLEP):
                rnd(c.n["h"] + LOOK)
                if n:
                    takes(FIRST["plep"][1] + 4 * (n - 1), [mix[:, 4 * (n - 1) + q, :] for q in range(4)])
                c.n["h"] += 1
            takes(FIRST["plep"][1] + 12, [mix[:, 12 + q, :] for q in range(4)])
            act.wait_ge(s_used, 2 * FIRST["pleg"][0])
            root_table()
            act.wait_ge(s_evac, FIRST["plep"][1])
            squares(N_PLE, 3)
            norm(N_PLE)

            def sigmoid(j):
                act.wait_ge(s_evac, FIRST["pleg"][1] + j + 1)
                nc.scalar.activation(yf[:, j % 2, :], yf[:, j % 2, :], ACT.Sigmoid).then_inc(s_ps, 1)
            for j in range(U_PLEG):
                step((lambda: sigmoid(j - 1)) if j else None,
                     lambda q: early_squares(N_ATTN2, 2 * j + q, SQ_PLE, 8, lambda g: act.wait_ge(s_pled, 4 * g + 4)))
            sigmoid(U_PLEG - 1)
            root_table()
            act.wait_ge(s_pled, KB)
            squares(N_ATTN2, 3)
            act.wait_ge(s_mod, 1)
            norm(N_ATTN2, mod[:, 0:KB])

            def swa(i):
                if i in REL_G:
                    g = REL_G.index(i)
                    act.wait_ge(s_rp, g + 1)
                    if g:
                        act.wait_ge(s_rw, 16 * g)
                    for q in range(4):
                        m = nc.scalar.activation(rrow[:, q, :], PS[4 + q][:, 0:384], ACT.Copy)
                    m.then_inc(s_rr, 1)
                if i == LAT:
                    act.wait_ge(s_evac, FIRST["in2"][1] + CKV + 1)
                    nc.scalar.activation(hsq4[:, :, :], sec[:, CQ:CQ + 4, :], ACT.Square).then_inc(s_hsq, 1)
                if i == LAT + 1:
                    act.wait_ge(s_rw, 64)
                    act.wait_ge(s_vT, 7)
                    nc.scalar.activation(vt[:, 0, 0:T], PS[7][:, 0:T], ACT.Copy).then_inc(s_vt, 1)
                    for j in range(2):
                        act.wait_ge(s_hss, 12 + j + 1)
                        nc.scalar.activation(hvr[:, j, :], PS[4 + j][:, 0:T], ACT.Sqrt, scale=1.0 / (MLA_QR, MLA_KVR)[j],
                                             bias=col("eps")).then_inc(s_hrms, 1)
                for j in swa_steps(i):
                    if j == 0:
                        act.wait_ge(s_qk, 2)
                    job_step(J_SWA, swa_job, SWA_H, j)

            for u in range(U_IN2):
                step(between=lambda q: swa(2 * u + q))
            his("uq", [sec[:, CQ + k, :] for k in range(4)])
            b = FIRST["uq"][1]
            for n in range(len(LATENT_DST)):
                rnd(c.n["h"] + LOOK)
                if n:
                    takes(b, LATENT_DST[n - 1])
                    b += len(LATENT_DST[n - 1])
                swa(2 * U_IN2 + n)
                c.n["h"] += 1
            takes(b, LATENT_DST[-1])

            def mla(i):
                if i < MLA_H // 2:
                    v_copy(7, i)
                for j in mla_steps(i):
                    job_step(J_MLA, mla_job, MLA_H, j)

            eights("out2", J_MLA, J_END, mla, N_MLP2)
            norm(N_MLP2, mod[:, 3 * KB:4 * KB])

            ups(0)
            ups(1, first=lambda: h_hi(0, CH - 1))
            c.loop(NC2 // 2 - 1, lambda: (downs(lambda: h_hi(1, CH - 1)), ups(0), downs(lambda: h_hi(0, CH - 1)), ups(1)),
                   h=8 * CH, y=2 * CH)
            downs(lambda: h_hi(1, CH - 1))
            for u in range(KB // 2):
                step(between=lambda q: early_squares(N_FINAL, 2 * u + q, SQ_EIGHT, 4,
                                                     lambda g: act.wait_ge(s_evac, FIRST["end"][1] - KB + 4 * g + 4)))
            root_table()
            act.wait_ge(s_evac, FIRST["end"][1])
            squares(N_FINAL, 3)
            norm(N_FINAL)

        @block.vector
        def _(dve):
            c = Counts(dve, h=0, b=0, c=0, m=0, g=0, y=0, l=0)

            def link(*ins):
                for i in ins:
                    i.then_inc(s_dch, 1)
                c.n["c"] += len(ins)
                dve.wait_ge(s_dch, c.val("c", c.n["c"]))

            def sub(h):
                if h < 2 * UNITS:
                    dve.wait_ge(s_round, c.val("h", h + 1))
                    nc.vector.tensor_tensor(wl[:, h % HS, :], raw[:, (h // 2) % RAW, (h % 2) * 1024:(h % 2 + 1) * 1024],
                                            wh[:, h % HS, :].bitcast(F32), ALU.subtract).then_inc(s_split, 1)

            def half(before=None, after=None):
                if before:
                    dve.wait_ge(s_used, c.val("h", c.n["h"]))
                    before()
                sub(c.n["h"] + LOOK)
                if after:
                    after()
                c.n["h"] += 1

            def tail(before):
                dve.wait_ge(s_used, c.val("h", c.n["h"]))
                before()

            def bank():
                c.n["b"] += 1
                return PS[(c.n["b"] - 1) % 4]

            def take(dst):
                nc.vector.tensor_reduce(dst, bank()[:, :].rearrange("p (a t) -> p t a", a=2), AX.X, ALU.add
                                        ).then_inc(s_evac, 1)

            def add_blocks(ks, gate=None):
                bs = [bank() for _ in ks]
                for q in range(2):
                    ins = []
                    for k, b in zip(ks, bs):
                        if gate is None:
                            ins.append(nc.vector.tensor_tensor(x[:, k, :], b[:, q * T:(q + 1) * T], x[:, k, :], ALU.add))
                        else:
                            ins.append(nc.vector.scalar_tensor_tensor(x[:, k, :], b[:, q * T:(q + 1) * T],
                                                                      gate[:, k:k + 1], x[:, k, :], ALU.mult, ALU.add))
                    if q == 0:
                        link(*ins)
                    else:
                        for i in ins:
                            i.then_inc(s_evac, 1)

            def mods(n, where=None):
                dst = modp if where is None else modt
                for j in range(n):
                    m = c.n["m"]
                    v = 16 * (m // 2 + 1)
                    dve.wait_ge(s_modl[m % 2], v + c.i * (8 * c.per["m"]) if c.per else v)
                    o = m if where is None else where + j
                    nc.vector.tensor_tensor_reduce(out=modraw[:, m % 2, :], in0=modraw[:, m % 2, :],
                                                   in1=cb[:, (m % 2) * 1024:(m % 2 + 1) * 1024],
                                                   scale=1.0, scalar=0.0, op0=ALU.mult, op1=ALU.add,
                                                   accum_out=dst[:, o:o + 1]).then_inc(s_modu, 1)
                    c.n["m"] += 1

            def fulls(n, ev, nmod=lambda j: 0, between=lambda i: None):
                for j in range(n):
                    half((lambda: ev(j - 1)) if j else None, after=lambda: between(2 * j))
                    half(after=lambda: (between(2 * j + 1), mods(nmod(j))))
                tail(lambda: ev(n - 1))

            def eights(name, jobs_done, between, gate=None, nmod=0):
                for part in range(2):
                    if part:
                        dve.wait_ge(s_oe, jobs_done)
                    for k in range(8 * part, 8 * part + 8):
                        lo(XS[name], k, mix[:, k, :])
                    for i in range(2 * U_OUT):
                        half((lambda: add_blocks([i - 1], gate)) if i else None,
                             after=lambda: (mods(nmod * (i % 2)) if part else between(i)))
                    tail(lambda: add_blocks([KB - 1], gate))

            def lo(x0, k, src, shift=None):
                dve.wait_ge(s_yh, x0 + k + 1)
                if shift is not None:
                    nc.vector.scalar_tensor_tensor(xs[:, k, 1, :], src, shift[:, k:k + 1], xs[:, k, 0, :].bitcast(F32),
                                                   ALU.add, ALU.subtract).then_inc(s_xs, 1)
                    return
                nc.vector.tensor_tensor(xs[:, k, 1, :], src, xs[:, k, 0, :].bitcast(F32), ALU.subtract).then_inc(s_xs, 1)

            def norm(n, gain, shift=None):
                dve.wait_ge(s_rms, n + 1)
                link(nc.vector.reciprocal(rstd[:, :], rstd[:, :]))
                for k in range(KB + 2):
                    if k < KB and n == N_FINAL:
                        nc.vector.scalar_tensor_tensor(mix[:, k, :], x[:, k, :], gain[:, k:k + 1], rstd[:, :],
                                                       ALU.mult, ALU.mult).then_inc(s_fin, 1)
                    elif k < KB:
                        if k >= 4:
                            dve.wait_ge(s_xs, XS[GAIN_XS[n]] + k - 3)
                        y = nc.vector.scalar_tensor_tensor(yn[:, k % 4, :], x[:, k, :], gain[:, k:k + 1], rstd[:, :],
                                                           ALU.mult, ALU.mult)
                        y.then_inc(s_yn, 1)
                    if k >= 2 and n != N_FINAL:
                        lo(XS[GAIN_XS[n]], k - 2, yn[:, (k - 2) % 4, :], shift)

            def head_norm(m, s0, gq, gk, i):
                if i == 3:
                    dve.wait_ge(s_hrms, m + 1)
                    nc.vector.reciprocal(hrs[:, :], hrs[:, :]).then_inc(s_hr, 1)
                if 5 <= i < 8:
                    for j in (2 * i - 10, 2 * i - 9):
                        dve.wait_ge(s_hb, 6 * m + j + 1)
                        b = sec[:, s0 + 2 * j:s0 + 2 * j + 2, :].rearrange("p a t -> p (a t)")
                        nc.vector.scalar_tensor_tensor(b, b, gq if j < 3 else gk, PS[4 + j % 2][:, :], ALU.mult, ALU.mult
                                                       ).then_inc(s_hn, 1)

            def job_step(j0, make, n, j):
                if j < n:
                    d, J = make(j), j0 + j
                    dve.wait_ge(s_sc, J + 1)
                    if J >= 3:
                        dve.wait_ge(s_tr, J - 2)
                    for t in range(2):
                        s, b = PS[4 + J % 2][:, part(t)], d["bias"][:, T - keys(t):T]
                        if d["slope"] is None:
                            m = nc.vector.scalar_tensor_tensor(prob[:, J % 3, part(t)], s, d["scale"], b, ALU.mult, ALU.add)
                        else:
                            m = nc.vector.scalar_tensor_tensor(prob[:, J % 3, part(t)], b, d["slope"], s, ALU.mult, ALU.add)
                    m.then_inc(s_lg, 1)
                    dve.wait_ge(s_lg, J + 1)
                    link(*[nc.vector.tensor_reduce(stat(J, 3)[:, t:t + 1], prob[:, J % 3, part(t)], AX.X, ALU.max)
                           for t in range(2)])
                    if d["sink"] is None:
                        m = nc.vector.tensor_scalar(stat(J, 0), stat(J, 3), -1.0, None, ALU.mult)
                    else:
                        m = nc.vector.tensor_scalar(stat(J, 0), stat(J, 3), d["sink"], -1.0, ALU.max, ALU.mult)
                    m.then_inc(s_nm, 1)
                if 0 < j <= n:
                    d, J = make(j - 1), j0 + j - 1
                    dve.wait_ge(s_ex, J + 1)
                    if d["sink"] is not None:
                        link(nc.vector.tensor_tensor(stat(J, 1), stat(J, 1), stat(J, 2), ALU.add))
                    link(nc.vector.reciprocal(stat(J, 1), stat(J, 1)))
                    for t in range(2):
                        p = prob[:, J % 3, part(t)]
                        m = nc.vector.tensor_scalar(p, p, stat(J, 1)[:, t:t + 1], None, ALU.mult)
                    m.then_inc(s_pr, 1)

            nc.vector.memset(ones[:, :], 1.0).then_inc(s_ones, 1)
            link(nc.vector.memset(strip, 0.0))
            nc.vector.memset(into(0, 1), 1.0).then_inc(s_ones, 1)
            dve.wait_ge(s_ones, 2)
            dve.wait_ge(s_par, 64)
            for g in range(4):
                dve.wait_ge(s_x[g], 16)
            for h in range(LOOK):
                sub(h)
            norm(N_ATTN, cols("attn"))
            dve.wait_ge(s_cact, 1)
            link(nc.vector.tensor_scalar(cexp[:, :], cexp[:, :], 1.0, None, ALU.add))
            link(nc.vector.reciprocal(cexp[:, :], cexp[:, :]))
            nc.vector.tensor_tensor(crow[:, :], crow[:, :], cexp[:, :], ALU.mult).then_inc(s_crow, 1)

            def first_mod(i):
                if i == 2 * MOD_UNIT:
                    dve.wait_ge(s_cb, 4)

            fulls(U_A, lambda j: take(sec[:, S1 + j, :]), lambda j: 2 - j % 2 if j >= MOD_UNIT else 0, first_mod)

            q4, f4, i4, g4 = (sec[:, S1 + o:S1 + o + 4, :] for o in (0, 4, 8, 12))
            lbd, lbe, lbs, lbc, oml = (small[:, o:o + 4] for o in (16, 20, 24, 28, 32))

            def decays(k):
                lv, prev = LEVELS[k], ([0] + LEVELS)[k]
                b = i4 if lv == 128 else f4
                n = A_H * T // (2 * lv)
                end = left(b, lv)[:, :, lv - 1:lv].to_broadcast([P, n, lv])
                dve.wait_ge(s_hp, HP[f"lvl{prev}"])
                if lv < 64:
                    nc.vector.tensor_tensor(right(kq[:, :, :], lv), right(b, lv), end, ALU.subtract)
                else:
                    nc.vector.tensor_copy(right(kq[:, :, :], lv), right(b, lv))
                nc.vector.tensor_tensor(left(kq[:, :, :], lv), end, left(b, lv), ALU.subtract).then_inc(s_hv, 1)
                mask = hmask[:, 0 if prev == 0 else 1 + LVL.index(prev), :].unsqueeze(1).to_broadcast([P, A_H, P])
                for t in range(2):
                    ps = PS[4 + t][:, :].rearrange("p (h s) -> p h s", h=A_H)
                    dst = atd[:, t, :].rearrange("p (h s) -> p h s", h=A_H)
                    if prev == 0:
                        m = nc.vector.tensor_tensor(dst, ps, mask, ALU.mult)
                    else:
                        m = nc.vector.copy_predicated(dst, mask.bitcast(mybir.dt.uint32), ps)
                link(m)

            def left(v, m):
                return v.rearrange("p h (n a m) -> p (h n) a m", a=2, m=m)[:, :, 0, :]

            def right(v, m):
                return v.rearrange("p h (n a m) -> p (h n) a m", a=2, m=m)[:, :, 1, :]

            mixf = mix[:, 0:4, :].rearrange("p h t -> p (h t)")

            def hgrn(i):
                k, r = divmod(i - LV0, 3)
                if i == 0:
                    nc.vector.tensor_tensor(lbd, cols("lb"), cols("lb"), ALU.subtract).then_inc(s_hv, 1)
                    dve.wait_ge(s_ha, HA["lb_exp"])
                    link(nc.vector.reciprocal(lbs, lbe))
                    link(nc.vector.tensor_tensor(lbs, lbs, lbe, ALU.mult))
                    link(nc.vector.tensor_tensor(lbc, lbs, lbs, ALU.subtract))
                    link(nc.vector.tensor_scalar(oml, lbc, -1.0, 1.0, ALU.mult, ALU.add))
                    link(nc.vector.tensor_scalar(kk[:, :, :], kq[:, :, :], 1.0 / TINY, None, ALU.min))
                    link(nc.vector.tensor_scalar(kq[:, :, :], kk[:, :, :], 1.0, None, ALU.add))
                if i in (1, 2):
                    half = kq[:, 2 * i - 2:2 * i, :]
                    link(nc.vector.reciprocal(half, half))
                if i == 3:
                    link(*[nc.vector.scalar_tensor_tensor(kk[:, h, :], kk[:, h, :], oml[:, h:h + 1], kq[:, h, :],
                                                          ALU.mult, ALU.mult) for h in range(A_H)])
                    link(*[nc.vector.tensor_scalar(kq[:, h, :], kq[:, h, :], oml[:, h:h + 1], lbc[:, h:h + 1],
                                                   ALU.mult, ALU.add) for h in range(A_H)])
                if i == 4:
                    nc.vector.tensor_scalar(f4, kq[:, :, :], LN_SPLIT, None, ALU.max)
                    nc.vector.tensor_scalar(kq[:, :, :], kq[:, :, :], TINY, LN_SPLIT, ALU.max, ALU.min).then_inc(s_hv, 1)
                if i == 6:
                    dve.wait_ge(s_ha, HA["ln"])
                    nc.vector.tensor_tensor(f4, f4, kq[:, :, :], ALU.add).then_inc(s_hv, 1)
                    dve.wait_ge(s_hv, HV["w_free_q"])
                    dve.wait_ge(s_hp, HP["vT"])
                    for h in range(A_H):
                        for t in range(2):
                            m = nc.vector.tensor_tensor_scan(i4[:, h, qt(t)], ones[:, :], f4[:, h, qt(t)], 0.0,
                                                             ALU.mult, ALU.add)
                    link(m)
                if i == 7:
                    for h in range(A_H):
                        for t in range(4):
                            s = slice(64 * t, 64 * t + 64)
                            m = nc.vector.tensor_tensor_scan(f4[:, h, s], ones[:, 0:64], f4[:, h, s], 0.0,
                                                             ALU.mult, ALU.add)
                    link(m)
                if i in (8, 9):
                    name, v = ("q", q4) if i == 8 else ("g", g4)
                    dve.wait_ge(s_ha, HA["sig_" + name])
                    nc.vector.tensor_tensor(v, v, kq[:, :, :], ALU.mult).then_inc(s_hv, 1)
                    dve.wait_ge(s_hv, HV["w_free_g" if i == 8 else "silu_g"])
                if r == 0 and 0 <= k < len(LEVELS):
                    if k == 0:
                        dve.wait_ge(s_hm, 16)
                    decays(k)
                if r == 1 and 0 <= k < len(LEVELS):
                    lv = LEVELS[k]
                    dve.wait_ge(s_ha, HA[f"exp{lv}"])
                    nc.vector.tensor_tensor(left(kq[:, :, :], lv), left(kq[:, :, :], lv), left(kk[:, :, :], lv), ALU.mult)
                    nc.vector.tensor_tensor(right(kq[:, :, :], lv), right(kq[:, :, :], lv), right(q4, lv),
                                            ALU.mult).then_inc(s_hv, 1)
                if i == LV0 + 3 * len(LEVELS) + 2:
                    dve.wait_ge(s_ha, HA["rms"])
                    nc.vector.reciprocal(kk[0:A_H, 0, :], kk[0:A_H, 0, :]).then_inc(s_hv, 1)
                    link(*[nc.vector.scalar_tensor_tensor(mixf[:, 512 * g:512 * (g + 1)], PS[6 + g][:, :], cols("onorm"),
                                                          g4[:, 2 * g:2 * g + 2, :].rearrange("p h t -> p (h t)"),
                                                          ALU.mult, ALU.mult) for g in range(2)])
                if i == LV0 + 3 * len(LEVELS) + 3:
                    dve.wait_ge(s_hp, HP["rstd"])
                    for g in range(2):
                        m = nc.vector.tensor_tensor(mixf[:, 512 * g:512 * (g + 1)], mixf[:, 512 * g:512 * (g + 1)],
                                                    PS[4 + g][:, :], ALU.mult)
                    m.then_inc(s_hv, 1)

            fulls(U_B, lambda j: take(sec[:, S0 + j, :]), between=hgrn)

            link(nc.vector.tensor_scalar(gsc[:, 0:1], cols("fq"), HD ** -0.5, None, ALU.mult),
                 nc.vector.tensor_scalar(gsc[:, 1:2], cols("mq"), HD ** -0.5, None, ALU.mult))
            z = sec[0:B_H, S0 + 18, :]

            def fox(i):
                head_norm(0, S0, gsc[:, 0:1], cols("fk"), i)
                if i == FOX_V:
                    nc.vector.tensor_scalar(z, z, cols("bf")[0:B_H, :], None, ALU.add).then_inc(s_fv, 1)
                if i == FOX_V + 2:
                    dve.wait_ge(s_fa, 2)
                    link(nc.vector.tensor_scalar(z, z, 0.0, None, ALU.min))
                    nc.vector.tensor_scalar(gtmp[:, :], gtmp[:, :], 1.0, None, ALU.add).then_inc(s_fv, 1)
                if i == FOX_V + 4:
                    dve.wait_ge(s_fa, 3)
                    link(nc.vector.tensor_tensor(z, z, gtmp[:, :], ALU.subtract))
                    link(nc.vector.tensor_tensor_scan(fnp[:, 0, qt(0)], ones[0:B_H, :], z[:, qt(0)], 0.0, ALU.mult, ALU.add))
                    link(nc.vector.tensor_tensor_scan(fnp[:, 0, qt(1)], ones[0:B_H, :], z[:, qt(1)], fnp[:, 0, P - 1:P],
                                                      ALU.mult, ALU.add))
                    nc.vector.tensor_scalar(fnp[:, 1, :], fnp[:, 0, :], -1.0, None, ALU.mult).then_inc(s_qk, 1)
                for j in fox_steps(i):
                    job_step(J_FOX, fox_job, B_H, j)
                head_norm(1, S1, gsc[:, 1:2], cols("mk"), i - MOBA_N)

            fulls(U_C, lambda j: take(sec[:, S1 + j, :]), lambda j: 1 + (6 <= j < 14), fox)

            def moba(i):
                for j in moba_steps(i):
                    job_step(J_MOBA, moba_job, C_H, j)

            dve.wait_ge(s_oe, J_MOBA)
            eights("mix", J_SWA, moba, nmod=1)
            norm(N_FFN, cols("ffn"))

            def conv(j):
                q = j % 2
                if c.n["g"] >= 2:
                    dve.wait_ge(s_conv, c.val("g", c.n["g"] - 1))
                take(hg[:, q, 2:T + 2])
                w = lambda i: cvp[:, 4 * j + i:4 * j + i + 1]
                dve.wait_ge(s_evac, c.val("b", c.n["b"]))
                if c.n["g"] >= 2:
                    dve.wait_ge(s_gel, c.val("g", c.n["g"] - 1))
                link(nc.vector.tensor_scalar(cv[:, q, :], hg[:, q, 2:T + 2], w(2), w(3), ALU.mult, ALU.add))
                link(nc.vector.scalar_tensor_tensor(cv[:, q, :], hg[:, q, 1:T + 1], w(1), cv[:, q, :], ALU.mult, ALU.add))
                nc.vector.scalar_tensor_tensor(cv[:, q, :], hg[:, q, 0:T], w(0), cv[:, q, :], ALU.mult, ALU.add).then_inc(s_conv, 1)
                c.n["g"] += 1

            def product(j):
                y = c.n["y"]
                if y >= 2:
                    dve.wait_ge(s_hy, c.val("y", y - 1))
                take(up[:, j % 2, :])
                dve.wait_ge(s_evac, c.val("b", c.n["b"]))
                dve.wait_ge(s_gel, c.val("y", y + 1))
                if y >= 2:
                    dve.wait_ge(s_h, c.val("y", y - 1))
                nc.vector.tensor_tensor(yf[:, y % 2, :], up[:, j % 2, :], gel[:, j, :], ALU.mult).then_inc(s_hy, 1)
                c.n["y"] += 1

            def h_lo(buf, j):
                l = c.n["l"]
                dve.wait_ge(s_hh, c.val("l", l + 1))
                nc.vector.tensor_tensor(hs[:, buf, j, 1, :], yf[:, l % 2, :], hs[:, buf, j, 0, :].bitcast(F32),
                                        ALU.subtract).then_inc(s_h, 1)
                c.n["l"] += 1

            def units(n, ev, first=None, lo_first=None, h_lo_of=None, nmod=0, m0=None):
                for j in range(n):
                    half((lambda: ev(j - 1)) if j else first,
                         after=(lambda: h_lo_of(j - 1)) if j and h_lo_of else (lo_first if j == 0 else None))
                    half(after=(lambda: mods(nmod, m0 if m0 is None else m0 + j * nmod)) if nmod else None)

            def downs(first, lo_first=None, gate=None, nmod=0, m0=None):
                for i in range(KB):
                    half((lambda: add_blocks([i - 1], gate)) if i else first,
                         after=lo_first if i == 0 else
                         ((lambda: mods(nmod, m0 if m0 is None else m0 + (i // 2) * nmod)) if nmod and i % 2 else None))

            def last_down(gate=None):
                return lambda: add_blocks([KB - 1], gate)

            def load_taps(n, blocks=CH, dyn=False):
                o = COLS["conv"][0] + 4 * CH * n
                src = par[:, bass.ds(c.i * (4 * CH) + o, 4 * CH)] if dyn else par[:, o:o + 4 * blocks]
                link(nc.vector.tensor_copy(cvp[:, 0:4 * blocks], src))

            link(nc.vector.memset(hg[:, :, 0:2], 0.0))
            load_taps(0)
            units(CH, conv, nmod=1)
            units(CH, product, first=lambda: conv(CH - 1), h_lo_of=lambda j: h_lo(0, j), nmod=1)

            def ffn1_body():
                units(CH, conv, first=lambda: product(CH - 1), lo_first=lambda: (h_lo(0, CH - 1), load_taps(1, dyn=True)),
                      nmod=1, m0=0)
                downs(lambda: conv(CH - 1), nmod=1, m0=CH)
                units(CH, product, first=last_down(), h_lo_of=lambda j: h_lo(0, j), nmod=1, m0=2 * CH)
                dve.wait_ge(s_modu, c.val("m", c.n["m"]))
                link(nc.vector.tensor_copy(modp[:, bass.ds(c.i * MODS + M0, MODS)], modt[:, 0:MODS]))
            MODS, M0 = 3 * CH, c.n["m"]
            c.loop(NC1 - 1, ffn1_body, h=6 * CH, b=2 * CH + KB, c=KB + 2 * CH + 2, m=MODS, g=CH, y=CH, l=CH)
            units(CH_LAST, conv, first=lambda: product(CH - 1),
                  lo_first=lambda: (h_lo(0, CH - 1), load_taps(NC1, CH_LAST)), nmod=1)
            downs(lambda: conv(CH_LAST - 1), nmod=1)
            units(CH_LAST, product, first=last_down(), h_lo_of=lambda j: h_lo(0, j), nmod=1)
            for j in range(KB // 4):
                half((lambda: add_blocks([4 * j - 2, 4 * j - 1])) if j else (lambda: product(CH_LAST - 1)),
                     after=None if j else (lambda: h_lo(0, CH_LAST - 1)))
                half(lambda: add_blocks([4 * j, 4 * j + 1]))
            tail(lambda: add_blocks([KB - 2, KB - 1]))

            for k in range(2):
                lo(XS["p"], k, mix[:, k, :])
            for n in range(2 * U_PLEP):
                half()
                c.n["b"] += 4
            dve.wait_ge(s_evac, FIRST["pleg"][1])
            norm(N_PLE, cols("ple"))

            def ple_in(j):
                take(yf[:, j % 2, :])

            def ple_add(j):
                dve.wait_ge(s_ps, j + 1)
                link(nc.vector.tensor_tensor(up[:, 1, :], yf[:, j % 2, :], mix[:, j, :], ALU.mult))
                nc.vector.tensor_tensor(x[:, j, :], x[:, j, :], up[:, 1, :], ALU.add).then_inc(s_pled, 1)

            rest = NMOD - c.n["m"]
            for j in range(U_PLEG):
                half((lambda: ple_in(j - 1)) if j else None, after=lambda: mods(rest * (j + 1) // U_PLEG - rest * j // U_PLEG))
                half(after=(lambda: ple_add(j - 1)) if j else None)
            tail(lambda: ple_in(U_PLEG - 1))
            ple_add(U_PLEG - 1)
            parts = modp[:, :].rearrange("p (n a) -> p n a", a=2)
            link(nc.vector.tensor_tensor(mod[:, :], parts[:, :, 0], parts[:, :, 1], ALU.add))
            link(nc.vector.tensor_tensor(mod[:, :], mod[:, :], cols("bmod"), ALU.add))
            SH1, SC1, G1, SH2, SC2, G2 = (mod[:, KB * i:KB * (i + 1)] for i in range(6))
            link(nc.vector.tensor_scalar(gmod[:, 0:KB], SC1, 1.0, None, ALU.add),
                 nc.vector.tensor_scalar(gmod[:, KB:2 * KB], SC2, 1.0, None, ALU.add))
            link(nc.vector.tensor_tensor(gmod[:, 0:KB], gmod[:, 0:KB], cols("attn2"), ALU.mult))
            m = nc.vector.tensor_tensor(gmod[:, KB:2 * KB], gmod[:, KB:2 * KB], cols("mlp2"), ALU.mult)
            m.then_inc(s_mod, 1)
            dve.wait_ge(s_mod, 1)
            norm(N_ATTN2, gmod[:, 0:KB], SH1)

            def swa(i):
                if i == REL_C:
                    dve.wait_ge(s_rl, 32)
                    nc.vector.tensor_copy(relh[:, :, :], relb[:, :].unsqueeze(2).to_broadcast([REL + 1, SWA_H, P])
                                          ).then_inc(s_rh, 1)
                if i == LAT + 2:
                    dve.wait_ge(s_hrms, 4)
                    link(nc.vector.reciprocal(hvr[:, :, :], hvr[:, :, :]))
                if i == LAT + 3:
                    for k in range(4):
                        g = cols("kvn") if k == 3 else cols("qn")[:, k:k + 1]
                        b = sec[:, CQ + k, :]
                        m = nc.vector.scalar_tensor_tensor(b, b, g, hvr[:, k // 3, :], ALU.mult, ALU.mult)
                    m.then_inc(s_qk, 1)
                    dve.wait_ge(s_qk, 2)
                for j in swa_steps(i):
                    if j == 0:
                        dve.wait_ge(s_rb, 16 * SWA_H)
                    job_step(J_SWA, swa_job, SWA_H, j)

            fulls(U_IN2, lambda j: take(sec[:, j, :]), between=swa)
            for k in range(4):
                lo(XS["cq"], k, sec[:, CQ + k, :])
            for n in range(len(LATENT_DST)):
                half(after=lambda: swa(2 * U_IN2 + n))
                c.n["b"] += len(LATENT_DST[n])

            def mla(i):
                if i == 0:
                    dve.wait_ge(s_cs, 32)
                    dve.wait_ge(s_evac, FIRST["out2"][1])
                if i < len(ROPE):
                    dve.wait_ge(s_pm, i + 1)
                    if i:
                        dve.wait_ge(s_kvr, i)
                    b = sec[:, ROPE[i], :]
                    m1 = nc.vector.tensor_tensor(rtmp[:, 0, :], PS[4 + i % 2][:, 0:T], cossin[:, 1, :], ALU.mult)
                    link(m1, nc.vector.tensor_tensor(rtmp[:, 1, :], b, cossin[:, 0, :], ALU.mult))
                    nc.vector.tensor_tensor(b, rtmp[:, 0, :], rtmp[:, 1, :], ALU.add).then_inc(s_kvr, 1)
                for j in mla_steps(i):
                    if j == 0:
                        dve.wait_ge(s_kvr, len(ROPE))
                    job_step(J_MLA, mla_job, MLA_H, j)

            dve.wait_ge(s_oe, J_MLA)
            dve.wait_ge(s_evac, FIRST["out2"][1])
            eights("mix2", J_END, mla, G1)
            norm(N_MLP2, gmod[:, KB:2 * KB], SH2)

            def relu2(j):
                y = c.n["y"]
                dve.wait_ge(s_hy, c.val("y", y - 1))
                take(up[:, j % 2, :])
                dve.wait_ge(s_evac, c.val("b", c.n["b"]))
                dve.wait_ge(s_h, c.val("y", y - 1))
                nc.vector.scalar_tensor_tensor(yf[:, y % 2, :], up[:, j % 2, :], 0.0, up[:, j % 2, :],
                                               ALU.max, ALU.mult).then_inc(s_hy, 1)
                c.n["y"] += 1

            units(CH, relu2, h_lo_of=lambda j: h_lo(0, j))
            units(CH, relu2, first=lambda: relu2(CH - 1), lo_first=lambda: h_lo(0, CH - 1), h_lo_of=lambda j: h_lo(1, j))

            def ffn2_body():
                for q in range(2):
                    downs(lambda: relu2(CH - 1), lo_first=lambda: h_lo(1 - q, CH - 1), gate=G2)
                    units(CH, relu2, first=last_down(G2), h_lo_of=lambda j: h_lo(q, j))
            c.loop(NC2 // 2 - 1, ffn2_body, h=8 * CH, b=2 * (CH + KB), c=2 * KB, y=2 * CH, l=2 * CH)
            downs(lambda: relu2(CH - 1), lo_first=lambda: h_lo(1, CH - 1), gate=G2)
            downs(last_down(G2), gate=G2)
            tail(last_down(G2))
            norm(N_FINAL, cols("final"))


_OUT = "out_0_dram"


def kernel(**inputs):
    import concourse.bacc as bacc
    from concourse.bass_utils import run_bass_kernel_spmd as run

    i = {k: np.asarray(v) for k, v in inputs.items()}
    f32 = np.float32

    def feature_major(m):
        return np.ascontiguousarray(m.T.reshape(-1, P, m.shape[0]).transpose(1, 0, 2))

    def tiles(m):
        k, n = m.shape
        return m.reshape(k // P, P, n // P, P).transpose(2, 1, 0, 3)

    w = np.zeros((UNITS, P, 2, 8, P), f32)
    at = [0]

    def put(t, per_half):
        b, _, k, _ = t.shape
        if per_half == 0:
            w[at[0]:at[0] + b] = t.reshape(b, P, 2, 8, P)
            at[0] += b
        else:
            t = t.reshape(b // (2 * per_half), 2, per_half, P, k, P).transpose(0, 3, 1, 2, 4, 5)
            n = t.shape[0]
            w[at[0]:at[0] + n, :, :, 0:per_half * k] = t.reshape(n, P, 2, per_half * k, P)
            at[0] += n

    w_in = i["w_in"][0]
    a_w, b_w, c_w = A_H * HD, B_H * HD, C_H * HD
    o = 4 * a_w + 3 * b_w
    put(tiles(w_in[:, 0:o]), 0)
    put(tiles(w_in[:, o:o + P]), 0)
    put(tiles(w_in[:, o + B_H:o + B_H + 3 * c_w]), 0)
    for k in (0, KB // 2):
        put(tiles(i["w_out"][0])[:, :, k:k + KB // 2, :], 1)
    gate, up, down = (i[k][0] for k in ("w_gate", "w_up", "w_down"))
    n = CH * P
    for c in range(NC1 + 1):
        put(tiles(gate[:, c * n:(c + 1) * n]), 0)
        if c:
            put(tiles(down[(c - 1) * n:c * n, :]), 1)
        put(tiles(up[:, c * n:(c + 1) * n]), 0)
    put(tiles(down[NC1 * n:, :]), 2)
    put(tiles(i["w_ple_proj"][0]), 4)
    put(tiles(i["w_ple_gate"][0]), 0)
    w2 = i["w_in_2"][0]
    q, kv = SWA_H * SWA_D, SWA_D
    kr = q + 2 * SWA_KV * kv + MLA_QR + MLA_KVR
    lat = q + 2 * SWA_KV * kv
    put(tiles(np.concatenate([w2[:, lat:kr], w2[:, kr:], w2[:, kr:]]
                             + [w2[:, q + g * kv:q + (g + 1) * kv] for g in (0, 0, 1, 1)]
                             + [w2[:, q + SWA_KV * kv:lat], w2[:, 0:q]], axis=1)), 0)
    uq = i["w_uq_2"][0].reshape(MLA_QR, MLA_H, MLA_N + MLA_R)
    put(tiles(np.concatenate([uq[:, :, :MLA_N].reshape(MLA_QR, -1), uq[:, :, MLA_N:].reshape(MLA_QR, -1)], axis=1)), 2)
    ukv = i["w_ukv_2"][0].reshape(MLA_KVR, MLA_H, MLA_N + HD)
    put(tiles(np.concatenate([ukv[:, :, :MLA_N].reshape(MLA_KVR, -1), ukv[:, :, MLA_N:].reshape(MLA_KVR, -1)], axis=1)), 4)
    for k in (0, KB // 2):
        put(tiles(i["w_out_2"][0])[:, :, k:k + KB // 2, :], 1)
    ff1, ff2 = i["w_ff1_2"][0], i["w_ff2_2"][0]
    for c in range(NC2 + 2):
        if c >= 2:
            put(tiles(ff2[(c - 2) * n:(c - 1) * n, :]), 1)
        if c < NC2:
            put(tiles(ff1[:, c * n:(c + 1) * n]), 0)
    assert at[0] == UNITS

    par = np.zeros((P, NPAR), f32)

    def param(name, v):
        o, k = COLS[name]
        par[:, o:o + k] = v.reshape(k, P).T
    for name, key in (("attn", "attn_norm"), ("ffn", "ffn_norm"), ("ple", "ple_norm"), ("attn2", "attn_norm_g_2"),
                      ("mlp2", "mlp_norm_g_2"), ("final", "final_norm_g_2"), ("fq", "fox_qnorm"), ("fk", "fox_knorm"),
                      ("mq", "moba_qnorm"), ("mk", "moba_knorm"), ("onorm", "hgrn_onorm"), ("lb", "lb_logits"),
                      ("qn", "mla_q_norm_g_2"), ("kvn", "mla_kv_norm_g_2"), ("bmod", "b_mod_2")):
        param(name, i[key])
    par[0:B_H, COLS["bf"][0]] = i["fox_bf"][0]
    par[:, COLS["eps"][0]] = EPS
    par[:, COLS["sink"][0]:COLS["sink"][0] + SWA_H] = i["swa_sinks_2"]
    taps = np.concatenate([i["conv_w"][0], i["conv_b"]], axis=0).reshape(4, -1, P)
    par[:, COLS["conv"][0]:] = taps.transpose(2, 1, 0).reshape(P, -1)

    p_, j_ = np.arange(P)[:, None], np.arange(T)[None, :]
    seen = j_ <= P + p_
    dist = np.where(seen, -(P + p_ - j_), -1e33).astype(f32)
    causal = np.where(seen, 0.0, NEG).astype(f32)
    s_, t_ = np.arange(P)[:, None], np.arange(P)[None, :]
    hmask = np.stack([s_ == t_] + [(s_ // (2 * m) == t_ // (2 * m)) & (s_ // m % 2 == 0) & (t_ // m % 2 == 1)
                                   for m in LVL], axis=1).astype(f32)
    d = 2 * P - 1 - np.arange(3 * P)
    ok = (d >= 0) & (d < P)
    nf = np.maximum(d, 1).astype(f32)
    far = REL // 2 + (np.log(nf / f32(REL // 2)) / f32(np.log(P / (REL // 2))) * f32(REL // 2)).astype(np.int32)
    bucket = np.where(ok, np.where(d < REL // 2, d, np.minimum(far, REL - 1)), REL)
    oneh = (np.arange(REL + 1)[:, None] == bucket[None, :]).astype(f32)
    rel = np.concatenate([i["rel_bias_2"], np.full((1, SWA_H), NEG, f32)], axis=0)
    half = MLA_R // 2
    freq = f32(10000.0) ** (-np.arange(half, dtype=f32) / f32(half))
    ang = (np.arange(T, dtype=f32)[None, :] * freq[:, None])[np.arange(P) % half]
    sign = np.where(np.arange(P) % MLA_R < half, -1.0, 1.0).astype(f32)[:, None]
    cossin = np.stack([np.cos(ang), sign * np.sin(ang)], axis=1).astype(f32)
    swap = np.where(np.arange(P) % MLA_R < half, np.arange(P) + half, np.arange(P) - half)
    perm = (np.arange(P)[:, None] == swap[None, :]).astype(f32)

    arrays = {
        "w": w.reshape(UNITS, P, 2048),
        "wmod": np.ascontiguousarray(i["w_mod_2"][0].T).reshape(6 * KB, P, 2, 1024).transpose(0, 2, 1, 3).reshape(NMOD, P, 1024),
        "x": feature_major(i["x"][0]), "p": feature_major(i["p"][0, 0]),
        "c": i["c_2"].reshape(KB, P),
        "par": par, "ident": np.eye(P, dtype=f32), "dist": dist, "causal": causal, "hmask": hmask,
        "rel": rel, "oneh": oneh, "cossin": cossin, "perm": perm,
    }
    nc = bacc.Bacc("TRN2", target_bir_lowering=False, num_devices=1)
    aps = {}
    for name, v in arrays.items():
        arrays[name] = v = np.ascontiguousarray(v)
        aps[name] = nc.dram_tensor(f"in_{name}", v.shape, mybir.dt.from_np(v.dtype), kind="ExternalInput").ap()
    aps["out"] = nc.dram_tensor(_OUT, (P, KB, T), F32, kind="ExternalOutput").ap()
    build(nc, aps)
    r = run(nc, [{f"in_{k}": v for k, v in arrays.items()}], core_ids=[0])
    got = r.results[0][_OUT]
    return got.transpose(2, 1, 0).reshape(1, T, DM)
```
